# Optimizing a Trainium2 kernel written in Bass

```python
import math
import jax
import jax.numpy as jnp
from jax import lax
import numpy as np
import jax, jax.numpy as jnp

D_MODEL = 1024
BATCH = 1
SEQ = 1024
DEPTH = 1

GRID_W = 64
CTX_LEN = 256
EPS = 1e-6

RET_HEADS = 4
RET_QK_DIM = 128
RET_V_DIM = 256
RET_QK_WIDTH = RET_HEADS * RET_QK_DIM
RET_V_WIDTH = RET_HEADS * RET_V_DIM
RET_CHUNK = 128
ROPE_BASE = 10000.0

HY_WIDTH = 512
HY_SHORT = 3
HY_POS_DIM = 33
HY_BANDS = (HY_POS_DIM - 1) // 2
HY_FFN = 64
HY_DECAY_TARGET = 1e-2
HY_FAST_PCT = 0.3
HY_SLOW_PCT = 1.5

N_GROUPS = 4
EXPERTS_PER_GROUP = 8
N_EXPERTS = N_GROUPS * EXPERTS_PER_GROUP
TOP_K = 2
EXPERT_HIDDEN = 512
MOE_BLOCK = 128

IN_WIDTH = 2 * RET_QK_WIDTH + 2 * RET_V_WIDTH + 3 * HY_WIDTH + 2 * D_MODEL
IN_SPLITS = (RET_QK_WIDTH, 2 * RET_QK_WIDTH, 2 * RET_QK_WIDTH + RET_V_WIDTH, 2 * RET_QK_WIDTH + 2 * RET_V_WIDTH, 2 * RET_QK_WIDTH + 2 * RET_V_WIDTH + 3 * HY_WIDTH, 2 * RET_QK_WIDTH + 2 * RET_V_WIDTH + 3 * HY_WIDTH + D_MODEL)


def rms_norm(x, gain=None):
    x32 = x.astype(jnp.float32)
    y = x32 * lax.rsqrt(jnp.mean(jnp.square(x32), axis=-1, keepdims=True) + EPS)
    if gain is not None:
        y = y * gain.astype(jnp.float32)
    return y.astype(x.dtype)

def modulate(h, shift, scale):
    return h * (1.0 + scale) + shift

def grid_rope_angles(n_tokens):
    rows = n_tokens // GRID_W
    r, col = jnp.meshgrid(jnp.arange(rows, dtype=jnp.float32), jnp.arange(GRID_W, dtype=jnp.float32), indexing='ij')
    n_freq = RET_QK_DIM // 4
    inv_freq = ROPE_BASE ** (-jnp.arange(n_freq, dtype=jnp.float32) / n_freq)
    return r.reshape(-1)[:, None] * inv_freq, col.reshape(-1)[:, None] * inv_freq

def rope_1d(x, ang):
    n_freq = ang.shape[-1]
    x1, x2 = x[..., :n_freq], x[..., n_freq:]
    cos, sin = jnp.cos(ang), jnp.sin(ang)
    return jnp.concatenate([x1 * cos - x2 * sin, x1 * sin + x2 * cos], axis=-1)

def rope_grid(x, ang_row, ang_col):
    half = RET_QK_DIM // 2
    return jnp.concatenate([rope_1d(x[..., :half], ang_row), rope_1d(x[..., half:], ang_col)], axis=-1)

def split_heads(t, n_heads):
    b, n, _ = t.shape
    return t.reshape(b, n, n_heads, -1).transpose(0, 2, 1, 3)

def retention_scan(q, k, v, log_g, s0, strict):
    b, h, n, _ = q.shape
    dv = v.shape[-1]
    n_chunks = n // RET_CHUNK
    pos = jnp.arange(RET_CHUNK, dtype=jnp.float32)
    diff = pos[:, None] - pos[None, :]
    mask = (diff > 0) if strict else (diff >= 0)
    lg = log_g[:, None, None]
    decay_in = jnp.where(mask[None], jnp.exp(lg * jnp.maximum(diff, 0.0)[None]), 0.0)
    decay_q = jnp.exp(lg * (pos + 1.0)[None, :, None])
    decay_k = jnp.exp(lg * (RET_CHUNK - 1.0 - pos)[None, :, None])
    decay_chunk = jnp.exp(lg * RET_CHUNK)

    def chunks(t):
        return t.reshape(b, h, n_chunks, RET_CHUNK, t.shape[-1]).transpose(2, 0, 1, 3, 4)

    def step(state, qkv):
        qc, kc, vc = qkv
        scores = jnp.einsum('bhid,bhjd->bhij', qc, kc) * decay_in
        out = jnp.einsum('bhij,bhjv->bhiv', scores, vc) + jnp.einsum('bhid,bhdv->bhiv', qc, state) * decay_q
        state = state * decay_chunk + jnp.einsum('bhjd,bhjv->bhdv', kc * decay_k, vc)
        return state, out

    s_final, o = lax.scan(step, s0, (chunks(q), chunks(k), chunks(v)))
    return o.transpose(1, 2, 0, 3, 4).reshape(b, h, n, dv), s_final

def retention_bidir(q, k, v, log_g, s0_fwd, s0_bwd):
    o_f, s_f = retention_scan(q, k, v, log_g[0], s0_fwd, False)
    o_b, s_b = retention_scan(jnp.flip(q, 2), jnp.flip(k, 2), jnp.flip(v, 2), log_g[1], s0_bwd, True)
    return o_f + jnp.flip(o_b, 2), s_f, s_b

def retention_readout(o, g):
    b, h, n, dv = o.shape
    o = rms_norm(o).transpose(0, 2, 1, 3).reshape(b, n, h * dv)
    return jax.nn.silu(g) * o.astype(g.dtype)

def short_conv(u, w, bias):
    n = u.shape[1]
    pad = HY_SHORT // 2
    up = jnp.pad(u, ((0, 0), (pad, pad), (0, 0)))
    return sum(up[:, j:j + n] * w[j] for j in range(HY_SHORT)) + bias

def hyena_filters(n, w1, b1, freq, w2, b2, w3):
    f32 = jnp.float32
    t = jnp.arange(n, dtype=f32) / n
    bands = jnp.linspace(1e-4, HY_BANDS - 1, HY_BANDS, dtype=f32)
    phase = 2.0 * math.pi * t[:, None] * bands[None, :]
    feats = jnp.concatenate([t[:, None], jnp.cos(phase), -jnp.sin(phase)], axis=-1)
    freq = freq.astype(f32)
    hid = jnp.sin(freq * (feats @ w1.astype(f32) + b1.astype(f32)))
    hid = jnp.sin(freq * (hid @ w2.astype(f32) + b2.astype(f32)))
    filt = hid @ w3.astype(f32)
    slow = abs(math.log(HY_DECAY_TARGET)) / HY_SLOW_PCT
    fast = abs(math.log(HY_DECAY_TARGET)) / HY_FAST_PCT
    deltas = jnp.tile(jnp.linspace(slow, fast, HY_WIDTH, dtype=f32), 2)
    filt = filt * jnp.exp(-t[:, None] * deltas[None, :])
    filt = filt / jnp.sum(jnp.abs(filt), axis=0, keepdims=True)
    return filt[:, :HY_WIDTH], filt[:, HY_WIDTH:]

def long_conv_bidir(z, h_fwd, h_bwd):
    n = z.shape[1]
    nfft = 2 * n
    zf = jnp.fft.rfft(z.astype(jnp.float32), n=nfft, axis=1)
    hf = jnp.fft.rfft(h_fwd, n=nfft, axis=0) + jnp.conj(jnp.fft.rfft(h_bwd, n=nfft, axis=0))
    return jnp.fft.irfft(zf * hf[None], n=nfft, axis=1)[:, :n]

def hyena_branch(u, conv_w, conv_b, ffn_w1, ffn_b1, ffn_freq, ffn_w2, ffn_b2, ffn_w3, skip):
    x0, x1, v = jnp.split(short_conv(u, conv_w, conv_b), 3, axis=-1)
    z = x1 * v
    h_fwd, h_bwd = hyena_filters(u.shape[1], ffn_w1, ffn_b1, ffn_freq, ffn_w2, ffn_b2, ffn_w3)
    y = long_conv_bidir(z, h_fwd, h_bwd).astype(u.dtype) + z * skip
    return x0 * y

def merge_branches(ret_gated, hy_out, gate_ret, gate_hy, ret_w_o, hy_w_o, w_out):
    mixed = jax.nn.sigmoid(gate_ret) * (ret_gated @ ret_w_o) + jax.nn.sigmoid(gate_hy) * (hy_out @ hy_w_o)
    return mixed @ w_out

def moe_ffn(u, rg_w, rg_b, re_w, re_b, w1, w3, w2):
    n_tok = u.shape[0]
    f32 = jnp.float32
    group_p = jax.nn.softmax((u @ rg_w).astype(f32) + rg_b.astype(f32), axis=-1)
    p_star, g_star = lax.top_k(group_p, 1)
    expert_logits = ((u @ re_w).astype(f32) + re_b.astype(f32)).reshape(n_tok, N_GROUPS, EXPERTS_PER_GROUP)
    in_group = jnp.take_along_axis(expert_logits, g_star[:, :, None], axis=1)[:, 0]
    w_top, e_top = lax.top_k(jax.nn.softmax(in_group, axis=-1), TOP_K)
    weights = p_star * w_top / jnp.sum(w_top, axis=-1, keepdims=True)
    expert_id = g_star * EXPERTS_PER_GROUP + e_top
    n_assign = n_tok * TOP_K
    flat_e = expert_id.reshape(n_assign)
    flat_tok = jnp.arange(n_assign, dtype=jnp.int32) // TOP_K
    flat_w = weights.reshape(n_assign)
    order = jnp.argsort(flat_e)
    se, stok, sw = flat_e[order], flat_tok[order], flat_w[order]
    counts = jnp.bincount(flat_e, length=N_EXPERTS)
    starts = jnp.cumsum(counts) - counts
    padded = (counts + MOE_BLOCK - 1) // MOE_BLOCK * MOE_BLOCK
    padded_end = jnp.cumsum(padded)
    padded_start = padded_end - padded
    dest = padded_start[se] + jnp.arange(n_assign, dtype=jnp.int32) - starts[se]
    n_blocks = -(-(n_assign + N_EXPERTS * (MOE_BLOCK - 1)) // MOE_BLOCK)
    n_rows = n_blocks * MOE_BLOCK
    row_tok = jnp.zeros((n_rows,), jnp.int32).at[dest].set(stok)
    block_expert = jnp.minimum(jnp.searchsorted(padded_end, jnp.arange(n_blocks, dtype=jnp.int32) * MOE_BLOCK, side='right'), N_EXPERTS - 1)
    xb = u[row_tok].reshape(n_blocks, MOE_BLOCK, u.shape[1])

    def expert_block(args):
        xblk, e = args
        return (jax.nn.silu(xblk @ w1[e]) * (xblk @ w3[e])) @ w2[e]

    yb = lax.map(expert_block, (xb, block_expert)).reshape(n_rows, u.shape[1])
    y = yb[dest] * sw[:, None].astype(u.dtype)
    return jax.ops.segment_sum(y, stok, num_segments=n_tok)

def first_inputs(seed: int = 0) -> dict:
    key = jax.random.key(seed)
    ks = jax.random.split(key, 32)
    f32 = jnp.float32

    def nrm(k, shape, scale):
        return scale * jax.random.normal(k, shape, f32)

    base_logit = np.log(2.0 ** (5 + np.arange(RET_HEADS)) - 1.0).astype(np.float32)
    return {
        'x': nrm(ks[0], (BATCH, SEQ, D_MODEL), 1.0),
        'c': nrm(ks[1], (BATCH, D_MODEL), 1.0),
        'ctx': nrm(ks[2], (BATCH, CTX_LEN, D_MODEL), 1.0),
        'c_ctx': nrm(ks[3], (D_MODEL,), 1.0),
        'ada_w': nrm(ks[4], (DEPTH, D_MODEL, 6 * D_MODEL), 0.5 * D_MODEL ** -0.5),
        'ada_b': nrm(ks[5], (DEPTH, 6 * D_MODEL), 0.02),
        'norm1_g': 1.0 + nrm(ks[6], (DEPTH, D_MODEL), 0.05),
        'norm2_g': 1.0 + nrm(ks[7], (DEPTH, D_MODEL), 0.05),
        'w_in': nrm(ks[8], (DEPTH, D_MODEL, IN_WIDTH), D_MODEL ** -0.5),
        'b_in': nrm(ks[9], (DEPTH, IN_WIDTH), 0.02),
        'ret_decay_logit': jnp.asarray(base_logit)[None, None, :] + nrm(ks[10], (DEPTH, 2, RET_HEADS), 0.1),
        'ret_w_o': nrm(ks[11], (DEPTH, RET_V_WIDTH, D_MODEL), RET_V_WIDTH ** -0.5),
        'hy_conv_w': nrm(ks[12], (DEPTH, HY_SHORT, 3 * HY_WIDTH), HY_SHORT ** -0.5),
        'hy_conv_b': nrm(ks[13], (DEPTH, 3 * HY_WIDTH), 0.02),
        'hy_ffn_w1': nrm(ks[14], (DEPTH, HY_POS_DIM, HY_FFN), HY_POS_DIM ** -0.5),
        'hy_ffn_b1': nrm(ks[15], (DEPTH, HY_FFN), 0.02),
        'hy_ffn_freq': 1.0 + nrm(ks[16], (DEPTH, HY_FFN), 0.05),
        'hy_ffn_w2': nrm(ks[17], (DEPTH, HY_FFN, HY_FFN), HY_FFN ** -0.5),
        'hy_ffn_b2': nrm(ks[18], (DEPTH, HY_FFN), 0.02),
        'hy_ffn_w3': nrm(ks[19], (DEPTH, HY_FFN, 2 * HY_WIDTH), HY_FFN ** -0.5),
        'hy_skip': nrm(ks[20], (DEPTH, HY_WIDTH), 0.5),
        'hy_w_o': nrm(ks[21], (DEPTH, HY_WIDTH, D_MODEL), HY_WIDTH ** -0.5),
        'w_out': nrm(ks[22], (DEPTH, D_MODEL, D_MODEL), D_MODEL ** -0.5),
        'router_group_w': nrm(ks[23], (DEPTH, D_MODEL, N_GROUPS), D_MODEL ** -0.5),
        'router_group_b': nrm(ks[24], (DEPTH, N_GROUPS), 0.01),
        'router_expert_w': nrm(ks[25], (DEPTH, D_MODEL, N_EXPERTS), D_MODEL ** -0.5),
        'router_expert_b': nrm(ks[26], (DEPTH, N_EXPERTS), 0.01),
        'expert_w1': nrm(ks[27], (DEPTH, N_EXPERTS, D_MODEL, EXPERT_HIDDEN), D_MODEL ** -0.5),
        'expert_w3': nrm(ks[28], (DEPTH, N_EXPERTS, D_MODEL, EXPERT_HIDDEN), D_MODEL ** -0.5),
        'expert_w2': nrm(ks[29], (DEPTH, N_EXPERTS, EXPERT_HIDDEN, D_MODEL), EXPERT_HIDDEN ** -0.5),
        'final_norm_g': 1.0 + nrm(ks[30], (D_MODEL,), 0.05),
    }

def first_block(x, c, ctx, c_ctx, ada_w, ada_b, norm1_g, norm2_g, w_in, b_in, ret_decay_logit, ret_w_o, hy_conv_w, hy_conv_b, hy_ffn_w1, hy_ffn_b1, hy_ffn_freq, hy_ffn_w2, hy_ffn_b2, hy_ffn_w3, hy_skip, hy_w_o, w_out, router_group_w, router_group_b, router_expert_w, router_expert_b, expert_w1, expert_w3, expert_w2, final_norm_g):
    f32 = jnp.float32
    batch, n_tokens = x.shape[0], x.shape[1]
    ang_row, ang_col = grid_rope_angles(n_tokens)
    silu_c = jax.nn.silu(c)
    silu_cc = jax.nn.silu(c_ctx)
    k_scale = RET_QK_DIM ** -0.5
    for layer in range(DEPTH):
        last = layer == DEPTH - 1
        sh1, sc1, gt1, sh2, sc2, gt2 = jnp.split((silu_c @ ada_w[layer] + ada_b[layer])[:, None, :], 6, axis=-1)
        csh1, csc1, cgt1, csh2, csc2, cgt2 = jnp.split(silu_cc @ ada_w[layer] + ada_b[layer], 6, axis=-1)
        h = modulate(rms_norm(x, norm1_g[layer]), sh1, sc1)
        hc = modulate(rms_norm(ctx, norm1_g[layer]), csh1, csc1)
        q, k, v, g, hy_u, gate_ret, gate_hy = jnp.split(h @ w_in[layer] + b_in[layer], IN_SPLITS, axis=-1)
        qc, kc, vc, gc, hyc_u, gate_ret_c, gate_hy_c = jnp.split(hc @ w_in[layer] + b_in[layer], IN_SPLITS, axis=-1)
        log_g = jax.nn.log_sigmoid(ret_decay_logit[layer].astype(f32))
        zero_state = jnp.zeros((batch, RET_HEADS, RET_QK_DIM, RET_V_DIM), f32)
        o_ctx, s_fwd, s_bwd = retention_bidir(split_heads(qc, RET_HEADS).astype(f32), split_heads(kc, RET_HEADS).astype(f32) * k_scale, split_heads(vc, RET_HEADS).astype(f32), log_g, zero_state, zero_state)
        q_h = rope_grid(split_heads(q, RET_HEADS).astype(f32), ang_row, ang_col)
        k_h = rope_grid(split_heads(k, RET_HEADS).astype(f32), ang_row, ang_col) * k_scale
        o_lat, _, _ = retention_bidir(q_h, k_h, split_heads(v, RET_HEADS).astype(f32), log_g, s_fwd, s_bwd)
        hy_args = (hy_conv_w[layer], hy_conv_b[layer], hy_ffn_w1[layer], hy_ffn_b1[layer], hy_ffn_freq[layer], hy_ffn_w2[layer], hy_ffn_b2[layer], hy_ffn_w3[layer], hy_skip[layer])
        out_args = (ret_w_o[layer], hy_w_o[layer], w_out[layer])
        moe_args = (router_group_w[layer], router_group_b[layer], router_expert_w[layer], router_expert_b[layer], expert_w1[layer], expert_w3[layer], expert_w2[layer])
        mix = merge_branches(retention_readout(o_lat, g), hyena_branch(hy_u, *hy_args), gate_ret, gate_hy, *out_args)
        x = x + gt1 * mix
        h2 = modulate(rms_norm(x, norm2_g[layer]), sh2, sc2)
        if last:
            x = x + gt2 * moe_ffn(h2.reshape(-1, D_MODEL), *moe_args).reshape(x.shape)
        else:
            mix_c = merge_branches(retention_readout(o_ctx, gc), hyena_branch(hyc_u, *hy_args), gate_ret_c, gate_hy_c, *out_args)
            ctx = ctx + cgt1 * mix_c
            h2c = modulate(rms_norm(ctx, norm2_g[layer]), csh2, csc2)
            y = moe_ffn(jnp.concatenate([h2.reshape(-1, D_MODEL), h2c.reshape(-1, D_MODEL)], axis=0), *moe_args)
            n_lat = batch * n_tokens
            x = x + gt2 * y[:n_lat].reshape(x.shape)
            ctx = ctx + cgt2 * y[n_lat:].reshape(ctx.shape)
    return rms_norm(x, final_norm_g)


MLA_HEADS = 8
QK_NOPE = 64
QK_ROPE = 32
V_DIM = 64
Q_LORA = 384
KV_LORA = 256
Q_BLOCK = 128
MLA_OUT = MLA_HEADS * V_DIM
RWKV_HEADS = 8
RWKV_HEAD = 64
RWKV_DIM = RWKV_HEADS * RWKV_HEAD
DECAY_LORA = 64
AAA_LORA = 64
GATE_LORA = 128
LNX_EPS = 64e-5
N_DIR = 2
N_BRANCH = 2
MLA_IN = Q_LORA + KV_LORA + QK_ROPE
RWKV_IN = 3 * RWKV_DIM + N_DIR * DECAY_LORA + N_DIR * AAA_LORA + GATE_LORA
GATE_IN = N_BRANCH * D_MODEL
IN_DIM = MLA_IN + RWKV_IN + GATE_IN
N_EXPERTS_2 = N_GROUPS * EXPERTS_PER_GROUP
D_EXPERT = 256
NORM_EPS = 1e-6


def rms_norm_2(x, g, eps=NORM_EPS):
    xf = x.astype(jnp.float32)
    y = xf * lax.rsqrt(jnp.mean(xf * xf, axis=-1, keepdims=True) + eps)
    return (y * g.astype(jnp.float32)).astype(x.dtype)

def apply_rope(x, cos, sin):
    half = x.shape[-1] // 2
    x1 = x[..., :half].astype(jnp.float32)
    x2 = x[..., half:].astype(jnp.float32)
    out = jnp.concatenate([x1 * cos - x2 * sin, x1 * sin + x2 * cos], axis=-1)
    return out.astype(x.dtype)

def mla_branch(z, q_norm_g, kv_norm_g, w_uq, w_ukv):
    B, S, _ = z.shape
    c_q = rms_norm_2(z[..., :Q_LORA], q_norm_g)
    c_kv = rms_norm_2(z[..., Q_LORA:Q_LORA + KV_LORA], kv_norm_g)
    k_rope = z[..., Q_LORA + KV_LORA:]
    q = (c_q @ w_uq).reshape(B, S, MLA_HEADS, QK_NOPE + QK_ROPE)
    kv = (c_kv @ w_ukv).reshape(B, S, MLA_HEADS, QK_NOPE + V_DIM)
    q_nope, q_rope = q[..., :QK_NOPE], q[..., QK_NOPE:]
    k_nope, v = kv[..., :QK_NOPE], kv[..., QK_NOPE:]
    pos = jnp.arange(S, dtype=jnp.float32)
    inv_freq = ROPE_BASE ** (-jnp.arange(0, QK_ROPE, 2, dtype=jnp.float32) / QK_ROPE)
    ang = pos[:, None] * inv_freq[None, :]
    cos, sin = jnp.cos(ang), jnp.sin(ang)
    q_rope = apply_rope(q_rope, cos[:, None, :], sin[:, None, :])
    k_rope = apply_rope(k_rope, cos, sin)
    scale = (QK_NOPE + QK_ROPE) ** -0.5
    nb = S // Q_BLOCK
    qn_b = q_nope.reshape(B, nb, Q_BLOCK, MLA_HEADS, QK_NOPE).transpose(1, 0, 2, 3, 4)
    qr_b = q_rope.reshape(B, nb, Q_BLOCK, MLA_HEADS, QK_ROPE).transpose(1, 0, 2, 3, 4)

    def attend(blk):
        qn, qr = blk
        s = (jnp.einsum('bqhd,bkhd->bhqk', qn, k_nope)
             + jnp.einsum('bqhd,bkd->bhqk', qr, k_rope))
        p = jax.nn.softmax(s.astype(jnp.float32) * scale, axis=-1).astype(v.dtype)
        return jnp.einsum('bhqk,bkhd->bqhd', p, v)

    o = lax.map(attend, (qn_b, qr_b))
    return o.transpose(1, 0, 2, 3, 4).reshape(B, S, MLA_OUT)

def token_shift_centred(z, mu_prev, mu_next):
    z_prev = jnp.pad(z[:, :-1], ((0, 0), (1, 0), (0, 0)))
    z_next = jnp.pad(z[:, 1:], ((0, 0), (0, 1), (0, 0)))
    return z + mu_prev * (z_prev - z) + mu_next * (z_next - z)

def wkv7_scan(r, w, k, v, a_vec, b_vec):
    B, S, H, N = r.shape

    def step(state, inp):
        r_t, w_t, k_t, v_t, a_t, b_t = inp
        sa = jnp.einsum('bhvk,bhk->bhv', state, a_t)
        state = (state * w_t[:, :, None, :] + sa[..., None] * b_t[:, :, None, :]
                 + v_t[..., None] * k_t[:, :, None, :])
        return state, jnp.einsum('bhvk,bhk->bhv', state, r_t)

    xs = tuple(jnp.moveaxis(t, 1, 0) for t in (r, w, k, v, a_vec, b_vec))
    s0 = jnp.zeros((B, H, N, N), jnp.float32)
    _, y = lax.scan(step, s0, xs)
    return jnp.moveaxis(y, 0, 1)

def rwkv_branch(z, mu_prev, mu_next, w0, w_up, a0, a_up, g_up, k_k, k_a, r_k, lnx_g, lnx_b):
    B, S, _ = z.shape
    C, H, N = RWKV_DIM, RWKV_HEADS, RWKV_HEAD
    f32 = jnp.float32
    zf = token_shift_centred(z.astype(f32), mu_prev.astype(f32), mu_next.astype(f32))
    r, k, v = zf[..., :C], zf[..., C:2 * C], zf[..., 2 * C:3 * C]
    o = 3 * C
    wd = zf[..., o:o + N_DIR * DECAY_LORA].reshape(B, S, N_DIR, DECAY_LORA)
    o += N_DIR * DECAY_LORA
    ad = zf[..., o:o + N_DIR * AAA_LORA].reshape(B, S, N_DIR, AAA_LORA)
    o += N_DIR * AAA_LORA
    gd = zf[..., o:]
    w_logit = w0.astype(f32) + jnp.einsum('bsdr,drc->bsdc', jnp.tanh(wd), w_up.astype(f32))
    decay = jnp.exp(-jnp.exp(-jax.nn.softplus(-w_logit) - 0.5))
    a = jax.nn.sigmoid(a0.astype(f32) + jnp.einsum('bsdr,drc->bsdc', ad, a_up.astype(f32)))
    g = jax.nn.sigmoid(gd) @ g_up.astype(f32)

    def heads(t):
        return t.reshape(t.shape[:-1] + (H, N))

    kk = heads(k * k_k.astype(f32))
    kk = kk / jnp.maximum(jnp.sqrt(jnp.sum(kk * kk, axis=-1, keepdims=True)), 1e-12)
    k_dir = heads(k[:, :, None, :] * (1.0 + (a - 1.0) * k_a.astype(f32)))
    a_h, decay_h = heads(a), heads(decay)
    r_h, v_h = heads(r), heads(v)
    y_f = wkv7_scan(r_h, decay_h[:, :, 0], k_dir[:, :, 0], v_h, -kk, kk * a_h[:, :, 0])
    fl = lambda t: jnp.flip(t, axis=1)
    y_b = fl(wkv7_scan(fl(r_h), fl(decay_h[:, :, 1]), fl(k_dir[:, :, 1]), fl(v_h),
                       fl(-kk), fl(kk * a_h[:, :, 1])))
    y = y_f + y_b
    mu = jnp.mean(y, axis=-1, keepdims=True)
    var = jnp.mean(jnp.square(y - mu), axis=-1, keepdims=True)
    y = ((y - mu) * lax.rsqrt(var + LNX_EPS)).reshape(B, S, C)
    y = y * lnx_g.astype(f32) + lnx_b.astype(f32)
    bonus = jnp.sum(r_h[:, :, None] * k_dir * heads(r_k.astype(f32)), axis=-1, keepdims=True) * v_h[:, :, None]
    y = y + jnp.sum(bonus, axis=2).reshape(B, S, C)
    return (y * g).astype(z.dtype)

def hier_moe(h, rg_w, rg_b, re_w, re_b, w1, w3, w2):
    B, S, D = h.shape
    T = B * S
    ht = h.reshape(T, D)
    group_p = jax.nn.softmax((ht @ rg_w + rg_b).astype(jnp.float32), axis=-1)
    gp, gi = lax.top_k(group_p, 1)
    gp, gi = gp[:, 0], gi[:, 0]
    e_logits = (ht @ re_w + re_b).astype(jnp.float32).reshape(T, N_GROUPS, EXPERTS_PER_GROUP)
    sel = jnp.take_along_axis(e_logits, gi[:, None, None], axis=1)[:, 0]
    ep = jax.nn.softmax(sel, axis=-1)
    tp, ti = lax.top_k(ep, TOP_K)
    tp = tp / jnp.sum(tp, axis=-1, keepdims=True)
    weight = gp[:, None] * tp
    expert = gi[:, None] * EXPERTS_PER_GROUP + ti
    A = T * TOP_K
    flat_e = expert.reshape(A)
    flat_w = weight.reshape(A)
    flat_tok = jnp.repeat(jnp.arange(T, dtype=jnp.int32), TOP_K)
    order = jnp.argsort(flat_e)
    se, stok, sw = flat_e[order], flat_tok[order], flat_w[order]
    counts = jnp.bincount(flat_e, length=N_EXPERTS_2)
    padded = ((counts + MOE_BLOCK - 1) // MOE_BLOCK) * MOE_BLOCK
    start = jnp.cumsum(counts) - counts
    pend = jnp.cumsum(padded)
    pstart = pend - padded
    dest = pstart[se] + (jnp.arange(A, dtype=jnp.int32) - start[se])
    n_blocks = -(-A // MOE_BLOCK) + N_EXPERTS_2
    cap = n_blocks * MOE_BLOCK
    slot_tok = jnp.full((cap,), T, jnp.int32).at[dest].set(stok)
    slot_w = jnp.zeros((cap,), h.dtype).at[dest].set(sw.astype(h.dtype))
    block_e = jnp.minimum(jnp.searchsorted(pend, jnp.arange(n_blocks) * MOE_BLOCK, side='right'),
                          N_EXPERTS_2 - 1)
    h_pad = jnp.concatenate([ht, jnp.zeros((1, D), ht.dtype)], axis=0)
    xb = h_pad[slot_tok].reshape(n_blocks, MOE_BLOCK, D)

    def expert_block(args):
        xblk, e = args
        hid = jax.nn.silu(xblk @ w1[e]) * (xblk @ w3[e])
        return hid @ w2[e]

    yb = lax.map(expert_block, (xb, block_e)).reshape(cap, D)
    y = jax.ops.segment_sum(yb * slot_w[:, None], slot_tok, num_segments=T + 1)[:T]
    return y.reshape(B, S, D)

def second_inputs(seed: int = 0) -> dict:
    key = jax.random.key(seed)
    ks = iter(jax.random.split(key, 48))
    L, D, C = DEPTH, D_MODEL, RWKV_DIM
    f32 = jnp.float32
    nrm = lambda shape, s: jax.random.normal(next(ks), shape, f32) * s
    uni = lambda shape, lo, hi: jax.random.uniform(next(ks), shape, f32, lo, hi)
    return {
        'x': nrm((BATCH, SEQ, D), 1.0),
        'norm_mix_g': 1.0 + nrm((L, D), 0.02),
        'w_in': nrm((L, D, IN_DIM), D ** -0.5),
        'q_norm_g': 1.0 + nrm((L, Q_LORA), 0.02),
        'kv_norm_g': 1.0 + nrm((L, KV_LORA), 0.02),
        'w_uq': nrm((L, Q_LORA, MLA_HEADS * (QK_NOPE + QK_ROPE)), Q_LORA ** -0.5),
        'w_ukv': nrm((L, KV_LORA, MLA_HEADS * (QK_NOPE + V_DIM)), KV_LORA ** -0.5),
        'w_br_mla': nrm((L, MLA_OUT, D), MLA_OUT ** -0.5),
        'mu_prev': uni((L, RWKV_IN), 0.0, 0.5),
        'mu_next': uni((L, RWKV_IN), 0.0, 0.5),
        'w0': uni((L, N_DIR, C), -3.0, 1.0),
        'w_up': nrm((L, N_DIR, DECAY_LORA, C), 0.5 * DECAY_LORA ** -0.5),
        'a0': nrm((L, N_DIR, C), 0.1),
        'a_up': nrm((L, N_DIR, AAA_LORA, C), 0.5 * AAA_LORA ** -0.5),
        'g_up': nrm((L, GATE_LORA, C), GATE_LORA ** -0.5),
        'k_k': 0.85 + nrm((L, C), 0.02),
        'k_a': 1.0 + nrm((L, C), 0.02),
        'r_k': nrm((L, C), 0.1),
        'lnx_g': 1.0 + nrm((L, C), 0.02),
        'lnx_b': nrm((L, C), 0.01),
        'w_br_rwkv': nrm((L, C, D), C ** -0.5),
        'gate_b': nrm((L, N_BRANCH, D), 0.01),
        'w_out': nrm((L, D, D), D ** -0.5),
        'norm_ffn_g': 1.0 + nrm((L, D), 0.02),
        'router_group_w': nrm((L, D, N_GROUPS), D ** -0.5),
        'router_group_b': nrm((L, N_GROUPS), 0.01),
        'router_expert_w': nrm((L, D, N_EXPERTS_2), D ** -0.5),
        'router_expert_b': nrm((L, N_EXPERTS_2), 0.01),
        'w1': nrm((L, N_EXPERTS_2, D, D_EXPERT), D ** -0.5),
        'w3': nrm((L, N_EXPERTS_2, D, D_EXPERT), D ** -0.5),
        'w2': nrm((L, N_EXPERTS_2, D_EXPERT, D), D_EXPERT ** -0.5),
        'norm_final_g': 1.0 + nrm((D,), 0.02),
    }

def second_block(x, norm_mix_g, w_in, q_norm_g, kv_norm_g, w_uq, w_ukv, w_br_mla,
              mu_prev, mu_next, w0, w_up, a0, a_up, g_up, k_k, k_a, r_k, lnx_g, lnx_b,
              w_br_rwkv, gate_b, w_out, norm_ffn_g, router_group_w, router_group_b,
              router_expert_w, router_expert_b, w1, w3, w2, norm_final_g):
    B, S, D = x.shape
    for l in range(DEPTH):
        h = rms_norm_2(x, norm_mix_g[l])
        z = h @ w_in[l]
        z_mla = z[..., :MLA_IN]
        z_rwkv = z[..., MLA_IN:MLA_IN + RWKV_IN]
        z_gate = z[..., MLA_IN + RWKV_IN:].reshape(B, S, N_BRANCH, D)
        o_mla = mla_branch(z_mla, q_norm_g[l], kv_norm_g[l], w_uq[l], w_ukv[l])
        o_rwkv = rwkv_branch(z_rwkv, mu_prev[l], mu_next[l], w0[l], w_up[l], a0[l], a_up[l],
                             g_up[l], k_k[l], k_a[l], r_k[l], lnx_g[l], lnx_b[l])
        gates = jax.nn.sigmoid(z_gate + gate_b[l])
        mixed = gates[:, :, 0] * (o_mla @ w_br_mla[l]) + gates[:, :, 1] * (o_rwkv @ w_br_rwkv[l])
        x = x + mixed @ w_out[l]
        h2 = rms_norm_2(x, norm_ffn_g[l])
        x = x + hier_moe(h2, router_group_w[l], router_group_b[l], router_expert_w[l],
                         router_expert_b[l], w1[l], w3[l], w2[l])
    return rms_norm_2(x, norm_final_g)


def setup_inputs(seed=0):
    out = dict(first_inputs(seed))
    for name, value in second_inputs(seed + 1).items():
        if name != "x":
            out[name + "_2"] = value
    return out


def reference(
    x, c, ctx, c_ctx, ada_w, ada_b, norm1_g, norm2_g, w_in, b_in, ret_decay_logit, ret_w_o,
    hy_conv_w, hy_conv_b, hy_ffn_w1, hy_ffn_b1, hy_ffn_freq, hy_ffn_w2, hy_ffn_b2, hy_ffn_w3,
    hy_skip, hy_w_o, w_out, router_group_w, router_group_b, router_expert_w, router_expert_b,
    expert_w1, expert_w3, expert_w2, final_norm_g, norm_mix_g_2, w_in_2, q_norm_g_2,
    kv_norm_g_2, w_uq_2, w_ukv_2, w_br_mla_2, mu_prev_2, mu_next_2, w0_2, w_up_2, a0_2, a_up_2,
    g_up_2, k_k_2, k_a_2, r_k_2, lnx_g_2, lnx_b_2, w_br_rwkv_2, gate_b_2, w_out_2, norm_ffn_g_2,
    router_group_w_2, router_group_b_2, router_expert_w_2, router_expert_b_2, w1_2, w3_2, w2_2,
    norm_final_g_2,
):
    x = first_block(
        x, c, ctx, c_ctx, ada_w, ada_b, norm1_g, norm2_g, w_in, b_in, ret_decay_logit, ret_w_o,
        hy_conv_w, hy_conv_b, hy_ffn_w1, hy_ffn_b1, hy_ffn_freq, hy_ffn_w2, hy_ffn_b2,
        hy_ffn_w3, hy_skip, hy_w_o, w_out, router_group_w, router_group_b, router_expert_w,
        router_expert_b, expert_w1, expert_w3, expert_w2, final_norm_g,
    )
    return second_block(
        x, norm_mix_g_2, w_in_2, q_norm_g_2, kv_norm_g_2, w_uq_2, w_ukv_2, w_br_mla_2,
        mu_prev_2, mu_next_2, w0_2, w_up_2, a0_2, a_up_2, g_up_2, k_k_2, k_a_2, r_k_2, lnx_g_2,
        lnx_b_2, w_br_rwkv_2, gate_b_2, w_out_2, norm_ffn_g_2, router_group_w_2,
        router_group_b_2, router_expert_w_2, router_expert_b_2, w1_2, w3_2, w2_2,
        norm_final_g_2,
    )


_drawn_inputs = setup_inputs


def setup_inputs(seed=0):
    import zlib

    import numpy as np

    out = dict(_drawn_inputs(seed))
    spreads = {}
    factors = {'hy_conv_b': 4.084,
     'hy_ffn_b1': 6.079,
     'hy_ffn_freq': 5.954,
     'hy_ffn_b2': 4.314,
     'router_group_b': 4.868,
     'router_expert_b': 4.748,
     'q_norm_g_2': 8.0,
     'kv_norm_g_2': 4.656,
     'k_k_2': 39.064,
     'k_a_2': 3.049,
     'lnx_g_2': 20.345,
     'lnx_b_2': 44.181,
     'gate_b_2': 6.03,
     'router_group_b_2': 12.191,
     'router_expert_b_2': 16.449,
     'norm_final_g_2': 7.869,
     'norm_ffn_g_2': 5.235}
    for name, (base, spread) in spreads.items():
        noise = np.random.default_rng([zlib.crc32(name.encode()), seed]).standard_normal(out[name].shape)
        drawn = base * np.exp(spread * noise) if base else spread * noise
        out[name] = jnp.asarray(drawn.astype(out[name].dtype))
    for name, factor in factors.items():
        out[name] = (out[name] * factor).astype(out[name].dtype)
    return out
```

```python
import concourse.bass as bass
from concourse import mybir
from contextlib import ExitStack
import numpy as np

F32 = mybir.dt.float32
I32 = mybir.dt.int32
U32 = mybir.dt.uint32
ALU = mybir.AluOpType
ACT = mybir.ActivationFunctionType
AXX = mybir.AxisListType.X
P = 128
D = 1024
KT = D // P
SEQ = 1024
CTX = 256
HALF = 512
EPS = 1e-6


class Named:
    pass


class Mem:
    spent = []

    def __init__(self, nc, phase):
        self.nc, self.phase, self.stack, self.own = nc, phase, ExitStack(), []

    def __enter__(self):
        return self

    def __exit__(self, *exc):
        Mem.spent.extend(self.own)
        return self.stack.__exit__(*exc)

    def sb(self, name, shape, dt=F32):
        return self.stack.enter_context(self.nc.sbuf_tensor(f"{self.phase}_{name}", shape, dt))

    def banks(self, count):
        return [self.stack.enter_context(self.nc.psum_tensor(f"{self.phase}_bank{n}", [P, HALF], F32))
                for n in range(count)]

    def sems(self, *names):
        new = [self.nc.alloc_semaphore(name=f"{self.phase}_{n}") for n in names]
        self.own.extend(new)
        return new

    def block(self):
        return self.stack.enter_context(self.nc.Block())

    @staticmethod
    def retire(nc):
        nc.clear_and_free_semaphores(Mem.spent)
        nc.all_engine_barrier()
        Mem.spent = []


def hold(act, sem, value):
    act.wait_ge(sem, value)
    act.nop(nofuse=True)


VECS = [("norm1_g", 8), ("norm2_g", 8), ("b_in", 52), ("hy_conv_w", 36), ("hy_conv_b", 12), ("hy_skip", 4),
        None,
        ("ada_b", 48), ("c", 8), ("c_ctx", 8), ("q_norm_g_2", 3), ("kv_norm_g_2", 2), ("k_k_2", 4), ("k_a_2", 4),
        ("r_k_2", 4), ("lnx_g_2", 4), ("lnx_b_2", 4), ("gate_b_2", 16), ("norm_mix_g_2", 8), ("norm_ffn_g_2", 8),
        None,
        ("mu_prev_2", 15), ("mu_next_2", 15), ("w0_2", 8), ("a0_2", 8)]


def vec_places():
    places, group, row = {}, 0, 0
    for v in VECS:
        if v is None:
            group, row = group + 1, 0
        else:
            places[v[0]] = (group * P + row, v[1])
            row += v[1]
    return places, group + 1


PLACES, VGROUPS = vec_places()


def vec(cols, name, n=0):
    return cols[:, PLACES[name][0] + n:PLACES[name][0] + n + 1]


def flat(ap):
    names = "abcdefg"[:len(ap.shape)]
    return ap.rearrange(f"{' '.join(names)} -> ({' '.join(names)})") if len(ap.shape) > 1 else ap


def phase_vectors(nc, I, K):
    with Mem(nc, "vec") as m:
        rows = m.sb("rows", [P, VGROUPS, P])
        w = m.sb("w", [P, 2, KT, 256])
        cc = m.sb("cc", [P, KT, 2])
        ada = m.sb("ada", [P, 48, 2])
        diag = m.sb("diag", [P, 2, P])
        sq = m.sb("sq", [P, 8])
        bk = m.banks(8)
        wfull = m.sems("wfull0", "wfull1")
        loaded, wfree, zeroed, turned, cols_ok, silu_ok, ada_mm, ada_ok, dg, dgfree, bc, bcfree, chain = m.sems(
            "loaded", "wfree", "zeroed", "turned", "cols_ok", "silu_ok", "ada_mm", "ada_ok", "dg", "dgfree",
            "bc", "bcfree", "chain")
        ada_w = I["ada_w"].rearrange("l (k p) n -> p (l k) n", p=P)
        nload = [0]
        b = m.block()

        @b.sync
        def _(sp):
            sp.dma_start(K.ident[:, :], I["k_eye"]).then_inc(loaded, 16)
            sp.wait_ge(zeroed, 1)
            for name, n in [v for v in VECS if v]:
                g, r = divmod(PLACES[name][0], P)
                sp.dma_start(rows[r:r + n, g, :], flat(I[name]).rearrange("(n p) -> n p", p=P)).then_inc(loaded, 16)
            with sp.Fori(0, 12) as i:
                for s in range(2):
                    sp.wait_ge(wfree, i * 2 + (s + 1))
                    sp.dma_start(w[:, s, :, :], ada_w[:, :, bass.ds(i * 512 + s * 256, 256)]).then_inc(wfull[s], 16)

        @b.gpsimd
        def _(gp):
            gp.memset(rows[:, :, :], 0.0).then_inc(zeroed, 1)
            gp.memset(K.ones[:, :], 1.0).then_inc(zeroed, 1)
            gp.memset(K.eps[:, :], EPS).then_inc(zeroed, 1)

        @b.tensor
        def _(pe):
            pe.sem_inc(wfree, 2)
            pe.wait_ge(loaded, 16 * (1 + sum(1 for v in VECS if v)))
            for g in range(VGROUPS):
                pe.transpose(bk[0][:, g * P:(g + 1) * P], rows[:, g, :], K.ident[:, :]).then_inc(turned, 1)
            pe.wait_ge(silu_ok, 2)
            with pe.Fori(0, 12) as i:
                for s in range(2):
                    pe.wait_ge(wfull[s], i * 16 + 16)
                    for j in range(2):
                        for k in range(KT):
                            last = pe.matmul(bk[1][:, bass.ds(i * 8 + (s * 4 + j * 2), 2)], w[:, s, k, j * P:(j + 1) * P],
                                             cc[:, k, :], start=(k == 0), stop=(k == KT - 1))
                    last.then_inc(wfree, 1)
            pe.sem_inc(dgfree, 2)
            pe.drain().then_inc(ada_mm, 1)
            pe.wait_ge(zeroed, 3)
            for n in range(16):
                pe.wait_ge(dg, n + 1)
                pe.matmul(bk[2 + n // 4][:, n % 4 * P:(n % 4 + 1) * P], K.ones[:, :], diag[:, n % 2, :],
                          start=True, stop=True).then_inc(dgfree, 1)

        @b.scalar
        def _(act):
            act.wait_ge(cols_ok, 1)
            for j, name in enumerate(("c", "c_ctx")):
                r = PLACES[name][0]
                act.activation(cc[:, :, j], K.cols[:, r:r + 8], ACT.Silu).then_inc(silu_ok, 1)
            for n in range(4):
                act.wait_ge(dgfree, 2 + 4 * (n + 1))
                act.activation(K.gt[:, n // 2, n % 2 * HALF:(n % 2 + 1) * HALF], bk[2 + n][:, :], ACT.Copy)

        @b.vector
        def _(dve):
            step = [0]

            def then(ins):
                step[0] += 1
                ins.then_inc(chain, 1)
                dve.wait_ge(chain, step[0])

            dve.wait_ge(turned, VGROUPS)
            dve.tensor_copy(K.cols[:, :], bk[0][:, 0:VGROUPS * P]).then_inc(cols_ok, 1)
            dve.wait_ge(cols_ok, 1)
            dve.wait_ge(ada_mm, 1)
            r = PLACES["ada_b"][0]
            for j in range(2):
                then(dve.tensor_tensor(ada[:, :, j], bk[1][:, 0:96].rearrange("p (n j) -> p n j", j=2)[:, :, j],
                                       K.cols[:, r:r + 48], ALU.add))
            for out, vecname, sc, sh, j in ((0, "norm1_g", 1, 0, 0), (1, "norm1_g", 1, 0, 1), (2, "norm2_g", 4, 3, 0)):
                g = PLACES[vecname][0]
                then(dve.scalar_tensor_tensor(K.mod[:, out, 0, :], ada[:, sc * 8:sc * 8 + 8, j], 1.0,
                                              K.cols[:, g:g + 8], ALU.add, ALU.mult))
                then(dve.tensor_copy(K.mod[:, out, 1, :], ada[:, sh * 8:sh * 8 + 8, j]))
            for n in range(16):
                col = (16 if n < 8 else 40) + n % 8
                dve.wait_ge(dgfree, n + 1)
                dve.tensor_scalar(diag[:, n % 2, :], K.ident[:, :], ada[:, col, 0:1], None, ALU.mult).then_inc(dg, 1)


def phase_norm(nc, name, src, ntiles, outT, col0, scale, shift, K, src_sb=None, y_dram=None, pre=None):
    with Mem(nc, name) as m:
        xs = m.sb("x", [P, 2, D]) if src_sb is None else None
        sq = m.sb("sq", [P, D])
        ys = m.sb("y", [P, 2, D])
        ss = m.sb("ss", [P, 2, 4])
        bk = m.banks(4)
        xfree, summed, rooted, inv, yok, turned, evac = m.sems(
            "xfree", "summed", "rooted", "inv", "yok", "turned", "evac")
        xin = m.sems("xin0", "xin1")
        ysaved = m.sems("ysaved0", "ysaved1")
        b = m.block()
        tok = lambda i, s: bass.ds(i * 256 + s * P, P)

        def x_of(i, s, lo=0, n=D):
            if src_sb is None:
                return xs[:, s, :]
            return src_sb[:, bass.ds(i * 2 + s, 1), :].rearrange("p a n -> p (a n)")

        @b.sync
        def _(sp):
            if src_sb is None:
                with sp.Fori(0, ntiles // 2) as i:
                    for s in range(2):
                        sp.wait_ge(xfree, i * 2 + (s + 1))
                        sp.dma_start(xs[:, s, :], src[tok(i, s), :]).then_inc(xin[s], 16)
            if y_dram is not None:
                with sp.Fori(0, ntiles // 2) as i:
                    for s in range(2):
                        sp.wait_ge(yok, i * 2 + (s + 1))
                        sp.dma_start(y_dram[tok(i, s), :], ys[:, s, :]).then_inc(ysaved[s], 16)
                for s in range(2):
                    sp.wait_ge(ysaved[s], 16 * (ntiles // 2 + 1))

        @b.scalar
        def _(act):
            act.sem_inc(evac, 4)
            with act.Fori(0, ntiles // 2) as i:
                for s in range(2):
                    if src_sb is None:
                        act.wait_ge(xin[s], i * 16 + 16)
                    act.activation(sq[:, :], x_of(i, s), ACT.Square, accum_out=ss[:, s, 0:1]).then_inc(summed, 1)
                    act.wait_ge(summed, i * 2 + (s + 1))
                    act.activation(ss[:, s, 1:2], ss[:, s, 0:1], ACT.Sqrt, scale=1.0 / D, bias=K.eps[:, 0:1]).then_inc(rooted, 1)
                    for h in range(2):
                        hold(act, turned, i * 4 + (2 * s + h + 1))
                        for q in range(4):
                            k = 4 * h + q
                            o = outT[:, k, bass.ds(i * 256 + (s * P + col0), P)]
                            last = act.activation(o, bk[2 * s + h][:, q * P:(q + 1) * P], ACT.Identity, scale=scale(k),
                                                  bias=shift(k) if shift else 0.0)
                        last.then_inc(evac, 1)

        @b.vector
        def _(dve):
            dve.sem_inc(xfree, 2)
            if y_dram is not None:
                for s in range(2):
                    dve.sem_inc(ysaved[s], 16)
            with dve.Fori(0, ntiles // 2) as i:
                for s in range(2):
                    dve.wait_ge(rooted, i * 2 + (s + 1))
                    dve.reciprocal(ss[:, s, 2:3], ss[:, s, 1:2]).then_inc(inv, 1)
                    dve.wait_ge(inv, i * 2 + (s + 1))
                    dve.wait_ge(evac, i * 4 + (2 * s + 1))
                    if y_dram is not None:
                        dve.wait_ge(ysaved[s], i * 16 + 16)
                    dve.tensor_scalar(ys[:, s, :], x_of(i, s), ss[:, s, 2:3], None, ALU.mult).then_inc(yok, 1)
                    if src_sb is None:
                        dve.wait_ge(yok, i * 2 + (s + 1))
                        dve.sem_inc(xfree, 1)

        @b.tensor
        def _(pe):
            with pe.Fori(0, ntiles // 2) as i:
                for s in range(2):
                    pe.wait_ge(yok, i * 2 + (s + 1))
                    for h in range(2):
                        pe.wait_ge(evac, i * 4 + (2 * s + h + 1))
                        for q in range(4):
                            last = pe.transpose(bk[2 * s + h][:, q * P:(q + 1) * P],
                                                ys[:, s, (4 * h + q) * P:(4 * h + q + 1) * P], K.ident[:, :])
                        last.then_inc(turned, 1)


class Chain:

    def __init__(self, eng, sem, i=None, per=0):
        self.eng, self.sem, self.i, self.per, self.n = eng, sem, i, per, 0

    def __call__(self, ins):
        self.n += 1
        ins.then_inc(self.sem, 1)
        self.eng.wait_ge(self.sem, self.n if self.i is None else self.i * self.per + self.n)

    def end(self):
        assert self.n == self.per, (self.n, self.per)


def phase_proj_T(nc, name, w, kt, xT, ntiles, unroll, evac, uses_dve=False, ntok=SEQ):
    with Mem(nc, name) as m:
        wt = m.sb("w", [P, unroll, kt, P])
        nh = max(1, ntok // HALF)
        width = ntok // nh
        nb = unroll * nh
        bk = m.banks(nb)
        wfull = m.sems(*[f"wfull{s}" for s in range(unroll)])
        wfree, done, free = m.sems("wfree", "done", "free")
        b = m.block()
        steps = ntiles // unroll
        assert steps * unroll == ntiles

        @b.sync
        def _(sp):
            with sp.Fori(0, steps) as i:
                for s in range(unroll):
                    sp.wait_ge(wfree, i * unroll + (s + 1))
                    sp.dma_start(wt[:, s, :, :], w[:, :, bass.ds(i * (unroll * P) + s * P, P)]).then_inc(wfull[s], 16)

        @b.tensor
        def _(pe):
            pe.sem_inc(wfree, unroll)
            with pe.Fori(0, steps) as i:
                for s in range(unroll):
                    pe.wait_ge(wfull[s], i * 16 + 16)
                    for h in range(nh):
                        pe.wait_ge(free, i * nb + (s * nh + h + 1))
                        for k in range(kt):
                            last = pe.matmul(bk[s * nh + h][:, 0:width], wt[:, s, k, :], xT[:, k, h * width:(h + 1) * width],
                                             start=(k == 0), stop=(k == kt - 1))
                        last.then_inc(done, 1)
                    pe.wait_ge(done, i * nb + (s + 1) * nh)
                    pe.sem_inc(wfree, 1)

        wait = (lambda e, sem, n: e.wait_ge(sem, n)) if uses_dve else hold

        def readout(eng):
            eng.sem_inc(free, nb)
            with eng.Fori(0, steps) as i:
                for s in range(unroll):
                    for h in range(nh):
                        wait(eng, done, i * nb + (s * nh + h + 1))
                        evac(eng, i * unroll + s, h, bk[s * nh + h][:, 0:width]).then_inc(free, 1)

        if uses_dve:
            b.vector(readout)
        else:
            b.scalar(readout)


def phase_proj_N(nc, name, w, kt, xT, tok0, ntok_tiles, ngroups, width, evac, uses_dve=False, unroll=2):
    with Mem(nc, name) as m:
        wt = m.sb("w", [P, unroll, kt, width])
        T = ntok_tiles
        nb = min(8, T)
        bk = m.banks(nb)
        wfull = m.sems(*[f"wfull{s}" for s in range(unroll)])
        wfree, done, free = m.sems("wfree", "done", "free")
        b = m.block()
        steps = ngroups // unroll
        assert steps * unroll == ngroups and T == nb

        @b.sync
        def _(sp):
            with sp.Fori(0, steps) as i:
                for s in range(unroll):
                    sp.wait_ge(wfree, i * unroll + (s + 1))
                    sp.dma_start(wt[:, s, :, :], w[:, :, bass.ds(i * (unroll * width) + s * width, width)])\
                      .then_inc(wfull[s], 16)

        @b.tensor
        def _(pe):
            pe.sem_inc(wfree, unroll)
            with pe.Fori(0, steps) as i:
                for s in range(unroll):
                    pe.wait_ge(wfull[s], i * 16 + 16)
                    for t in range(T):
                        pe.wait_ge(free, i * (unroll * T) + (s * T + t + 1))
                        for k in range(kt):
                            last = pe.matmul(bk[t][:, 0:width], xT[:, k, tok0 + t * P:tok0 + (t + 1) * P],
                                             wt[:, s, k, :], start=(k == 0), stop=(k == kt - 1))
                        last.then_inc(done, 1)
                    pe.wait_ge(done, i * (unroll * T) + (s + 1) * T)
                    pe.sem_inc(wfree, 1)

        wait = (lambda e, sem, n: e.wait_ge(sem, n)) if uses_dve else hold

        def readout(eng):
            eng.sem_inc(free, T)
            with eng.Fori(0, steps) as i:
                for s in range(unroll):
                    for t in range(T):
                        wait(eng, done, i * (unroll * T) + (s * T + t + 1))
                        evac(eng, i * unroll + s, t, bk[t][:, 0:width]).then_inc(free, 1)

        if uses_dve:
            b.vector(readout)
        else:
            b.scalar(readout)


RH = 4
RV = 256
KSCALE = 128 ** -0.5


def phase_decay(nc, I, K, R):
    with Mem(nc, "dec") as m:
        z = m.sb("z", [P, 8]); a = m.sb("a", [P, 8]); e = m.sb("e", [P, 8]); l1 = m.sb("l1", [P, 8]); mn = m.sb("mn", [P, 8])
        pos = m.sb("pos", [P, 6, P])
        cpos = m.sb("cpos", [P, 8])
        tmp = m.sb("tmp", [P, 2, P])
        come, chain, ex, lg, tt = m.sems("come", "chain", "ex", "lg", "tt")
        b = m.block()

        @b.sync
        def _(sp):
            sp.dma_start(z[:, :], flat(I["ret_decay_logit"]).rearrange("(a n) -> a n", a=1).to_broadcast([P, 8])).then_inc(come, 16)
            sp.dma_start(pos[:, :, :], I["k_pos"]).then_inc(come, 16)
            sp.dma_start(cpos[:, :], I["k_cpos"]).then_inc(come, 16)

        @b.vector
        def _(dve):
            then = Chain(dve, chain)
            dve.wait_ge(come, 48)
            then(dve.tensor_scalar(mn[:, :], z[:, :], 0.0, None, ALU.min))
            then(dve.scalar_tensor_tensor(a[:, :], z[:, :], -1.0, z[:, :], ALU.mult, ALU.min))
            dve.wait_ge(ex, 2)
            dve.tensor_tensor(R.lg[:, :], mn[:, :], l1[:, :], ALU.subtract).then_inc(lg, 1)
            for h in range(RH):
                for d in range(2):
                    dve.wait_ge(tt, 2 * h + d + 1)
                    then(dve.tensor_tensor(tmp[:, d, :], tmp[:, d, :], pos[:, 4 + d, :], ALU.mult))
                then(dve.tensor_tensor(R.DT[:, h, :], tmp[:, 0, :], tmp[:, 1, :], ALU.add))

        @b.scalar
        def _(act):
            act.wait_ge(chain, 2)
            act.activation(e[:, :], a[:, :], ACT.Exp).then_inc(ex, 1)
            act.wait_ge(ex, 1)
            act.activation(l1[:, :], e[:, :], ACT.Ln, bias=1.0).then_inc(ex, 1)
            act.wait_ge(lg, 1)
            for d in range(2):
                for h in range(RH):
                    c = R.lg[:, d * RH + h:d * RH + h + 1]
                    act.activation(R.DQ[:, h, d, :], pos[:, d, :], ACT.Exp, scale=c)
                    act.activation(R.DC[:, d, h, :], cpos[:, d * 4:d * 4 + 4], ACT.Exp, scale=c)
            for h in range(RH):
                for d in range(2):
                    if h:
                        act.wait_ge(chain, 2 + 3 * h)
                    c = R.lg[:, d * RH + h:d * RH + h + 1]
                    act.activation(tmp[:, d, :], pos[:, 2 + d, :], ACT.Exp, scale=c).then_inc(tt, 1)


def phase_ctx(nc, I, K, R, hcT, w_in):
    with Mem(nc, "ctx") as m:
        kv = m.sb("kv", [P, 2, 1536])
        w = m.sb("w", [P, 3, KT, HALF])
        kd = m.sb("kd", [P, 2, 2, HALF])
        bias = m.sb("bias", [P, 1536])
        bk = m.banks(8)
        w0, w1, w2, done, ev, kds, st = m.sems("w0", "w1", "w2", "done", "ev", "kds", "st")
        wf = [w0, w1, w2]
        b = m.block()

        @b.sync
        def _(sp):
            sp.dma_start(w[:, 0, :, :], w_in[:, :, 512:1024]).then_inc(w0, 16)
            sp.dma_start(w[:, 1, :, :], w_in[:, :, 1024:1536]).then_inc(w1, 16)
            sp.dma_start(bias[:, :], I["b_in"][:, 512:2048].to_broadcast([P, 1536])).then_inc(w2, 16)
            sp.dma_start(w[:, 2, :, :], w_in[:, :, 1536:2048]).then_inc(w2, 16)

        @b.tensor
        def _(pe):
            for g in range(3):
                pe.wait_ge(wf[g], 16 if g < 2 else 32)
                for t in range(2):
                    for k in range(KT):
                        last = pe.matmul(bk[g * 2 + t][:, :], hcT[:, k, t * P:(t + 1) * P], w[:, g, k, :],
                                         start=(k == 0), stop=(k == KT - 1))
                    last.then_inc(done, 1)
            pe.wait_ge(ev, 6)
            pe.wait_ge(kds, 16)
            for d in range(2):
                for h in range(RH):
                    o = bk[d * 2 + h // 2][:, h % 2 * RV:(h % 2 + 1) * RV]
                    for t in range(2):
                        last = pe.matmul(o, kd[:, d, t, h * P:(h + 1) * P], kv[:, t, 512 + h * RV:512 + (h + 1) * RV],
                                         start=(t == 0), stop=(t == 1))
                    last.then_inc(done, 1)

        @b.vector
        def _(dve):
            dve.wait_ge(w2, 32)
            for g in range(3):
                for t in range(2):
                    dve.wait_ge(done, g * 2 + t + 1)
                    dve.tensor_tensor(kv[:, t, g * HALF:(g + 1) * HALF], bk[g * 2 + t][:, :], bias[:, g * HALF:(g + 1) * HALF],
                                      ALU.add).then_inc(ev, 1)
            dve.wait_ge(ev, 6)
            for d in range(2):
                for t in range(2):
                    for h in range(RH):
                        dve.tensor_scalar(kd[:, d, t, h * P:(h + 1) * P], kv[:, t, h * P:(h + 1) * P],
                                          R.DC[:, d, h, 1 + t:2 + t], KSCALE, ALU.mult, ALU.mult).then_inc(kds, 1)
            for d in range(2):
                for h in range(RH):
                    dve.wait_ge(done, 6 + d * 4 + h // 2 * 2 + 2)
                    dve.tensor_copy(R.S0[:, d, h, :], bk[d * 2 + h // 2][:, h % 2 * RV:(h % 2 + 1) * RV])


def phase_retention(nc, I, K, R, qk, v, g, retT, st):
    NCH = SEQ // P
    with Mem(nc, "ret") as m:
        cs = m.sb("cs", [P, 2, SEQ])
        rot = m.sb("rot", [P, P])
        qr = m.sb("qr", [P, 2, SEQ])
        qd = m.sb("qd", [P, 2, SEQ])
        kn = m.sb("kn", [P, 2, NCH, P])
        t1, t2 = (kn[:, j, :, :].rearrange("p c n -> p (c n)") for j in range(2))
        on = qr[:, :, :].rearrange("p j (c n) -> p (j c) n", n=RV)
        sc = m.sb("sc", [P, NCH, P])
        sq = m.sb("sq", [P, 2, RV])
        ss = m.sb("ss", [P, 3, NCH])
        bk = m.banks(8)
        (come, swapped, roped, qdone, kturn, kscaled, scored, masked, upd, stated, outd, ssum, rstd, normed, turned,
         stored, chain, inv) = m.sems(
            "come", "swapped", "roped", "qdone", "kturn", "kscaled", "scored", "masked", "upd", "stated", "outd", "ssum",
            "rstd", "normed", "turned", "stored", "chain", "inv")
        b = m.block()

        @b.sync
        def _(sp):
            sp.dma_start(cs[:, :, :], I["k_rope1"]).then_inc(come, 16)
            sp.dma_start(rot[:, :], I["k_rot1"]).then_inc(come, 16)

        def head(ap, h, off=0):
            return ap[:, bass.ds(h + off, 1), :].rearrange("p a n -> p (a n)")

        @b.tensor
        def _(pe):
            pe.wait_ge(come, 32)
            pe.sem_inc(turned, 1)
            with pe.Fori(0, RH) as h:
                pe.wait_ge(normed, h * NCH + 1)
                for j in range(2):
                    for x in range(2):
                        pe.matmul(bk[2 * j + x][:, :], rot[:, :], qk[:, bass.ds(h + 4 * j, 1), x * HALF:(x + 1) * HALF].rearrange("p a n -> p (a n)"),
                                  start=True, stop=True).then_inc(swapped, 1)
                pe.wait_ge(roped, h * 2 + 2)
                pe.wait_ge(stored, h * 8 + 1)
                for c in range(NCH):
                    cc = slice(c * P, (c + 1) * P)
                    pe.transpose(bk[6 + c // 4][:, c % 4 * P:(c % 4 + 1) * P], qr[:, 1, cc], K.ident[:, :]).then_inc(kturn, 1)
                for c in range(NCH):
                    cc = slice(c * P, (c + 1) * P)
                    pe.matmul(bk[4 + c // 4][:, c % 4 * P:(c % 4 + 1) * P], qr[:, 1, cc], qr[:, 0, cc],
                              start=True, stop=True).then_inc(scored, 1)
                vch = lambda c: v[:, c, bass.ds(h * RV, RV)]
                pe.wait_ge(kscaled, h * 16 + 16)
                pe.wait_ge(masked, h * 2 + 2)
                for d in range(2):
                    for n in range(NCH - 1):
                        c = n if d == 0 else NCH - 1 - n
                        pe.matmul(bk[4 * d + n // 2][:, n % 2 * RV:(n % 2 + 1) * RV], kn[:, d, c, :], vch(c),
                                  start=True, stop=True).then_inc(upd, 1)
                pe.wait_ge(qdone, h * 2 + 2)
                pe.wait_ge(stated, h * 16 + 16)
                for c in range(NCH):
                    cc = slice(c * P, (c + 1) * P)
                    o = bk[c // 2][:, c % 2 * RV:(c % 2 + 1) * RV]
                    pe.matmul(o, sc[:, c, :], vch(c), start=True, stop=False)
                    pe.matmul(o, qd[:, 0, cc], st[:, 0, c, :], start=False, stop=False)
                    pe.matmul(o, qd[:, 1, cc], st[:, 1, c, :], start=False, stop=True).then_inc(outd, 1)
                for c in range(NCH):
                    pe.wait_ge(normed, h * NCH + (c + 2))
                    for x in range(2):
                        pe.transpose(bk[4 + c // 4 + 2 * x][:, c % 4 * P:(c % 4 + 1) * P], on[:, c, x * P:(x + 1) * P],
                                     K.ident[:, :]).then_inc(turned, 1)

        @b.vector
        def _(dve):
            dve.wait_ge(come, 32)
            dve.sem_inc(normed, 1)
            with dve.Fori(0, RH) as h:
                then = Chain(dve, chain, h, 4)
                dve.wait_ge(turned, h * 16 + 1)
                for j in range(2):
                    then(dve.scalar_tensor_tensor(t1, head(qk, h, 4 * j), KSCALE if j else 1.0, cs[:, 0, :],
                                             ALU.mult, ALU.mult))
                    dve.wait_ge(swapped, h * 4 + 2 * j + 2)
                    for x in range(2):
                        xx = slice(x * HALF, (x + 1) * HALF)
                        last = dve.scalar_tensor_tensor(t2[:, xx], bk[2 * j + x][:, :], KSCALE if j else 1.0, cs[:, 1, xx],
                                                        ALU.mult, ALU.mult)
                    then(last)
                    dve.tensor_tensor(qr[:, j, :], t1, t2, ALU.add).then_inc(roped, 1)
                    dve.wait_ge(roped, h * 2 + j + 1)
                then.end()
                for d in range(2):
                    dq = R.DQ[:, bass.ds(h, 1), d, :].to_broadcast([P, NCH, P])
                    dve.tensor_tensor(qd[:, d, :].rearrange("p (c n) -> p c n", n=P),
                                      qr[:, 0, :].rearrange("p (c n) -> p c n", n=P), dq, ALU.mult).then_inc(qdone, 1)
                for x in range(2):
                    dve.wait_ge(scored, h * 8 + 4 * x + 4)
                    dve.tensor_tensor(sc[:, 4 * x:4 * x + 4, :], bk[4 + x][:, :].rearrange("p (c n) -> p c n", n=P),
                                      R.DT[:, bass.ds(h, 1), :].to_broadcast([P, 4, P]), ALU.mult).then_inc(masked, 1)
                for d in range(2):
                    first = 0 if d == 0 else NCH - 1
                    dve.tensor_copy(st[:, d, first, :], head(R.S0[:, d, :, :], h)).then_inc(stated, 1)
                    for n in range(NCH - 1):
                        c, nx = (n, n + 1) if d == 0 else (NCH - 1 - n, NCH - 2 - n)
                        dve.wait_ge(stated, h * 16 + d * 8 + n + 1)
                        dve.wait_ge(upd, h * 14 + (d * 7 + min(n // 2 * 2 + 2, NCH - 1)))
                        dve.scalar_tensor_tensor(st[:, d, nx, :], st[:, d, c, :], R.DC[:, d, bass.ds(h, 1), 3:4].rearrange("p a b -> p (a b)"),
                                                 bk[4 * d + n // 2][:, n % 2 * RV:(n % 2 + 1) * RV], ALU.mult, ALU.add).then_inc(stated, 1)
                dve.wait_ge(rstd, h + 1)
                dve.reciprocal(ss[:, 2, :], ss[:, 1, :]).then_inc(inv, 1)
                dve.wait_ge(inv, h + 1)
                dve.wait_ge(turned, h * 16 + 1)
                for c in range(NCH):
                    dve.scalar_tensor_tensor(on[:, c, :], bk[c // 2][:, c % 2 * RV:(c % 2 + 1) * RV], ss[:, 2, c:c + 1],
                                             g[:, c, bass.ds(h * RV, RV)], ALU.mult, ALU.mult).then_inc(normed, 1)

        @b.scalar
        def _(act):
            act.sem_inc(stored, 1)
            with act.Fori(0, RH) as h:
                for c in range(NCH):
                    hold(act, kturn, h * 8 + (c // 4 * 4 + 4))
                    for d in range(2):
                        act.activation(kn[:, d, c, :], bk[6 + c // 4][:, c % 4 * P:(c % 4 + 1) * P], ACT.Copy,
                                       scale=R.DC[:, d, bass.ds(h, 1), 0:1].rearrange("p a b -> p (a b)")).then_inc(kscaled, 1)
                for c in range(NCH):
                    act.wait_ge(outd, h * 8 + (c // 2 * 2 + 2))
                    if c >= 2:
                        act.wait_ge(ssum, h * 8 + (c - 1))
                    act.activation(sq[:, c % 2, :], bk[c // 2][:, c % 2 * RV:(c % 2 + 1) * RV], ACT.Square,
                                   accum_out=ss[:, 0, c:c + 1]).then_inc(ssum, 1)
                act.wait_ge(ssum, h * 8 + 8)
                act.activation(ss[:, 1, :], ss[:, 0, :], ACT.Sqrt, scale=1.0 / RV, bias=K.eps[:, 0:1]).then_inc(rstd, 1)
                for x in range(2):
                    for y in range(2):
                        hold(act, turned, h * 16 + (8 * y + 9))
                        act.activation(retT[:, bass.ds(h * 2 + x, 1), y * HALF:(y + 1) * HALF].rearrange("p a n -> p (a n)"),
                                       bk[4 + y + 2 * x][:, :], ACT.Copy).then_inc(stored, 2)


C = 512
MAGIC = 12582912.0
TWO_PI_HI, TWO_PI_LO = 6.28125, 0.0019353071795864769
PI_BELOW = 3.1415925


def phase_filters(nc, I, K, he, ho, fl):
    NT = SEQ // P
    with Mem(nc, "filt") as m:
        feats = m.sb("feats", [33, SEQ])
        w1 = m.sb("w1", [33, 64])
        w2 = m.sb("w2", [64, 64])
        w3 = m.sb("w3", [64, 2 * C])
        vecs = m.sb("vecs", [64, 3])
        negt = m.sb("negt", [P, NT])
        delta = m.sb("delta", [P, C])
        arg = m.sb("arg", [64, SEQ])
        turns = m.sb("turns", [64, SEQ])
        hid = m.sb("hid", [64, SEQ])
        dec = m.sb("dec", [P, 2, C])

        ab = m.sb("ab", [P, 2, 2 * C])
        rn = m.sb("rn", [P, 2 * C])
        bk = m.banks(8)
        (come, lin, chain, sine, mm, decs, fls, abss, sums) = m.sems(
            "come", "lin", "chain", "sine", "mm", "decs", "fls", "abss", "sums")
        b = m.block()

        @b.sync
        def _(sp):
            loads = [(feats[:, :], I["k_feats"]), (w1[:, :], I["hy_ffn_w1"][0]), (w2[:, :], I["hy_ffn_w2"][0]),
                     (w3[:, :], I["hy_ffn_w3"][0]), (negt[:, :], I["k_negt"]), (delta[:, :], I["k_delta"])]
            loads += [(vecs[:, j:j + 1], I[n].rearrange("a p -> p a")) for j, n in
                      enumerate(("hy_ffn_b1", "hy_ffn_freq", "hy_ffn_b2"))]
            for dst, src in loads:
                sp.dma_start(dst, src).then_inc(come, 16)

        def norm_sum(pe, t):
            pe.wait_ge(abss, t + 1)
            for x in range(2):
                last = pe.matmul(bk[6 + x][:, :], K.ones[:, :], ab[:, t % 2, x * C:(x + 1) * C], start=(t == 0), stop=(t == NT - 1))
            last.then_inc(sums, 1)

        @b.tensor
        def _(pe):
            pe.wait_ge(come, 16 * 9)
            for x in range(2):
                pe.matmul(bk[x][0:64, :], w1[:, :], feats[:, x * HALF:(x + 1) * HALF], start=True, stop=True).then_inc(lin, 1)
            pe.wait_ge(sine, 1)
            for x in range(2):
                pe.matmul(bk[x][0:64, :], w2[:, :], hid[:, x * HALF:(x + 1) * HALF], start=True, stop=True).then_inc(lin, 1)
            pe.wait_ge(sine, 2)
            for t in range(NT):
                if t >= 2:
                    pe.wait_ge(fls, t - 1)
                for x in range(2):
                    last = pe.matmul(bk[2 + t % 2 * 2 + x][:, :], hid[:, t * P:(t + 1) * P], w3[:, x * C:(x + 1) * C],
                                     start=True, stop=True)
                last.then_inc(mm, 1)
                if t >= 1:
                    norm_sum(pe, t - 1)
            norm_sum(pe, NT - 1)

        @b.scalar
        def _(act):
            for n in range(2):
                act.wait_ge(chain, 6 * (n + 1))
                act.activation(hid[:, :], arg[:, :], ACT.Sin).then_inc(sine, 1)
            for t in range(NT):
                if t >= 2:
                    act.wait_ge(fls, t - 1)
                act.activation(dec[:, t % 2, :], delta[:, :], ACT.Exp, scale=negt[:, t:t + 1]).then_inc(decs, 1)
                act.wait_ge(fls, t + 1)
                if t >= 2:
                    act.wait_ge(sums, t - 1)
                act.activation(ab[:, t % 2, :], fl[:, t, :], ACT.Abs).then_inc(abss, 1)

        @b.vector
        def _(dve):
            then = Chain(dve, chain)
            dve.wait_ge(come, 16 * 9)
            for n in range(2):
                dve.wait_ge(lin, 2 * n + 2)
                if n:
                    dve.wait_ge(sine, 1)
                for x in range(2):
                    last = dve.tensor_scalar(arg[:, x * HALF:(x + 1) * HALF], bk[x][0:64, :], vecs[:, 2 * n:2 * n + 1],
                                             vecs[:, 1:2], ALU.add, ALU.mult)
                then(last)
                then(dve.tensor_scalar(turns[:, :], arg[:, :], float(1 / (2 * np.pi)), MAGIC, ALU.mult, ALU.add))
                then(dve.tensor_scalar(turns[:, :], turns[:, :], MAGIC, None, ALU.subtract))
                then(dve.scalar_tensor_tensor(arg[:, :], turns[:, :], -TWO_PI_HI, arg[:, :], ALU.mult, ALU.add))
                then(dve.scalar_tensor_tensor(arg[:, :], turns[:, :], -TWO_PI_LO, arg[:, :], ALU.mult, ALU.add))
                then(dve.tensor_scalar(arg[:, :], arg[:, :], PI_BELOW, -PI_BELOW, ALU.min, ALU.max))
            for t in range(NT):
                dve.wait_ge(mm, t + 1)
                dve.wait_ge(decs, t + 1)
                for x in range(2):
                    last = dve.tensor_tensor(fl[:, t, x * C:(x + 1) * C], bk[2 + t % 2 * 2 + x][:, :], dec[:, t % 2, :], ALU.mult)
                last.then_inc(fls, 1)
            dve.wait_ge(sums, NT)
            for x in range(2):
                last = dve.reciprocal(rn[:, x * C:(x + 1) * C], bk[6 + x][:, :])
            then(last)
            for t in range(NT):
                last = dve.tensor_tensor(fl[:, t, :], fl[:, t, :], rn[:, :], ALU.mult)
            then(last)
            for t in range(NT):
                dve.tensor_tensor(he[:, t, :], fl[:, t, 0:C], fl[:, t, C:2 * C], ALU.add)
                dve.tensor_tensor(ho[:, t, :], fl[:, t, 0:C], fl[:, t, C:2 * C], ALU.subtract)


def phase_forward(nc, name, I, cos_in, sin_in, H, prod=None, y=None):
    with Mem(nc, name) as m:
        tab = m.sb("tab", [P, 2, 16, P])
        odd = m.sb("odd", [P, 2, C])
        z = m.sb("z", [P, 4, C]) if prod is not None else None
        t = m.sb("t", [P, 4, C]) if prod is not None else None
        bk = m.banks(8)
        full = m.sems("full0", "full1")
        mm, free, copied, outs, chain = m.sems("mm", "free", "copied", "outs", "chain")
        b = m.block()

        @b.sync
        def _(sp):
            for kt in range(4):
                if kt >= 2:
                    sp.wait_ge(mm, 4 * (kt - 1))
                sp.dma_start(tab[:, kt % 2, :, :], I["k_fwd"][kt].rearrange("p (a n) -> p a n", n=P)).then_inc(full[kt % 2], 16)

        @b.tensor
        def _(pe):
            for kt in range(4):
                pe.wait_ge(full[kt % 2], 16 * (kt // 2 + 1))
                if kt >= 2:
                    pe.wait_ge(outs, kt - 1)
                for a in range(4):
                    src = cos_in if a < 2 else sin_in
                    for mt in range(4):
                        last = pe.matmul(bk[kt % 2 * 4 + a][:, :], tab[:, kt % 2, a * 4 + mt, :], src[:, (a % 2) * 4 + mt, :],
                                         start=(mt == 0), stop=(mt == 3))
                    last.then_inc(mm, 1)

        @b.scalar
        def _(act):
            for kt in range(4):
                for j in range(2):
                    act.wait_ge(mm, 4 * kt + (2 if j == 0 else 4))
                    if kt:
                        act.wait_ge(outs, kt)
                    act.activation(odd[:, j, :], bk[kt % 2 * 4 + 1 + 2 * j][:, :], ACT.Copy).then_inc(copied, 1)

        @b.vector
        def _(dve):
            then = Chain(dve, chain)
            for kt in range(4):
                dst = [H[:, kt, n, :] for n in range(4)] if prod is None else [z[:, n, :] for n in range(4)]
                dve.wait_ge(copied, 2 * kt + 2)
                e = [bk[kt % 2 * 4], bk[kt % 2 * 4 + 2]]
                dve.tensor_tensor(dst[0], e[0][:, :], odd[:, 0, :], ALU.add)
                dve.tensor_tensor(dst[1], e[0][:, :], odd[:, 0, :], ALU.subtract)
                dve.tensor_tensor(dst[2], odd[:, 1, :], e[1][:, :], ALU.add)
                dve.tensor_tensor(dst[3], odd[:, 1, :], e[1][:, :], ALU.subtract).then_inc(outs, 1)
                if prod is None:
                    continue
                dve.wait_ge(outs, kt + 1)
                h = [H[:, kt, n, :] for n in range(4)]
                for j in range(2):
                    dve.tensor_tensor(t[:, 0, :], z[:, j, :], h[j], ALU.mult)
                    dve.tensor_tensor(t[:, 1, :], z[:, 2 + j, :], h[2 + j], ALU.mult)
                    dve.tensor_tensor(t[:, 2, :], z[:, j, :], h[2 + j], ALU.mult)
                    then(dve.tensor_tensor(t[:, 3, :], z[:, 2 + j, :], h[j], ALU.mult))
                    dve.tensor_tensor(y[:, j, :], t[:, 0, :], t[:, 1, :], ALU.subtract)
                    then(dve.tensor_tensor(y[:, 2 + j, :], t[:, 2, :], t[:, 3, :], ALU.add))
                dve.tensor_tensor(prod[:, kt, 0, :], y[:, 0, :], y[:, 1, :], ALU.add)
                dve.tensor_tensor(prod[:, kt, 1, :], y[:, 2, :], y[:, 3, :], ALU.subtract)
                dve.tensor_tensor(prod[:, kt, 2, :], y[:, 0, :], y[:, 1, :], ALU.subtract)
                then(dve.tensor_tensor(prod[:, kt, 3, :], y[:, 2, :], y[:, 3, :], ALU.add))


def phase_hyena_in(nc, I, K, w, hT, xc, bcol):
    with Mem(nc, "hin") as m:
        wt = m.sb("w", [P, 2, KT, P])
        up = m.sb("up", [P, 2, SEQ + 2])
        bk = m.banks(4)
        wfull = m.sems("wfull0", "wfull1")
        wfree, done, free, evac, conv, chain, zero = m.sems("wfree", "done", "free", "evac", "conv", "chain", "zero")
        b = m.block()

        @b.sync
        def _(sp):
            with sp.Fori(0, 6) as i:
                for s in range(2):
                    sp.wait_ge(wfree, i * 2 + (s + 1))
                    sp.dma_start(wt[:, s, :, :], w[:, :, bass.ds(i * 256 + s * P, P)]).then_inc(wfull[s], 16)

        @b.gpsimd
        def _(gp):
            for s in range(2):
                for n in (0, SEQ + 1):
                    gp.memset(up[:, s, n:n + 1], 0.0).then_inc(zero, 1)

        @b.tensor
        def _(pe):
            pe.sem_inc(wfree, 2)
            with pe.Fori(0, 6) as i:
                for s in range(2):
                    pe.wait_ge(wfull[s], i * 16 + 16)
                    for h in range(2):
                        pe.wait_ge(free, i * 4 + (s * 2 + h + 1))
                        for k in range(KT):
                            last = pe.matmul(bk[s * 2 + h][:, :], wt[:, s, k, :], hT[:, k, h * HALF:(h + 1) * HALF],
                                             start=(k == 0), stop=(k == KT - 1))
                        last.then_inc(done, 1)
                    pe.wait_ge(done, i * 4 + (s + 1) * 2)
                    pe.sem_inc(wfree, 1)

        @b.scalar
        def _(act):
            act.sem_inc(free, 4)
            with act.Fori(0, 6) as i:
                for s in range(2):
                    act.wait_ge(conv, i * 2 + (s + 1))
                    for h in range(2):
                        hold(act, done, i * 4 + (s * 2 + h + 1))
                        act.activation(up[:, s, 1 + h * HALF:1 + (h + 1) * HALF], bk[s * 2 + h][:, :], ACT.Identity,
                                       bias=K.cols[:, bass.ds(i * 2 + (s + bcol), 1)]).then_inc(evac, 1)
                    act.wait_ge(evac, i * 4 + (s * 2 + 2))
                    act.sem_inc(free, 2)

        @b.vector
        def _(dve):
            dve.sem_inc(conv, 2)
            dve.wait_ge(zero, 4)
            cw, cb = PLACES["hy_conv_w"][0], PLACES["hy_conv_b"][0]
            with dve.Fori(0, 6) as i:
                then = Chain(dve, chain, i, 4)
                for s in range(2):
                    dve.wait_ge(evac, i * 4 + (s * 2 + 2))
                    o = xc[:, bass.ds(i * 2 + s, 1), :].rearrange("p a n -> p (a n)")
                    tap = [K.cols[:, bass.ds(i * 2 + (s + cw + 12 * j), 1)] for j in range(3)]
                    bias = K.cols[:, bass.ds(i * 2 + (s + cb), 1)]
                    then(dve.tensor_scalar(o, up[:, s, 0:SEQ], tap[0], bias, ALU.mult, ALU.add))
                    then(dve.scalar_tensor_tensor(o, up[:, s, 1:SEQ + 1], tap[1], o, ALU.mult, ALU.add))
                    dve.scalar_tensor_tensor(o, up[:, s, 2:SEQ + 2], tap[2], o, ALU.mult, ALU.add).then_inc(conv, 1)
                then.end()


def phase_hyena_turn(nc, K, xc, zn):
    with Mem(nc, "hturn") as m:
        bk = m.banks(8)
        z, tr, = m.sems("z", "tr")
        b = m.block()

        @b.vector
        def _(dve):
            for c in range(4):
                dve.tensor_tensor(xc[:, 4 + c, :], xc[:, 4 + c, :], xc[:, 8 + c, :], ALU.mult).then_inc(z, 1)
            for n in range(8):
                dve.wait_ge(tr, 4 * n + 4)
                dve.tensor_copy(zn[:, n, :], bk[n][:, :])

        @b.tensor
        def _(pe):
            pe.wait_ge(z, 4)
            for par in range(2):
                for mt in range(4):
                    for c in range(4):
                        src = xc[:, 4 + c, :].rearrange("p (n two) -> p two n", two=2)[:, par, mt * P:(mt + 1) * P]
                        pe.transpose(bk[par * 4 + mt][:, c * P:(c + 1) * P], src, K.ident[:, :]).then_inc(tr, 1)


def phase_inverse(nc, I, K, prod, xc, hyT):
    with Mem(nc, "inv") as m:
        tab = m.sb("tab", [P, 2, 8, C])
        t = m.sb("t", [P, 2, C])
        bk = m.banks(8)
        full = m.sems("full0", "full1")
        mm, tdone = m.sems("mm", "tdone")
        b = m.block()

        @b.sync
        def _(sp):
            for par in range(2):
                sp.dma_start(tab[:, par, :, :], I["k_inv"][par].rearrange("p (a n) -> p a n", n=C)).then_inc(full[par], 16)

        @b.tensor
        def _(pe):
            for par in range(2):
                pe.wait_ge(full[par], 16)
                for c in range(4):
                    for n in range(8):
                        a, kt = divmod(n, 4)
                        last = pe.matmul(bk[par * 4 + c][:, :], prod[:, kt, 2 * par + a, c * P:(c + 1) * P],
                                         tab[:, par, n, :], start=(n == 0), stop=(n == 7))
                    last.then_inc(mm, 1)

        @b.vector
        def _(dve):
            split = lambda ap, par: ap.rearrange("p (n two) -> p two n", two=2)[:, par, :]
            for par in range(2):
                for c in range(4):
                    n = par * 4 + c
                    dve.wait_ge(mm, n + 1)
                    dve.scalar_tensor_tensor(t[:, n % 2, :], split(xc[:, 4 + c, :], par), vec(K.cols, "hy_skip", c),
                                             bk[n][:, :], ALU.mult, ALU.add).then_inc(tdone, 1)
                    dve.wait_ge(tdone, n + 1)
                    dve.tensor_tensor(split(hyT[:, c, :], par), t[:, n % 2, :], split(xc[:, c, :], par), ALU.mult)


BIG = 1e30
NG, EG, NE = 4, 8, 32
MAXB = 48


def phase_merge(nc, name, parts, K, mixedT, gate_w, gate_col):
    (wa, ka, aT), (wb, kb, bT) = parts
    wg, hT = gate_w
    nk = 2 * KT + ka + kb
    with Mem(nc, name) as m:
        w = m.sb("w", [P, 2, nk, P])
        sg = m.sb("sg", [P, 2, 2, HALF])
        pr = m.sb("pr", [P, 2, 2, HALF])
        bk = m.banks(8)
        full = m.sems("full0", "full1")
        wfree, mm, sig, prod, summed = m.sems("wfree", "mm", "sig", "prod", "summed")
        b = m.block()
        srcs = [(0, KT, wg, 0), (KT, KT, wg, D), (2 * KT, ka, wa, 0), (2 * KT + ka, kb, wb, 0)]

        @b.sync
        def _(sp):
            with sp.Fori(0, 4) as i:
                for s in range(2):
                    sp.wait_ge(wfree, i * 2 + (s + 1))
                    for k0, n, src, off in srcs:
                        sp.dma_start(w[:, s, k0:k0 + n, :], src[:, :, bass.ds(i * 256 + (s * P + off), P)]).then_inc(full[s], 16)

        @b.tensor
        def _(pe):
            pe.sem_inc(wfree, 2)
            with pe.Fori(0, 4) as i:
                for s in range(2):
                    pe.wait_ge(full[s], i * 64 + 64)
                    for h in range(2):
                        hh = slice(h * HALF, (h + 1) * HALF)
                        pe.wait_ge(sig, i * 8 + (4 * s + 2 * h + 2))
                        pe.wait_ge(prod, i * 8 + (4 * s + 2 * h + 2))
                        for j, (k0, n, x) in enumerate(((0, KT, hT), (KT, KT, hT), (2 * KT, ka, aT), (2 * KT + ka, kb, bT))):
                            for k in range(n):
                                last = pe.matmul(bk[4 * h + j][:, :], w[:, s, k0 + k, :], x[:, k, hh], start=(k == 0), stop=(k == n - 1))
                            last.then_inc(mm, 1)
                    pe.wait_ge(mm, i * 16 + (8 * s + 8))
                    pe.sem_inc(wfree, 1)

        @b.scalar
        def _(act):
            act.sem_inc(sig, 4)
            with act.Fori(0, 4) as i:
                for s in range(2):
                    for h in range(2):
                        act.wait_ge(summed, i * 4 + (2 * s + h + 1))
                        for j in range(2):
                            hold(act, mm, i * 16 + (8 * s + 4 * h + j + 1))
                            act.activation(sg[:, h, j, :], bk[4 * h + j][:, :], ACT.Sigmoid,
                                           bias=K.cols[:, bass.ds(i * 2 + (s + gate_col + 8 * j), 1)]).then_inc(sig, 1)

        @b.vector
        def _(dve):
            dve.sem_inc(prod, 4)
            dve.sem_inc(summed, 2)
            with dve.Fori(0, 4) as i:
                for s in range(2):
                    for h in range(2):
                        for j in range(2):
                            dve.wait_ge(mm, i * 16 + (8 * s + 4 * h + 2 + j + 1))
                            dve.wait_ge(sig, i * 8 + (4 * s + 2 * h + j + 5))
                            dve.tensor_tensor(pr[:, h, j, :], bk[4 * h + 2 + j][:, :], sg[:, h, j, :], ALU.mult).then_inc(prod, 1)
                        dve.wait_ge(prod, i * 8 + (4 * s + 2 * h + 6))
                        dve.tensor_tensor(mixedT[:, bass.ds(i * 2 + s, 1), h * HALF:(h + 1) * HALF].rearrange("p a n -> p (a n)"),
                                          pr[:, h, 0, :], pr[:, h, 1, :], ALU.add).then_inc(summed, 1)


def phase_residual(nc, name, w, xT, X, gate=None):
    with Mem(nc, name) as m:
        wt = m.sb("w", [P, 2, KT, HALF])
        t = m.sb("t", [P, 2, HALF])
        bk = m.banks(8)
        full = m.sems("full0", "full1")
        mm, gated, added = m.sems("mm", "gated", "added")
        b = m.block()

        @b.sync
        def _(sp):
            for g in range(2):
                sp.dma_start(wt[:, g, :, :], w[:, :, g * HALF:(g + 1) * HALF]).then_inc(full[g], 16)

        @b.tensor
        def _(pe):
            for g in range(2):
                pe.wait_ge(full[g], 16)
                for n in range(8):
                    if g:
                        pe.wait_ge(added, n + 1)
                    for k in range(KT):
                        last = pe.matmul(bk[n][:, :], xT[:, k, n * P:(n + 1) * P], wt[:, g, k, :], start=(k == 0), stop=(k == KT - 1))
                    last.then_inc(mm, 1)

        @b.vector
        def _(dve):
            for g in range(2):
                gg = slice(g * HALF, (g + 1) * HALF)
                for n in range(8):
                    dve.wait_ge(mm, 8 * g + n + 1)
                    if gate is None:
                        dve.tensor_tensor(X[:, n, gg], X[:, n, gg], bk[n][:, :], ALU.add).then_inc(added, 1)
                        continue
                    c = 8 * g + n
                    if c >= 2:
                        dve.wait_ge(added, c - 1)
                    dve.tensor_tensor(t[:, c % 2, :], bk[n][:, :], gate[:, gg], ALU.mult).then_inc(gated, 1)
                    dve.wait_ge(gated, c + 1)
                    dve.tensor_tensor(X[:, n, gg], X[:, n, gg], t[:, c % 2, :], ALU.add).then_inc(added, 1)


def phase_rownorm(nc, name, K, X, gain, out=None):
    NT = SEQ // P
    with Mem(nc, name) as m:
        sq = m.sb("sq", [P, 2, D])
        ss = m.sb("ss", [P, 3, NT])
        gr = m.sb("gr", [P, D])
        come, summed, rooted, inv, normed, saved = m.sems("come", "summed", "rooted", "inv", "normed", "saved")
        b = m.block()

        @b.sync
        def _(sp):
            sp.dma_start(gr[:, :], gain.rearrange("(a n) -> a n", a=1).to_broadcast([P, D])).then_inc(come, 16)
            if out is not None:
                for t in range(NT):
                    sp.wait_ge(normed, t + 1)
                    sp.dma_start(out[t * P:(t + 1) * P, :], X[:, t, :]).then_inc(saved, 16)
                sp.wait_ge(saved, 16 * NT)

        @b.scalar
        def _(act):
            for t in range(NT):
                if t >= 2:
                    act.wait_ge(summed, t - 1)
                act.activation(sq[:, t % 2, :], X[:, t, :], ACT.Square, accum_out=ss[:, 0, t:t + 1]).then_inc(summed, 1)
            act.wait_ge(summed, NT)
            act.activation(ss[:, 1, :], ss[:, 0, :], ACT.Sqrt, scale=1.0 / D, bias=K.eps[:, 0:1]).then_inc(rooted, 1)

        @b.vector
        def _(dve):
            dve.wait_ge(rooted, 1)
            dve.reciprocal(ss[:, 2, :], ss[:, 1, :]).then_inc(inv, 1)
            dve.wait_ge(inv, 1)
            dve.wait_ge(come, 16)
            for t in range(NT):
                dve.scalar_tensor_tensor(X[:, t, :], X[:, t, :], ss[:, 2, t:t + 1], gr[:, :], ALU.mult, ALU.mult).then_inc(normed, 1)


def phase_router(nc, name, I, K, uT, rgw, rgb, rew, reb, T, slot_dram):
    NT = SEQ // P
    with Mem(nc, name) as m:
        rw = m.sb("rw", [P, KT, NG + NE])
        rb = m.sb("rb", [P, NG + NE])
        L = m.sb("L", [P, NT, NG + NE])
        rc = m.sb("rc", [P, 3, NE + 16])
        upper = m.sb("upper", [P, P])
        a4 = m.sb("a4", [P, NT, NG]); b4 = m.sb("b4", [P, NT, NG]); g1 = m.sb("g1", [P, NT, 1])
        oh = m.sb("oh", [P, NT, NG]); ps = m.sb("ps", [P, NT, 1])
        big = m.sb("big", [P, NT, NG, EG]); sel = m.sb("sel", [P, NT, EG])
        m12 = m.sb("m12", [P, 2, NT, 1]); o12 = m.sb("o12", [P, 2, NT, EG]); c8 = m.sb("c8", [P, NT, EG]); s2 = m.sb("s2", [P, NT, EG])
        e2 = m.sb("e2", [P, NT, 1]); d2 = m.sb("d2", [P, NT, 1])
        A12 = m.sb("A12", [P, 2, NT, NE]); A = m.sb("A", [P, NT, NE])
        pre = m.sb("pre", [P, NT + 1, NE]); rank = m.sb("rank", [P, NT, NE])
        nbf = m.sb("nbf", [P, NE]); nbi = m.sb("nbi", [P, NE], I32); inc = m.sb("inc", [P, NE]); one = m.sb("one", [P, NE])
        start = m.sb("start", [P, NE])
        df = m.sb("df", [P, 2, NT, 1])
        cmp_ = m.sb("cmp", [1, MAXB, NE]); bef = m.sb("bef", [1, MAXB])
        tok = m.sb("tok", [P, NT], I32); zero = m.sb("zero", [MAXB, P], I32)
        bk = m.banks(3)
        come, mm, ev, chain, ex, az, cnt, pool, zeroed, scat = m.sems("come", "mm", "ev", "chain", "ex", "az", "cnt", "pool", "zeroed", "scat")
        b = m.block()
        slots = slot_dram.rearrange("(b p) -> b p", p=P)

        @b.sync
        def _(sp):
            rk = lambda ap: ap.rearrange("l (k p) n -> p (l k) n", p=P)
            sp.dma_start(rw[:, :, 0:NG], rk(rgw)).then_inc(come, 16)
            sp.dma_start(rw[:, :, NG:], rk(rew)).then_inc(come, 16)
            sp.dma_start(rb[:, 0:NG], rgb.to_broadcast([P, NG])).then_inc(come, 16)
            sp.dma_start(rb[:, NG:], reb.to_broadcast([P, NE])).then_inc(come, 16)
            sp.dma_start(rc[:, :, :], I["k_iotas"]).then_inc(come, 16)
            sp.dma_start(upper[:, :], I["k_upper"]).then_inc(come, 16)
            sp.wait_ge(pool, 2)
            sp.dma_start(slots, zero[:, :]).then_inc(zeroed, 16)

        @b.gpsimd
        def _(gp):
            gp.iota(tok[:, :], pattern=[[P, NT]], base=0, channel_multiplier=1).then_inc(pool, 1)
            gp.memset(zero[:, :], 0).then_inc(pool, 1)
            gp.wait_ge(az, 1)
            gp.wait_ge(pool, 2)
            gp.wait_ge(zeroed, 16)
            for j in range(2):
                for t in range(NT):
                    gp.indirect_dma_start(slot_dram.rearrange("(n a) -> n a", a=1),
                                          bass.IndirectOffsetOnAxis(T.dest[:, j, t:t + 1], 0),
                                          tok[:, t:t + 1], None).then_inc(scat, 16)
            gp.wait_ge(scat, 16 * 2 * NT)

        @b.tensor
        def _(pe):
            pe.wait_ge(come, 16 * 6)
            for t in range(NT):
                for k in range(KT):
                    last = pe.matmul(bk[0][:, t * (NG + NE):(t + 1) * (NG + NE)], uT[:, k, t * P:(t + 1) * P], rw[:, k, :],
                                     start=(k == 0), stop=(k == KT - 1))
            last.then_inc(mm, 1)
            pe.wait_ge(cnt, 1)
            flatA = A[:, :, :].rearrange("p t e -> p (t e)")
            pe.matmul(bk[1][:, 0:NT * NE], upper[:, :], flatA, start=True, stop=True)
            pe.matmul(bk[2][:, 0:NT * NE], K.ones[:, :], flatA, start=True, stop=True).then_inc(mm, 1)

        @b.scalar
        def _(act):
            act.wait_ge(chain, 3)
            act.activation(b4[:, :, :], a4[:, :, :], ACT.Exp).then_inc(ex, 1)
            act.wait_ge(cnt, 1)
            act.activation(e2[:, :, :], d2[:, :, :], ACT.Exp).then_inc(ex, 1)

        @b.vector
        def _(dve):
            then = Chain(dve, chain)
            dve.wait_ge(mm, 1)
            dve.wait_ge(come, 16 * 6)
            bc = lambda ap, n: ap.to_broadcast([P, NT, n])
            row = lambda ap, n: ap.rearrange("p (a n) -> p a n", a=1).to_broadcast([P, NT, n])
            then(dve.tensor_tensor(L[:, :, :], bk[0][:, 0:NT * (NG + NE)].rearrange("p (t n) -> p t n", t=NT), row(rb[:, :], NG + NE), ALU.add))
            LG = L[:, :, 0:NG]
            then(dve.tensor_reduce(g1[:, :, :], LG, AXX, ALU.max))
            then(dve.tensor_tensor(a4[:, :, :], LG, bc(g1[:, :, :], NG), ALU.subtract))
            dve.wait_ge(ex, 1)
            then(dve.tensor_reduce(ps[:, :, :], b4[:, :, :], AXX, ALU.add))
            then(dve.reciprocal(ps[:, :, :], ps[:, :, :]))

            def first(out, scratch, x, best, iota, n):
                then(dve.tensor_tensor(scratch, x, bc(best, n), ALU.is_equal))
                then(dve.tensor_tensor(scratch, scratch, iota, ALU.mult))
                then(dve.tensor_reduce(g1[:, :, :], scratch, AXX, ALU.max))
                then(dve.tensor_tensor(out, scratch, bc(g1[:, :, :], n), ALU.is_equal))

            then(dve.tensor_reduce(g1[:, :, :], LG, AXX, ALU.max))
            then(dve.tensor_tensor(b4[:, :, :], LG, bc(g1[:, :, :], NG), ALU.is_equal))
            then(dve.tensor_tensor(b4[:, :, :], b4[:, :, :], row(rc[:, 0, 0:NG], NG), ALU.mult))
            then(dve.tensor_reduce(g1[:, :, :], b4[:, :, :], AXX, ALU.max))
            then(dve.tensor_tensor(oh[:, :, :], b4[:, :, :], bc(g1[:, :, :], NG), ALU.is_equal))
            for t in range(NT):
                last = dve.tensor_tensor(big[:, t, :, :], L[:, t, NG:].rearrange("p (g e) -> p g e", g=NG),
                                         oh[:, t, :].rearrange("p (g a) -> p g a", a=1).to_broadcast([P, NG, EG]), ALU.mult)
            then(last)
            then(dve.tensor_tensor(sel[:, :, :], big[:, :, 0, :], big[:, :, 1, :], ALU.add))
            then(dve.tensor_tensor(sel[:, :, :], sel[:, :, :], big[:, :, 2, :], ALU.add))
            then(dve.tensor_tensor(sel[:, :, :], sel[:, :, :], big[:, :, 3, :], ALU.add))
            then(dve.tensor_reduce(m12[:, 0, :, :], sel[:, :, :], AXX, ALU.max))
            first(o12[:, 0, :, :], c8[:, :, :], sel[:, :, :], m12[:, 0, :, :], row(rc[:, 1, 0:EG], EG), EG)
            then(dve.scalar_tensor_tensor(s2[:, :, :], o12[:, 0, :, :], -BIG, sel[:, :, :], ALU.mult, ALU.add))
            then(dve.tensor_reduce(m12[:, 1, :, :], s2[:, :, :], AXX, ALU.max))
            first(o12[:, 1, :, :], c8[:, :, :], s2[:, :, :], m12[:, 1, :, :], row(rc[:, 1, 0:EG], EG), EG)
            then(dve.tensor_tensor(d2[:, :, :], m12[:, 1, :, :], m12[:, 0, :, :], ALU.subtract))
            for j in range(2):
                for t in range(NT):
                    last = dve.tensor_tensor(A12[:, j, t, :].rearrange("p (g e) -> p g e", g=NG),
                                             oh[:, t, :].rearrange("p (g a) -> p g a", a=1).to_broadcast([P, NG, EG]),
                                             o12[:, j, t, :].rearrange("p (a e) -> p a e", a=1).to_broadcast([P, NG, EG]), ALU.mult)
            then(last)
            dve.tensor_tensor(A[:, :, :], A12[:, 0, :, :], A12[:, 1, :, :], ALU.add).then_inc(cnt, 1)
            dve.wait_ge(ex, 2)
            then(dve.tensor_scalar(d2[:, :, :], e2[:, :, :], 1.0, None, ALU.add))
            then(dve.reciprocal(d2[:, :, :], d2[:, :, :]))
            w = lambda j: T.wt[:, j, :].rearrange("p (t a) -> p t a", a=1)
            then(dve.tensor_tensor(w(0), ps[:, :, :], d2[:, :, :], ALU.mult))
            then(dve.tensor_tensor(w(1), w(0), e2[:, :, :], ALU.mult))
            dve.wait_ge(mm, 2)
            then(dve.memset(pre[:, 0, :], 0.0))
            for t in range(NT):
                then(dve.tensor_tensor(pre[:, t + 1, :], pre[:, t, :], bk[2][:, t * NE:(t + 1) * NE], ALU.add))
            then(dve.tensor_scalar(nbf[:, :], pre[:, NT, :], float(P - 1), None, ALU.add))
            then(dve.tensor_copy(nbi[:, :], nbf[:, :]))
            then(dve.tensor_scalar(nbi[:, :], nbi[:, :], 7, None, ALU.arith_shift_right))
            then(dve.tensor_copy(nbf[:, :], nbi[:, :]))
            then(dve.memset(one[:, :], 1.0))
            then(dve.tensor_tensor_scan(inc[:, :], one[:, :], nbf[:, :], 0.0, ALU.mult, ALU.add))
            then(dve.tensor_tensor(start[:, :], inc[:, :], nbf[:, :], ALU.subtract))
            then(dve.tensor_tensor(rank[:, :, :], bk[1][:, 0:NT * NE].rearrange("p (t e) -> p t e", t=NT), pre[:, 0:NT, :], ALU.add))
            then(dve.scalar_tensor_tensor(rank[:, :, :], row(start[:, :], NE), float(P), rank[:, :, :], ALU.mult, ALU.add))
            for j in range(2):
                then(dve.tensor_tensor(A12[:, j, :, :], A12[:, j, :, :], rank[:, :, :], ALU.mult))
                then(dve.tensor_reduce(df[:, j, :, :], A12[:, j, :, :], AXX, ALU.add))
            dve.tensor_copy(T.dest[:, :, :], df[:, :, :, :].rearrange("p j t a -> p j (t a)")).then_inc(az, 1)
            then(dve.tensor_tensor(cmp_[:, :, :], inc[0:1, :].rearrange("p (a e) -> p a e", a=1).to_broadcast([1, MAXB, NE]),
                                   rc[0:1, 2, 0:MAXB].rearrange("p (b a) -> p b a", a=1).to_broadcast([1, MAXB, NE]), ALU.is_le))
            then(dve.tensor_reduce(bef[:, :].rearrange("p (b a) -> p b a", a=1), cmp_[:, :, :], AXX, ALU.add))
            then(dve.tensor_scalar(bef[:, :], bef[:, :], float(NE - 1), None, ALU.min))
            dve.tensor_copy(T.be[:, :], bef[:, :])
            then(dve.tensor_scalar(nbf[0:1, 0:1], inc[0:1, NE - 1:NE], 1.0, None, ALU.add))
            then(dve.tensor_copy(nbi[0:1, 0:1], nbf[0:1, 0:1]))
            dve.tensor_scalar(T.nb[:, :], nbi[0:1, 0:1], 1, None, ALU.arith_shift_right)


def phase_experts(nc, name, K, hidden, w1, w3, w2, scale, shift, T, slot_dram, y_dram, out_dram):
    HT = hidden // P
    with Mem(nc, name) as m:
        wu = m.sb("wu", [P, 2, 2, KT, hidden])
        wd = m.sb("wd", [P, 2, HT, D])
        idx = m.sb("idx", [P, 2], I32)
        xg = m.sb("xg", [P, 2, D])
        uT = m.sb("uT", [P, KT, P])
        si = m.sb("si", [P, hidden])
        hh = m.sb("hh", [P, hidden])
        hT = m.sb("hT", [P, HT, P])
        yo = m.sb("yo", [P, 2, D])
        nil = m.sb("nil", [P, D])
        zmade, zsaved = m.sems("zmade", "zsaved")
        bk = m.banks(8)
        wufull = m.sems("wufull0", "wufull1"); wdfull = m.sems("wdfull0", "wdfull1"); ifull = m.sems("ifull0", "ifull1")
        xfull = m.sems("xfull0", "xfull1"); saved = m.sems("saved0", "saved1")
        wufree, wdfree, xt, ux, up, sil, gated, ht, hx, ymm, yout = m.sems(
            "wufree", "wdfree", "xt", "ux", "up", "sil", "gated", "ht", "hx", "ymm", "yout")
        b = m.block()
        slots = slot_dram.rearrange("(b p a) -> p b a", p=P, a=1)
        pairs = dict(min_val=1, max_val=MAXB // 2)

        @b.sync
        def _(sp):
            n = sp.value_load(T.nb[0:1, 0:1], **pairs)
            with sp.Fori(0, n) as i:
                for s in range(2):
                    e = sp.value_load(T.be[0:1, bass.ds(i * 2 + s, 1)], min_val=0, max_val=NE - 1)
                    sp.wait_ge(wufree, i * 2 + (s + 1))
                    for j, wj in enumerate((w1, w3)):
                        sp.dma_start(wu[:, s, j, :, :], wj[:, bass.ds(e, 1), :, :].rearrange("p a k n -> p (a k) n")).then_inc(wufull[s], 16)
                    sp.wait_ge(wdfree, i * 2 + (s + 1))
                    sp.dma_start(wd[:, s, :, :], w2[:, bass.ds(e, 1), :, :].rearrange("p a k n -> p (a k) n")).then_inc(wdfull[s], 16)
                sp.sem_inc(zsaved, 32)
            sp.wait_ge(zmade, 1)
            with sp.Fori(n, MAXB // 2 + 1) as i:
                sp.dma_start(out_dram[bass.ds(i * 256, P), :], nil[:, :]).then_inc(zsaved, 16)
                sp.dma_start(out_dram[bass.ds(i * 256 + P, P), :], nil[:, :]).then_inc(zsaved, 16)
            sp.wait_ge(zsaved, 32 * (MAXB // 2 + 1))

        @b.gpsimd
        def _(gp):
            gp.memset(nil[:, :], 0.0).then_inc(zmade, 1)
            n = gp.value_load(T.nb[0:1, 0:1], **pairs)
            with gp.Fori(0, n) as i:
                for s in range(2):
                    gp.wait_ge(xt, i * 2 + (s + 1))
                    gp.dma_start(idx[:, s:s + 1], slots[:, bass.ds(i * 2 + s, 1), :].rearrange("p b a -> p (b a)")).then_inc(ifull[s], 16)
                    hold(gp, ifull[s], i * 16 + 16)
                    gp.indirect_dma_start(xg[:, s, :], None, y_dram, bass.IndirectOffsetOnAxis(idx[:, s:s + 1], 0)).then_inc(xfull[s], 16)

        @b.tensor
        def _(pe):
            n = pe.value_load(T.nb[0:1, 0:1], **pairs)
            pe.sem_inc(wufree, 2)
            pe.sem_inc(wdfree, 2)
            pe.sem_inc(xt, 2)
            with pe.Fori(0, n) as i:
                for s in range(2):
                    c = i * 2 + s
                    pe.wait_ge(xfull[s], i * 16 + 16)
                    pe.wait_ge(ux, i * 4 + (2 * s + 2))
                    for k in range(KT):
                        last = pe.transpose(bk[k // 4][:, k % 4 * P:(k % 4 + 1) * P], xg[:, s, k * P:(k + 1) * P], K.ident[:, :])
                    last.then_inc(xt, 1)
                    pe.wait_ge(ux, i * 4 + (2 * s + 4))
                    pe.wait_ge(wufull[s], i * 32 + 32)
                    pe.wait_ge(gated, i * 2 + (s + 1))
                    for j in range(2):
                        for k in range(KT):
                            last = pe.matmul(bk[2 + j][:, 0:hidden], uT[:, k, :], wu[:, s, j, k, :], start=(k == 0), stop=(k == KT - 1))
                        last.then_inc(up, 1)
                    pe.wait_ge(up, i * 4 + (2 * s + 2))
                    pe.sem_inc(wufree, 1)
                    pe.wait_ge(gated, i * 2 + (s + 2))
                    for k in range(HT):
                        last = pe.transpose(bk[4][:, k * P:(k + 1) * P], hh[:, k * P:(k + 1) * P], K.ident[:, :])
                    last.then_inc(ht, 1)
                    pe.wait_ge(hx, i * 2 + (s + 1))
                    pe.wait_ge(wdfull[s], i * 16 + 16)
                    pe.wait_ge(yout, i * 4 + (2 * s + 2))
                    for j in range(2):
                        for k in range(HT):
                            last = pe.matmul(bk[5 + j][:, :], hT[:, k, :], wd[:, s, k, j * HALF:(j + 1) * HALF], start=(k == 0), stop=(k == HT - 1))
                        last.then_inc(ymm, 1)
                    pe.wait_ge(ymm, i * 4 + (2 * s + 2))
                    pe.sem_inc(wdfree, 1)

        @b.scalar
        def _(act):
            n = act.value_load(T.nb[0:1, 0:1], **pairs)
            act.sem_inc(ux, 2)
            with act.Fori(0, n) as i:
                for s in range(2):
                    act.wait_ge(xt, i * 2 + (s + 3))
                    act.wait_ge(up, i * 4 + 2 * s) if s else None
                    for k in range(KT):
                        last = act.activation(uT[:, k, :], bk[k // 4][:, k % 4 * P:(k % 4 + 1) * P], ACT.Identity, scale=scale(k),
                                              bias=shift(k) if shift else 0.0)
                        if k % 4 == 3:
                            last.then_inc(ux, 1)
                    act.wait_ge(up, i * 4 + (2 * s + 1))
                    act.activation(si[:, :], bk[2][:, 0:hidden], ACT.Silu).then_inc(sil, 1)
                    for j in range(2):
                        act.wait_ge(ymm, i * 4 + (2 * s + j + 1))
                        if j == 0:
                            act.wait_ge(saved[s], i * 16 + 16)
                        act.activation(yo[:, s, j * HALF:(j + 1) * HALF], bk[5 + j][:, :], ACT.Copy).then_inc(yout, 1)
                    act.wait_ge(yout, i * 4 + (2 * s + 4))
                    act.dma_start(out_dram[bass.ds(i * 256 + s * P, P), :], yo[:, s, :]).then_inc(saved[s], 16)
            for s in range(2):
                hold(act, saved[s], n * 16 + 16)

        @b.vector
        def _(dve):
            n = dve.value_load(T.nb[0:1, 0:1], **pairs)
            dve.sem_inc(gated, 1)
            dve.sem_inc(yout, 2)
            for s in range(2):
                dve.sem_inc(saved[s], 16)
            with dve.Fori(0, n) as i:
                for s in range(2):
                    dve.wait_ge(sil, i * 2 + (s + 1))
                    dve.wait_ge(up, i * 4 + (2 * s + 2))
                    dve.tensor_tensor(hh[:, :], si[:, :], bk[3][:, 0:hidden], ALU.mult).then_inc(gated, 1)
                    dve.wait_ge(ht, i * 2 + (s + 1))
                    dve.tensor_copy(hT[:, :, :].rearrange("p k n -> p (k n)"), bk[4][:, 0:hidden]).then_inc(hx, 1)


def phase_combine(nc, name, X, T, out_dram, gate=None):
    NT = SEQ // P
    with Mem(nc, name) as m:
        g = m.sb("g", [P, 2, 2, D])
        a = m.sb("a", [P, 2, D])
        full = m.sems("full0", "full1")
        free, chain = m.sems("free", "chain")
        b = m.block()

        @b.gpsimd
        def _(gp):
            for t in range(NT):
                if t >= 2:
                    gp.wait_ge(free, t - 1)
                for j in range(2):
                    gp.indirect_dma_start(g[:, t % 2, j, :], None, out_dram[0:MAXB * P, :], bass.IndirectOffsetOnAxis(T.dest[:, j, t:t + 1], 0)).then_inc(full[t % 2], 16)

        @b.vector
        def _(dve):
            then = Chain(dve, chain)
            for t in range(NT):
                s = t % 2
                dve.wait_ge(full[s], 32 * (t // 2 + 1))
                then(dve.tensor_scalar(a[:, s, :], g[:, s, 0, :], T.wt[:, 0, t:t + 1], None, ALU.mult))
                dve.scalar_tensor_tensor(a[:, s, :], g[:, s, 1, :], T.wt[:, 1, t:t + 1], a[:, s, :], ALU.mult, ALU.add).then_inc(free, 1)
                dve.wait_ge(free, t + 1)
                if gate is not None:
                    then(dve.tensor_tensor(a[:, s, :], a[:, s, :], gate, ALU.mult))
                then(dve.tensor_tensor(X[:, t, :], X[:, t, :], a[:, s, :], ALU.add))


RC = 512
NP = 4
CH = 64
NC = SEQ // CH
DECAY = float(np.exp(-0.5))
LNX_EPS = 64e-5
LEVELS = 5


def phase_taps(nc, name, w, xT, zc, ntiles, unroll, tap, bias=None):
    with Mem(nc, name) as m:
        wt = m.sb("w", [P, unroll, KT, P])
        up = m.sb("up", [P, unroll, SEQ + 2])
        nb = 2 * unroll
        bk = m.banks(nb)
        wfull = m.sems(*[f"wfull{s}" for s in range(unroll)])
        wfree, done, free, evac, conv, chain, zero = m.sems("wfree", "done", "free", "evac", "conv", "chain", "zero")
        b = m.block()
        steps = ntiles // unroll
        assert steps * unroll == ntiles

        @b.sync
        def _(sp):
            with sp.Fori(0, steps) as i:
                for s in range(unroll):
                    sp.wait_ge(wfree, i * unroll + (s + 1))
                    sp.dma_start(wt[:, s, :, :], w[:, :, bass.ds(i * (unroll * P) + s * P, P)]).then_inc(wfull[s], 16)

        @b.gpsimd
        def _(gp):
            for s in range(unroll):
                for n in (0, SEQ + 1):
                    gp.memset(up[:, s, n:n + 1], 0.0).then_inc(zero, 1)

        @b.tensor
        def _(pe):
            pe.sem_inc(wfree, unroll)
            with pe.Fori(0, steps) as i:
                for s in range(unroll):
                    pe.wait_ge(wfull[s], i * 16 + 16)
                    for h in range(2):
                        pe.wait_ge(free, i * nb + (s * 2 + h + 1))
                        for k in range(KT):
                            last = pe.matmul(bk[s * 2 + h][:, :], wt[:, s, k, :], xT[:, k, h * HALF:(h + 1) * HALF],
                                             start=(k == 0), stop=(k == KT - 1))
                        last.then_inc(done, 1)
                    pe.wait_ge(done, i * nb + (s + 1) * 2)
                    pe.sem_inc(wfree, 1)

        @b.scalar
        def _(act):
            act.sem_inc(free, nb)
            with act.Fori(0, steps) as i:
                for s in range(unroll):
                    act.wait_ge(conv, i * unroll + (s + 1))
                    for h in range(2):
                        hold(act, done, i * nb + (s * 2 + h + 1))
                        act.activation(up[:, s, 1 + h * HALF:1 + (h + 1) * HALF], bk[s * 2 + h][:, :], ACT.Identity,
                                       bias=bias(i * unroll + s) if bias else 0.0).then_inc(evac, 1)
                    act.wait_ge(evac, i * nb + (s * 2 + 2))
                    act.sem_inc(free, 2)

        @b.vector
        def _(dve):
            dve.sem_inc(conv, unroll)
            dve.wait_ge(zero, 2 * unroll)
            with dve.Fori(0, steps) as i:
                then = Chain(dve, chain, i, 2 * unroll)
                for s in range(unroll):
                    t = i * unroll + s
                    dve.wait_ge(evac, i * nb + (s * 2 + 2))
                    o = zc[:, bass.ds(t, 1), :].rearrange("p a n -> p (a n)")
                    then(dve.tensor_scalar(o, up[:, s, 0:SEQ], tap(0, t), tap(3, t), ALU.mult, ALU.add))
                    then(dve.scalar_tensor_tensor(o, up[:, s, 1:SEQ + 1], tap(1, t), o, ALU.mult, ALU.add))
                    dve.scalar_tensor_tensor(o, up[:, s, 2:SEQ + 2], tap(2, t), o, ALU.mult, ALU.add).then_inc(conv, 1)
                then.end()


def phase_rwkv_consts(nc, I, K, W):
    with Mem(nc, "rwc") as m:
        come, s = m.sems("come", "s")
        b = m.block()

        @b.sync
        def _(sp):
            for dst, src in ((W.tri[:, :, :, :], I["k_tri"]), (W.level[:, :, :, :], I["k_level"]),
                             (W.headones[:, :], I["k_headones"]), (W.carry[:, :], I["k_carry"]), (W.eye64[:, :], I["k_eye64"]),
                             (W.wup[:, :], I["w_up_2"].rearrange("l d r c -> (l d r) c")),
                             (W.aup[:, :], I["a_up_2"].rearrange("l d r c -> (l d r) c")), (W.gup[:, :], I["g_up_2"][0])):
                sp.dma_start(dst, src).then_inc(come, 16)
            sp.wait_ge(come, 16 * 8)

        @b.vector
        def _(dve):
            p, n = PLACES["mu_prev_2"][0], PLACES["mu_next_2"][0]
            k = PLACES["k_a_2"][0]
            dve.tensor_tensor(W.mid[:, :], K.cols[:, p:p + 15], K.cols[:, n:n + 15], ALU.add).then_inc(s, 1)
            dve.wait_ge(s, 1)
            dve.tensor_scalar(W.mid[:, :], W.mid[:, :], -1.0, 1.0, ALU.mult, ALU.add)
            dve.tensor_scalar(W.ka1[:, :], K.cols[:, k:k + 4], -1.0, 1.0, ALU.mult, ALU.add)
            dve.memset(W.lnx_eps[:, :], LNX_EPS)
            dve.memset(W.zero[:, :], 0.0)


def phase_rwkv_gates(nc, Z):
    with Mem(nc, "rwg") as m:
        b = m.block()

        @b.scalar
        def _(act):
            act.activation(Z[:, 12, :], Z[:, 12, :], ACT.Tanh)
            act.activation(Z[:, 14, :], Z[:, 14, :], ACT.Sigmoid)


def phase_rwkv_prep(nc, K, W, Z, p, pr, elc, bv):
    with Mem(nc, f"rp{p}") as m:
        sw = m.sb("sw", [P, 2, SEQ]); ag = m.sb("ag", [P, 2, SEQ]); kk = m.sb("kk", [P, SEQ]); sq = m.sb("sq", [P, SEQ])
        cs = m.sb("cs", [P, 2, SEQ]); ex = m.sb("ex", [P, 2, SEQ]); E = m.sb("E", [P, 3, SEQ]); kd = m.sb("kd", [P, 2, SEQ])
        bk = m.banks(8)
        mm, sg, chain, act_done, ew, totok = m.sems("mm", "sg", "chain", "act_done", "ew", "totok")
        r, k, v = Z[:, p, :], Z[:, 4 + p, :], Z[:, 8 + p, :]
        hs = [slice(0, HALF), slice(HALF, SEQ)]
        NORM, PER = 5, 6
        b = m.block()

        @b.tensor
        def _(pe):
            for j, (up, src) in enumerate(((W.wup, 12), (W.aup, 13))):
                for d in range(2):
                    dd = slice(64 * d, 64 * d + 64)
                    for x in range(2):
                        pe.matmul(bk[4 * j + 2 * d + x][:, :], up[dd, p * P:(p + 1) * P], Z[dd, src, hs[x]], start=True, stop=True).then_inc(mm, 1)
            pe.wait_ge(sg, 8)
            pe.wait_ge(act_done, 1)
            for x in range(2):
                pe.matmul(bk[x][:, :], W.headones[:, :], sq[:, hs[x]], start=True, stop=True).then_inc(mm, 1)
            pe.wait_ge(ew, 1)
            for x in range(2):
                pe.matmul(bk[2 + x][:, :], W.headones[:, :], sq[:, hs[x]], start=True, stop=True).then_inc(mm, 1)

        @b.scalar
        def _(act):
            for j, (dst, name) in enumerate(((sw, "w0_2"), (ag, "a0_2"))):
                for d in range(2):
                    for x in range(2):
                        act.wait_ge(mm, 4 * j + 2 * d + x + 1)
                        act.activation(dst[:, d, hs[x]], bk[4 * j + 2 * d + x][:, :], ACT.Sigmoid, bias=vec(K.cols, name, 4 * d + p)).then_inc(sg, 1)
            act.wait_ge(chain, 1)
            act.activation(sq[:, :], kk[:, :], ACT.Square).then_inc(act_done, 1)
            for x in range(2):
                act.wait_ge(mm, 9 + x)
                act.activation(E[:, 0, hs[x]], bk[x][:, :], ACT.Sqrt).then_inc(act_done, 1)
            for d in range(2):
                act.wait_ge(chain, NORM + d * PER + 3)
                act.activation(E[:, 0, :], cs[:, d, :], ACT.Exp, scale=-DECAY)
                act.activation(E[:, 1, :], cs[:, d, :], ACT.Exp, scale=DECAY)
                act.activation(E[:, 2, :], ex[:, d, :], ACT.Exp, scale=-DECAY)
                act.activation(elc[:, d, :], W.tot[:, d, :], ACT.Exp, scale=-DECAY).then_inc(act_done, 1)

        @b.vector
        def _(dve):
            then = Chain(dve, chain)
            then(dve.tensor_scalar(kk[:, :], k, vec(K.cols, "k_k_2", p), None, ALU.mult))
            dve.wait_ge(act_done, 3)
            then(dve.tensor_scalar(E[:, 0, :], E[:, 0, :], 1e-12, None, ALU.max))
            then(dve.reciprocal(E[:, 0, :], E[:, 0, :]))
            then(dve.tensor_tensor(kk[:, :], kk[:, :], E[:, 0, :], ALU.mult))
            dve.wait_ge(sg, 8)
            for d in range(2):
                last = dve.tensor_scalar(kd[:, d, :], ag[:, d, :], vec(K.cols, "k_a_2", p), W.ka1[:, p:p + 1], ALU.mult, ALU.add)
            then(last)
            assert then.n == NORM
            for d in range(2):
                n0 = then.n
                t3 = lambda ap: ap.rearrange("p (c n) -> p c n", n=CH)
                then(dve.tensor_tensor_scan(cs[:, d, :], W.carry[:, :], sw[:, d, :], 0.0, ALU.mult, ALU.add))
                if d == 0:
                    then(dve.tensor_tensor(ex[:, 0, :], cs[:, 0, :], sw[:, 0, :], ALU.subtract))
                    then(dve.tensor_copy(W.tot[:, 0, :], t3(cs[:, 0, :])[:, :, CH - 1]))
                else:
                    dve.tensor_copy(W.tot[:, 1, :], t3(cs[:, 1, :])[:, :, CH - 1]).then_inc(totok, 1)
                    dve.wait_ge(totok, 1)
                    then(dve.tensor_tensor(t3(ex[:, 1, :]), t3(cs[:, 1, :])[:, :, CH - 1:CH].to_broadcast([P, NC, CH]), t3(cs[:, 1, :]), ALU.subtract))
                    then(dve.tensor_tensor(cs[:, 1, :], ex[:, 1, :], sw[:, 1, :], ALU.add))
                dve.tensor_tensor(kd[:, d, :], kd[:, d, :], k, ALU.mult)
                then(dve.tensor_tensor(ag[:, d, :], ag[:, d, :], kk[:, :], ALU.mult))
                dve.wait_ge(act_done, 4 + d)
                dve.scalar_tensor_tensor(pr[:, d, 0, :], kk[:, :], -1.0, E[:, 2, :], ALU.mult, ALU.mult)
                dve.tensor_tensor(pr[:, d, 1, :], ag[:, d, :], E[:, 1, :], ALU.mult)
                dve.tensor_tensor(pr[:, d, 2, :], kd[:, d, :], E[:, 1, :], ALU.mult)
                then(dve.tensor_tensor(pr[:, d, 3, :], r, E[:, 0, :], ALU.mult))
                if d == 0:
                    then(dve.memset(W.junk[:, :], 0.0))
                else:
                    then(dve.tensor_tensor(kk[:, :], kd[:, 0, :], kd[:, 1, :], ALU.add))
                assert then.n == n0 + PER
            dve.scalar_tensor_tensor(sq[:, :], kk[:, :], vec(K.cols, "r_k_2", p), r, ALU.mult, ALU.mult).then_inc(ew, 1)
            for x in range(2):
                dve.wait_ge(mm, 11 + x)
                dve.tensor_tensor(bv[:, hs[x]], bk[2 + x][:, :], v[:, hs[x]], ALU.mult)


PE_O = ["b0", "b1", "b2", "b3", "x1", "akv"] + [f"{s}{l}" for l in range(1, 6) for s in ("p1_", "p23_")] + ["w", "qg", "h0", "s1", "y", "s2"]
ACT_O = ["aN", "bN", "kvN", "x1", "akv"] + [f"p1_{l}" for l in range(1, 6)] + ["w", "h"]
DVE_O = ["ATb", "ATk"] + [f"xy{l}" for l in range(1, 6)] + ["qg", "s1", "s2", "y"]
POOL_O = ["fillA", "fillR", "y1"] + [f"m{l}" for l in range(1, 6)]


def count(order, i, name):
    return i * len(order) + (order.index(name) + 2)


def phase_rwkv_chunks(nc, K, W, Z, p, pr, elc, Y):
    with Mem(nc, f"rc{p}") as m:
        sb2 = lambda name, shape: [m.sb(f"{name}{d}", [P] + shape) for d in range(2)]
        ar = sb2("ar", [2, 2, P])
        bT, kT, vT = sb2("bT", [2, P]), sb2("kT", [2, P]), sb2("vT", [2, P])
        ri = sb2("ri", [2, 2, P])
        lev = sb2("lev", [6, 2, P])
        arb = sb2("arb", [2, 3, P])
        ark = sb2("ark", [2, 2, P])
        rw = sb2("rw", [2, 2, P])
        kv = sb2("kv", [2, 2, P])
        xy = sb2("xy", [2, 2, P])
        p1 = sb2("p1", [2, P])
        w = sb2("w", [2, 2, P])
        qg = sb2("qg", [2, 2, P])
        hh = sb2("hh", [2, P])
        S = sb2("S", [P])
        bk8 = m.banks(8)
        bk = [bk8[0:4], bk8[4:8]]
        pes, acs, dvs, pos = m.sems("pe0", "pe1"), m.sems("act0", "act1"), m.sems("dve0", "dve1"), m.sems("pool0", "pool1")
        zeroed, = m.sems("zeroed")
        xyinit = m.sems("xyinit0", "xyinit1")
        b = m.block()
        STEPS = NC // 2
        b4 = lambda bank: bank[:, :].rearrange("p (j x n) -> p j x n", j=2, x=2)
        bj = lambda bank, j: bank[:, j * P:(j + 1) * P]
        b2 = lambda bank, half=0: bank[:, half * 256:half * 256 + 256].rearrange("p (j n) -> p j n", j=2)
        tok0 = lambda it, d: it * 128 if d == 0 else it * -128 + 14 * CH
        order = lambda d: (0, 1) if d == 0 else (1, 0)

        @b.gpsimd
        def _(gp):
            for d in range(2):
                gp.memset(S[d][:, :], 0.0).then_inc(zeroed, 1)
            gp.wait_ge(zeroed, 2)
            for d in range(2):
                for j in range(2):
                    gp.tensor_copy(ri[d][:, j, 1, :], K.ident[:, :])
            for d in range(2):
                gp.sem_inc(pos[d], 1)
            with gp.Fori(0, STEPS) as it:
                for d in range(2):
                    def spread(dst, src):
                        for j in range(2):
                            last = gp.tensor_tensor(dst[:, j, :].rearrange("p (h n) -> p h n", h=2),
                                                    src[:, bass.ds(tok0(it, d) + j * CH, CH)].rearrange("p (a n) -> p a n", a=1).to_broadcast([P, 2, CH]),
                                                    W.headones[:, :].rearrange("p (h n) -> p h n", h=2), ALU.mult)
                        return last
                    hold(gp, pes[d], it * len(PE_O) + 1)
                    spread(ar[d][:, :, 0, :], pr[:, d, 0, :])
                    spread(ar[d][:, :, 1, :], pr[:, d, 3, :])
                    spread(bT[d], pr[:, d, 1, :])
                    spread(kT[d], pr[:, d, 2, :])
                    spread(vT[d], Z[:, 8 + p, :]).then_inc(pos[d], 1)
                    hold(gp, dvs[d], it * len(DVE_O) + 1)
                    spread(ri[d][:, :, 0, :], pr[:, d, 3, :]).then_inc(pos[d], 1)
                for d in range(2):
                    hold(gp, dvs[d], count(DVE_O, it, "ATb"))
                    lv = lambda l: W.level[:, d, l:l + 1, :].to_broadcast([P, 2, P])
                    for l in range(6):
                        ins = gp.tensor_tensor(lev[d][:, l, :, :], arb[d][:, :, 0, :], lv(l), ALU.mult)
                        ins.then_inc(pos[d], 1)

        @b.tensor
        def _(pe):
            pe.wait_ge(zeroed, 2)
            for d in range(2):
                pe.sem_inc(pes[d], 1)
            with pe.Fori(0, STEPS) as it:
                at = lambda sems, o, d, name: pe.wait_ge(sems[d], count(o, it, name))
                for d in range(2):
                    B = bk[d]
                    at(pos, POOL_O, d, "fillA")
                    pe.wait_ge(dvs[d], it * len(DVE_O) + 1)
                    pe.wait_ge(acs[d], it * len(ACT_O) + 1)
                    for j in range(2):
                        last = pe.matmul(B[0][:, j * 256:(j + 1) * 256], bT[d][:, j, :], ar[d][:, j, :, :].rearrange("p x n -> p (x n)"), start=True, stop=True)
                    last.then_inc(pes[d], 1)
                    for j in range(2):
                        last = pe.matmul(B[1][:, j * 256:(j + 1) * 256], kT[d][:, j, :], ar[d][:, j, :, :].rearrange("p x n -> p (x n)"), start=True, stop=True)
                    last.then_inc(pes[d], 1)
                    for j in range(2):
                        pe.transpose(bj(B[2], j), ar[d][:, j, 0, :], K.ident[:, :])
                    for j in range(2):
                        last = pe.transpose(bj(B[2], 2 + j), bT[d][:, j, :], K.ident[:, :])
                    last.then_inc(pes[d], 1)
                    for j in range(2):
                        pe.transpose(bj(B[3], j), kT[d][:, j, :], K.ident[:, :])
                    for j in range(2):
                        last = pe.transpose(bj(B[3], 2 + j), vT[d][:, j, :], K.ident[:, :])
                    last.then_inc(pes[d], 1)
                for d in range(2):
                    at(dvs, DVE_O, d, "ATk")
                    at(acs, ACT_O, d, "kvN")
                    for j in range(2):
                        last = pe.matmul(bj(bk[d][1], j), ark[d][:, j, 0, :], kv[d][:, 1, j, :], start=True, stop=True)
                    at(pos, POOL_O, d, "y1")
                    pe.wait_ge(xyinit[d], it + 1)
                    for j in range(2):
                        last2 = pe.transpose(bj(bk[d][0], j), xy[d][:, 1, j, :], K.ident[:, :])
                    last2.then_inc(pes[d], 2)
                for l in range(1, 6):
                    for d in range(2):
                        at(pos, POOL_O, d, f"m{l}")
                        if l == 1:
                            at(acs, ACT_O, d, "akv")
                        else:
                            at(dvs, DVE_O, d, f"xy{l - 1}")
                        for j in range(2):
                            last = pe.matmul(bj(bk[d][2], j), lev[d][:, l, j, :], xy[d][:, 0, j, :], start=True, stop=True)
                        last.then_inc(pes[d], 1)
                    for d in range(2):
                        at(acs, ACT_O, d, f"p1_{l}")
                        if l < 5:
                            for j in range(2):
                                pe.matmul(bj(bk[d][3], j), xy[d][:, 1, j, :], p1[d][:, j, :], start=True, stop=True)
                        for j in range(2):
                            last = pe.matmul(bj(bk[d][3], 2 + j), p1[d][:, j, :], xy[d][:, 1, j, :], start=True, stop=True)
                        last.then_inc(pes[d], 1)
                for d in range(2):
                    at(dvs, DVE_O, d, "xy5")
                    for j in range(2):
                        last = pe.matmul(bk[d][0][:, j * 256:(j + 1) * 256], xy[d][:, 1, j, :], rw[d][:, j, :, :].rearrange("p x n -> p (x n)"), start=True, stop=True)
                    last.then_inc(pes[d], 1)
                for d in range(2):
                    at(acs, ACT_O, d, "w")
                    for j in range(2):
                        last = pe.matmul(bk[d][1][:, j * 256:(j + 1) * 256], w[d][:, j, 0, :], arb[d][:, j, 1:3, :].rearrange("p x n -> p (x n)"), start=True, stop=True)
                    last.then_inc(pes[d], 1)
                    for j in range(2):
                        pe.matmul(bj(bk[d][2], j), arb[d][:, j, 2, :], w[d][:, j, 1, :], start=True, stop=False)
                        last = pe.matmul(bj(bk[d][2], j), kv[d][:, 0, j, :], kv[d][:, 1, j, :], start=False, stop=True)
                    last.then_inc(pes[d], 1)
                for n in range(2):
                    for d in range(2):
                        j = order(d)[n]
                        at(dvs, DVE_O, d, "qg" if n == 0 else "s1")
                        y = lambda: (pe.matmul(bj(bk[d][3], j), qg[d][:, j, 0, :], S[d][:, :], start=True, stop=False),
                                     pe.matmul(bj(bk[d][3], j), arb[d][:, j, 1, :], w[d][:, j, 1, :], start=False, stop=False),
                                     pe.matmul(bj(bk[d][3], j), ark[d][:, j, 1, :], kv[d][:, 1, j, :], start=False, stop=True))[-1]
                        if n == 0:
                            y()
                        else:
                            y().then_inc(pes[d], 1)
                        pe.matmul(bj(bk[d][0], j), qg[d][:, j, 1, :], S[d][:, :], start=True, stop=True).then_inc(pes[d], 1)

        @b.scalar
        def _(act):
            for d in range(2):
                act.sem_inc(acs[d], 1)
            with act.Fori(0, STEPS) as it:
                at = lambda sems, o, d, name: hold(act, sems[d], count(o, it, name))
                for d in range(2):
                    at(pes, PE_O, d, "b2")
                    act.activation(rw[d][:, :, 0, :], b2(bk[d][2]), ACT.Copy).then_inc(acs[d], 1)
                    act.activation(arb[d][:, :, 2, :], b2(bk[d][2], 1), ACT.Copy).then_inc(acs[d], 1)
                    at(pes, PE_O, d, "b3")
                    act.activation(kv[d][:, :, :, :].rearrange("p x j n -> p (x j n)"), bk[d][3][:, :], ACT.Copy).then_inc(acs[d], 1)
                for d in range(2):
                    at(pes, PE_O, d, "akv")
                    act.activation(xy[d][:, 0, :, :], b2(bk[d][0]), ACT.Copy).then_inc(acs[d], 1)
                    act.activation(rw[d][:, :, 1, :], b2(bk[d][1]), ACT.Copy).then_inc(acs[d], 1)
                for l in range(1, 6):
                    for d in range(2):
                        at(pes, PE_O, d, f"p1_{l}")
                        act.activation(p1[d][:, :, :], b2(bk[d][2]), ACT.Copy).then_inc(acs[d], 1)
                for d in range(2):
                    at(pes, PE_O, d, "w")
                    act.activation(w[d][:, :, :, :].rearrange("p j x n -> p (j x n)"), bk[d][0][:, :], ACT.Copy).then_inc(acs[d], 1)
                for d in range(2):
                    at(pes, PE_O, d, "h0")
                    for j in range(2):
                        c = it * 2 + j if d == 0 else it * -2 + (14 + j)
                        last = act.activation(hh[d][:, j, :], bj(bk[d][2], j), ACT.Copy, scale=elc[:, d, bass.ds(c, 1)])
                    last.then_inc(acs[d], 1)

        @b.vector
        def _(dve):
            for d in range(2):
                dve.sem_inc(dvs[d], 1)
            with dve.Fori(0, STEPS) as it:
                at = lambda sems, o, d, name: dve.wait_ge(sems[d], count(o, it, name))
                for d in range(2):
                    tri = W.tri[:, d:d + 1, :, :].to_broadcast([P, 2, 2, P])
                    at(pes, PE_O, d, "b0")
                    dve.tensor_tensor(arb[d][:, :, 0:2, :].rearrange("p j x n -> p j (x n)"), bk[d][0][:, :].rearrange("p (j n) -> p j n", j=2),
                                      W.tri[:, d:d + 1, :, :].rearrange("p a x n -> p a (x n)").to_broadcast([P, 2, 256]), ALU.mult).then_inc(dvs[d], 1)
                    at(pes, PE_O, d, "b1")
                    dve.tensor_tensor(ark[d][:, :, :, :].rearrange("p j x n -> p j (x n)"), bk[d][1][:, :].rearrange("p (j n) -> p j n", j=2),
                                      W.tri[:, d:d + 1, :, :].rearrange("p a x n -> p a (x n)").to_broadcast([P, 2, 256]), ALU.mult).then_inc(dvs[d], 1)
                for d in range(2):
                    at(pos, POOL_O, d, "y1")
                    dve.tensor_tensor(xy[d][:, 1, :, :], lev[d][:, 0, :, :], ri[d][:, :, 1, :], ALU.add).then_inc(xyinit[d], 1)
                for l in range(1, 6):
                    for d in range(2):
                        at(pes, PE_O, d, f"p23_{l}")
                        if l < 5:
                            x = xy[d][:, :, :, :].rearrange("p x j n -> p (x j n)")
                            ins = dve.tensor_tensor(x, x, bk[d][3][:, :], ALU.add)
                        else:
                            ins = dve.tensor_tensor(xy[d][:, 1, :, :], xy[d][:, 1, :, :], b2(bk[d][3], 1), ALU.add)
                        ins.then_inc(dvs[d], 1)
                for d in range(2):
                    at(pes, PE_O, d, "qg")
                    at(pos, POOL_O, d, "fillR")
                    dve.tensor_tensor(qg[d][:, :, :, :].rearrange("p j x n -> p (j x n)"), bk[d][1][:, :],
                                      ri[d][:, :, :, :].rearrange("p j x n -> p (j x n)"), ALU.add).then_inc(dvs[d], 1)
                for n in range(2):
                    for d in range(2):
                        j = order(d)[n]
                        c = it * 2 + j if d == 0 else it * -2 + (14 + j)
                        at(acs, ACT_O, d, "h")
                        at(pes, PE_O, d, f"s{n + 1}")
                        dve.scalar_tensor_tensor(S[d][:, :], bj(bk[d][0], j), elc[:, d, bass.ds(c, 1)], hh[d][:, j, :], ALU.mult, ALU.add).then_inc(dvs[d], 1)
                for d in range(2):
                    at(pes, PE_O, d, "y")
                    c = it * 2 if d == 0 else it * -2 + 14
                    dve.tensor_reduce(Y[:, d, bass.ds(c, 2), :].rearrange("p c v -> p (c v)").rearrange("p (c v a) -> p c v a", c=2, a=1),
                                      bk[d][3][:, 0:256].rearrange("p (j h v) -> p j v h", j=2, h=2), AXX, ALU.add).then_inc(dvs[d], 1)


def phase_rwkv_out(nc, K, W, Z, p, Y, bv):
    with Mem(nc, f"ro{p}") as m:
        y2 = m.sb("y2", [P, NC, CH]); st = m.sb("st", [P, 4, NC, 1]); t = m.sb("t", [P, SEQ])
        bk = m.banks(4)
        chain, rooted, mm = m.sems("chain", "rooted", "mm")
        b = m.block()
        hs = [slice(0, HALF), slice(HALF, SEQ)]

        @b.vector
        def _(dve):
            then = Chain(dve, chain)
            bc = lambda n: st[:, n, :, :].to_broadcast([P, NC, CH])
            then(dve.tensor_tensor(Y[:, 0, :, :], Y[:, 0, :, :], Y[:, 1, :, :], ALU.add))
            then(dve.tensor_reduce(st[:, 0, :, :], Y[:, 0, :, :], AXX, ALU.add))
            then(dve.tensor_scalar(st[:, 1, :, :], st[:, 0, :, :], 1.0 / CH, None, ALU.mult))
            then(dve.tensor_tensor(Y[:, 0, :, :], Y[:, 0, :, :], bc(1), ALU.subtract))
            then(dve.tensor_tensor(y2[:, :, :], Y[:, 0, :, :], Y[:, 0, :, :], ALU.mult))
            then(dve.tensor_reduce(st[:, 2, :, :], y2[:, :, :], AXX, ALU.add))
            dve.wait_ge(rooted, 1)
            then(dve.reciprocal(st[:, 3, :, :], st[:, 3, :, :]))
            then(dve.tensor_tensor(Y[:, 0, :, :], Y[:, 0, :, :], bc(3), ALU.mult))
            dve.wait_ge(mm, 4)
            for x in range(2):
                last = dve.tensor_scalar(t[:, hs[x]], bk[x][:, :], vec(K.cols, "lnx_g_2", p), vec(K.cols, "lnx_b_2", p), ALU.mult, ALU.add)
            then(last)
            then(dve.tensor_tensor(t[:, :], t[:, :], bv[:, :], ALU.add))
            for x in range(2):
                dve.tensor_tensor(Z[:, p, hs[x]], t[:, hs[x]], bk[2 + x][:, :], ALU.mult)

        @b.scalar
        def _(act):
            act.wait_ge(chain, 6)
            act.activation(st[:, 3, :, :], st[:, 2, :, :], ACT.Sqrt, scale=1.0 / CH, bias=W.lnx_eps[:, 0:1]).then_inc(rooted, 1)

        @b.tensor
        def _(pe):
            for x in range(2):
                pe.matmul(bk[2 + x][:, :], W.gup[:, p * P:(p + 1) * P], Z[:, 14, hs[x]], start=True, stop=True).then_inc(mm, 1)
            pe.wait_ge(chain, 8)
            for x in range(2):
                for c in range(8):
                    for h in range(2):
                        hp = slice(64 * h, 64 * h + 64)
                        last = pe.matmul(bk[x][hp, c * CH:(c + 1) * CH], Y[hp, 0, x * 8 + c, :], W.eye64[hp, :], start=True, stop=True)
                last.then_inc(mm, 1)


QL, KVL, ROPE, NOPE = 384, 256, 32, 64
MH = 8
LQ = KVL + QL
MSCALE = float((NOPE + ROPE) ** -0.5)


def phase_mla_norm(nc, name, K, zm, cT):
    NT = SEQ // P
    parts = ((0, QL, 0, 3, "q_norm_g_2"), (QL, KVL, 3, 2, "kv_norm_g_2"))
    with Mem(nc, name) as m:
        sq = m.sb("sq", [P, 2, LQ])
        ss = m.sb("ss", [P, 3, 2, NT])
        bk = m.banks(4)
        squared, rooted, inv, normed, turned, evac = m.sems("squared", "rooted", "inv", "normed", "turned", "evac")
        b = m.block()

        @b.scalar
        def _(act):
            for t in range(NT):
                if t >= 2:
                    act.wait_ge(squared, 2 * (t - 1))
                for j, (c0, n, _, _, _) in enumerate(parts):
                    act.activation(sq[:, t % 2, c0:c0 + n], zm[:, t, c0:c0 + n], ACT.Square, accum_out=ss[:, 0, j, t:t + 1]).then_inc(squared, 1)
            act.wait_ge(squared, 2 * NT)
            for j, (_, n, _, _, _) in enumerate(parts):
                act.activation(ss[:, 1, j, :], ss[:, 0, j, :], ACT.Sqrt, scale=1.0 / n, bias=K.eps[:, 0:1]).then_inc(rooted, 1)
            act.sem_inc(evac, 4)
            with act.Fori(0, NT // 2) as i:
                for s in range(2):
                    for j, (_, _, k0, kn, gain) in enumerate(parts):
                        hold(act, turned, i * 4 + (2 * s + j + 1))
                        for k in range(kn):
                            last = act.activation(cT[:, k0 + k, bass.ds(i * 256 + s * P, P)], bk[2 * s + j][:, k * P:(k + 1) * P],
                                                  ACT.Copy, scale=vec(K.cols, gain, k))
                        last.then_inc(evac, 1)

        @b.vector
        def _(dve):
            dve.wait_ge(rooted, 2)
            dve.reciprocal(ss[:, 2, :, :], ss[:, 1, :, :]).then_inc(inv, 1)
            dve.wait_ge(inv, 1)
            for t in range(NT):
                for j, (c0, n, _, _, _) in enumerate(parts):
                    last = dve.tensor_scalar(zm[:, t, c0:c0 + n], zm[:, t, c0:c0 + n], ss[:, 2, j, t:t + 1], None, ALU.mult)
                last.then_inc(normed, 1)

        @b.tensor
        def _(pe):
            for t in range(NT):
                pe.wait_ge(normed, t + 1)
                for j, (c0, _, _, kn, _) in enumerate(parts):
                    pe.wait_ge(evac, 2 * t + j + 1)
                    for k in range(kn):
                        last = pe.transpose(bk[2 * (t % 2) + j][:, k * P:(k + 1) * P], zm[:, t, c0 + k * P:c0 + (k + 1) * P], K.ident[:, :])
                    last.then_inc(turned, 1)


def phase_mla_values(nc, name, I, w_in, w_ukv, hT, cT, rope, KTs, V):
    with Mem(nc, name) as m:
        wr = m.sb("wr", [P, KT, 64]); wv = m.sb("wv", [P, 2, MH, NOPE])
        fold = m.sb("fold", [P, 64]); t = m.sb("t", [P, SEQ])
        bk = m.banks(8)
        wcome, vcome, mm, turned, folded, vmm, ev = m.sems("wcome", "vcome", "mm", "turned", "folded", "vmm", "ev")
        b = m.block()

        @b.sync
        def _(sp):
            r0, half = LQ, ROPE // 2
            sp.dma_start(wr[:, :, 0:32], w_in[:, :, r0:r0 + 32]).then_inc(wcome, 16)
            sp.dma_start(wr[:, :, 32:48], w_in[:, :, r0 + half:r0 + 32]).then_inc(wcome, 16)
            sp.dma_start(wr[:, :, 48:64], w_in[:, :, r0:r0 + half]).then_inc(wcome, 16)
            sp.dma_start(fold[:, :], I["k_fold"]).then_inc(wcome, 16)
            sp.dma_start(rope[:, :], I["k_rope2"]).then_inc(wcome, 16)
            for k in range(2):
                sp.dma_start(wv[:, k, :, :], w_ukv[:, k, :].rearrange("p (h n) -> p h n", n=128)[:, :, 64:128]).then_inc(vcome, 16)

        @b.tensor
        def _(pe):
            pe.wait_ge(wcome, 80)
            for h in range(2):
                for k in range(KT):
                    last = pe.matmul(bk[h][64:128, :], wr[:, k, :], hT[:, k, h * HALF:(h + 1) * HALF], start=(k == 0), stop=(k == KT - 1))
                last.then_inc(mm, 1)
            for h in range(2):
                pe.wait_ge(turned, h + 1)
                pe.matmul(bk[2 + h][64:128, :], fold[64:128, :], t[64:128, h * HALF:(h + 1) * HALF], start=True, stop=True).then_inc(folded, 1)
            pe.wait_ge(vcome, 32)
            for n in range(8):
                if n >= 4:
                    pe.wait_ge(ev, n - 3)
                for k in range(2):
                    last = pe.matmul(bk[4 + n % 4][:, :], cT[:, 3 + k, n * P:(n + 1) * P], wv[:, k, :, :].rearrange("p h n -> p (h n)"),
                                     start=(k == 0), stop=(k == 1))
                last.then_inc(vmm, 1)

        @b.vector
        def _(dve):
            for h in range(2):
                hh = slice(h * HALF, (h + 1) * HALF)
                dve.wait_ge(mm, h + 1)
                dve.tensor_tensor(t[64:128, hh], bk[h][64:128, :], rope[64:128, hh], ALU.mult).then_inc(turned, 1)
            for n in range(8):
                dve.wait_ge(vmm, n + 1)
                dve.tensor_copy(V[:, n, :], bk[4 + n % 4][:, :]).then_inc(ev, 1)

        @b.scalar
        def _(act):
            for h in range(2):
                act.wait_ge(folded, h + 1)
                for s in range(2):
                    act.activation(KTs[64:128, s, h * HALF:(h + 1) * HALF], bk[2 + h][64:128, :], ACT.Copy, scale=MSCALE)


def phase_mla_heads(nc, name, K, w_uq, w_ukv, cT, rope, KTs, V, oN):
    NQ = SEQ // P
    with Mem(nc, name) as m:
        wq = m.sb("wq", [P, 2, 3, P]); wk = m.sb("wk", [P, 2, 2, NOPE])
        QT = m.sb("QT", [P, 2, SEQ])
        pb = m.sb("pb", [P, 2, SEQ]); pt = m.sb("pt", [P, 2, NQ, P])
        mx = m.sb("mx", [P, 2]); sm = m.sb("sm", [P, 2]); rs = m.sb("rs", [P, 2])
        sc = [m.stack.enter_context(nc.psum_tensor(f"{name}_sc{n}", [P, SEQ], F32)) for n in range(2)]
        bk = m.banks(4)
        tb, ob = bk[0:2], bk[2:4]
        full = m.sems("full0", "full1")
        wfree, proj, qe, ke, sdone, mxed, exped, tdone, pt0, pt1, odone, inv, oout = m.sems(
            "wfree", "proj", "qe", "ke", "sdone", "mxed", "exped", "tdone", "pt0", "pt1", "odone", "inv", "oout")
        b = m.block()
        NP2 = MH // 2

        @b.sync
        def _(sp):
            with sp.Fori(0, NP2) as i:
                for s in range(2):
                    q0 = i * 192 + s * 96
                    sp.wait_ge(wfree, i * 2 + (s + 1))
                    sp.dma_start(wq[:, s, :, 0:96], w_uq[:, :, bass.ds(q0, 96)]).then_inc(full[s], 16)
                    sp.dma_start(wq[:, s, :, 96:112], w_uq[:, :, bass.ds(q0 + 80, 16)]).then_inc(full[s], 16)
                    sp.dma_start(wq[:, s, :, 112:128], w_uq[:, :, bass.ds(q0 + 64, 16)]).then_inc(full[s], 16)
                    sp.dma_start(wk[:, s, :, :], w_ukv[:, :, bass.ds(i * 256 + s * P, NOPE)]).then_inc(full[s], 16)

        @b.tensor
        def _(pe):
            pe.sem_inc(wfree, 2)
            pe.sem_inc(tdone, 1)
            with pe.Fori(0, NP2) as i:
                for s in range(2):
                    c = lambda u, o=1: i * (2 * NQ) + (s * NQ + u + o)

                    def scores(u):
                        if u >= 2:
                            pe.wait_ge(exped, c(u, 0))
                        for h in range(2):
                            last = pe.matmul(sc[u % 2][:, h * HALF:(h + 1) * HALF], QT[:, s, u * P:(u + 1) * P],
                                             KTs[:, s, h * HALF:(h + 1) * HALF], start=True, stop=True)
                        last.then_inc(sdone, 1)

                    def turn(u):
                        pe.wait_ge(exped, c(u, 2))
                        for x in range(2):
                            pe.wait_ge((pt0, pt1)[x], c(u))
                            for k in range(4):
                                last = pe.transpose(tb[x][:, k * P:(k + 1) * P], pb[:, u % 2, (4 * x + k) * P:(4 * x + k + 1) * P], K.ident[:, :])
                            last.then_inc(tdone, 1)

                    def values(u):
                        pe.wait_ge(oout, c(u))
                        for k in range(NQ):
                            if k == 0:
                                pe.wait_ge(pt0, c(u, 2))
                            if k == 4:
                                pe.wait_ge(pt1, c(u, 2))
                            last = pe.matmul(ob[u % 2][:, 0:P], pt[:, u % 2, k, :], V[:, k, bass.ds(i * P, P)], start=(k == 0), stop=(k == NQ - 1))
                        last.then_inc(odone, 1)

                    pe.wait_ge(full[s], i * 64 + 64)
                    pe.wait_ge(exped, c(0))
                    for h in range(2):
                        for k in range(3):
                            last = pe.matmul(sc[0][:, h * HALF:(h + 1) * HALF], wq[:, s, k, :], cT[:, k, h * HALF:(h + 1) * HALF], start=(k == 0), stop=(k == 2))
                    last.then_inc(proj, 1)
                    for h in range(2):
                        for k in range(2):
                            last = pe.matmul(sc[1][0:64, h * HALF:(h + 1) * HALF], wk[:, s, k, :], cT[:, 3 + k, h * HALF:(h + 1) * HALF], start=(k == 0), stop=(k == 1))
                    last.then_inc(proj, 1)
                    pe.wait_ge(proj, i * 4 + (2 * s + 2))
                    pe.sem_inc(wfree, 1)
                    pe.wait_ge(qe, i * 2 + (s + 1))
                    pe.wait_ge(ke, i * 2 + (s + 1))
                    scores(0)
                    for u in range(NQ):
                        if u + 1 < NQ:
                            scores(u + 1)
                        if u:
                            values(u - 1)
                        turn(u)
                    values(NQ - 1)

        @b.scalar
        def _(act):
            act.sem_inc(exped, 1)
            with act.Fori(0, NP2) as i:
                for s in range(2):
                    c = lambda u, o=1: i * (2 * NQ) + (s * NQ + u + o)

                    def exps(u):
                        hold(act, mxed, c(u))
                        hold(act, tdone, i * (4 * NQ) + (2 * (s * NQ + u) + 1))
                        hold(act, oout, c(u))
                        act.activation(pb[:, u % 2, :], sc[u % 2][:, :], ACT.Exp, bias=mx[:, u % 2:u % 2 + 1], accum_out=sm[:, u % 2:u % 2 + 1]).then_inc(exped, 1)

                    hold(act, proj, i * 4 + (2 * s + 2))
                    act.activation(KTs[0:64, s, :], sc[1][0:64, :], ACT.Copy, scale=MSCALE).then_inc(ke, 1)
                    exps(0)
                    for u in range(NQ):
                        if u + 1 < NQ:
                            exps(u + 1)
                        hold(act, tdone, i * (4 * NQ) + (2 * (s * NQ + u) + 3))
                        hold(act, odone, c(u))
                        act.activation(pt[:, u % 2, 4:8, :].rearrange("p k n -> p (k n)"), tb[1][:, :], ACT.Copy).then_inc(pt1, 1)

        @b.vector
        def _(dve):
            dve.sem_inc(pt0, 1)
            dve.sem_inc(pt1, 1)
            dve.sem_inc(oout, 2)
            dve.sem_inc(odone, 2)
            with dve.Fori(0, NP2) as i:
                for s in range(2):
                    c = lambda u, o=1: i * (2 * NQ) + (s * NQ + u + o)

                    def maxima(u):
                        dve.wait_ge(sdone, c(u))
                        dve.wait_ge(exped, c(u, 0)) if s * NQ + u >= 1 else None
                        dve.tensor_reduce(mx[:, u % 2:u % 2 + 1], sc[u % 2][:, :], AXX, ALU.max, negate=True).then_inc(mxed, 1)

                    def out(u):
                        dve.reciprocal(rs[:, u % 2:u % 2 + 1], sm[:, u % 2:u % 2 + 1]).then_inc(inv, 1)
                        dve.wait_ge(inv, c(u))
                        dve.wait_ge(odone, c(u, 3))
                        o = oN[:, u, bass.ds(i * P + s * NOPE, NOPE)]
                        dve.tensor_scalar(o, ob[u % 2][:, s * NOPE:(s + 1) * NOPE], rs[:, u % 2:u % 2 + 1], None, ALU.mult).then_inc(oout, 1)

                    dve.wait_ge(proj, i * 4 + (2 * s + 1))
                    dve.tensor_tensor(QT[:, s, :], sc[0][:, :], rope[:, :], ALU.mult).then_inc(qe, 1)
                    maxima(0)
                    for u in range(NQ):
                        if u + 1 < NQ:
                            maxima(u + 1)
                        if u:
                            out(u - 1)
                        dve.wait_ge(tdone, i * (4 * NQ) + (2 * (s * NQ + u) + 2))
                        dve.wait_ge(odone, c(u))
                        dve.tensor_copy(pt[:, u % 2, 0:4, :].rearrange("p k n -> p (k n)"), tb[0][:, :]).then_inc(pt0, 1)
                    out(NQ - 1)


def phase_turn_out(nc, name, K, oN, oT):
    with Mem(nc, name) as m:
        bk = m.banks(8)
        mm, = m.sems("mm")
        b = m.block()

        @b.tensor
        def _(pe):
            for n in range(8):
                f, h = divmod(n, 2)
                for q in range(4):
                    last = pe.transpose(bk[n][:, q * P:(q + 1) * P], oN[:, 4 * h + q, f * P:(f + 1) * P], K.ident[:, :])
                last.then_inc(mm, 1)

        @b.vector
        def _(dve):
            for n in range(0, 8, 2):
                dve.wait_ge(mm, n + 1)
                dve.tensor_copy(oT[:, n // 2, 0:HALF], bk[n][:, :])

        @b.scalar
        def _(act):
            for n in range(1, 8, 2):
                act.wait_ge(mm, n + 1)
                act.activation(oT[:, n // 2, HALF:SEQ], bk[n][:, :], ACT.Copy)


def mla(nc, I, K, w_in, hT, oT):
    rr = lambda n: I[n].rearrange("l (k p) n -> p (l k) n", p=P)
    with Mem(nc, "mla") as m:
        cT = m.sb("cT", [P, 5, SEQ])
        rope = m.sb("rope", [P, SEQ]); KTs = m.sb("KTs", [P, 2, SEQ]); V = m.sb("V", [P, 8, MH * NOPE])
        with Mem(nc, "mlz") as mz:
            zm = mz.sb("zm", [P, 8, LQ])
            phase_proj_N(nc, "mp", w_in[:, :, 0:LQ], KT, hT, 0, 8, 2, LQ // 2,
                         lambda e, g, t, ps: e.tensor_copy(zm[:, t, bass.ds(g * (LQ // 2), LQ // 2)], ps), uses_dve=True)
            phase_mla_norm(nc, "mn", K, zm, cT)
        phase_mla_values(nc, "mv", I, w_in, rr("w_ukv_2"), hT, cT, rope, KTs, V)
        with Mem(nc, "mlo") as mo:
            oN = mo.sb("oN", [P, 8, MH * NOPE])
            phase_mla_heads(nc, "mh", K, rr("w_uq_2"), rr("w_ukv_2"), cT, rope, KTs, V, oN)
            phase_turn_out(nc, "mt", K, oN, oT)


def phase_move(nc, name, pairs):
    with Mem(nc, name) as m:
        moved, = m.sems("moved")
        b = m.block()

        @b.sync
        def _(sp):
            for dst, src in pairs:
                sp.dma_start(dst, src).then_inc(moved, 16)
            sp.wait_ge(moved, 16 * len(pairs))


def phase_silu(nc, name, t):
    with Mem(nc, name) as m:
        b = m.block()

        @b.scalar
        def _(act):
            act.activation(t, t, ACT.Silu)


def one(ap):
    return ap.rearrange("p a n -> p (a n)")


def rows_to_tiles(ap):
    return ap.rearrange("l (k p) n -> p (l k) n", p=P)


def experts_to_tiles(ap):
    return ap.rearrange("l e (k p) n -> p (l e) k n", p=P)


def retention_branch(nc, I, K, w_in, hT, spare):
    with Mem(nc, "ret") as m:
        R = Named()
        R.lg = m.sb("lg", [P, 8])
        R.DQ = m.sb("DQ", [P, RH, 2, P])
        R.DC = m.sb("DC", [P, 2, RH, 4])
        R.DT = m.sb("DT", [P, RH, P])
        R.S0 = m.sb("S0", [P, 2, RH, RV])
        phase_decay(nc, I, K, R)
        with Mem(nc, "ctx") as mc:
            hcT = mc.sb("hcT", [P, KT, CTX])
            phase_norm(nc, "ctxnorm", I["ctx"][0], 2, hcT, 0, lambda k: K.mod[:, 1, 0, k:k + 1], lambda k: K.mod[:, 1, 1, k:k + 1], K)
            phase_ctx(nc, I, K, R, hcT, w_in)
        qk = m.sb("qk", [P, 8, SEQ]); v = m.sb("v", [P, 8, D]); g = K.X
        b0 = PLACES["b_in"][0]
        phase_proj_T(nc, "qkproj", w_in[:, :, 0:D], KT, hT, 8, 2,
                     lambda e, t, h, ps: e.activation(one(qk[:, bass.ds(t, 1), h * HALF:(h + 1) * HALF]), ps, ACT.Identity,
                                                      bias=K.cols[:, bass.ds(t + b0, 1)]))
        with Mem(nc, "vg") as mb:
            bb = mb.sb("bb", [P, 2 * D])
            phase_move(nc, "vgbias", [(bb[:, :], I["b_in"][:, D:3 * D].to_broadcast([P, 2 * D]))])
            for name, dst, off in (("vproj", v, 0), ("gproj", g, D)):
                phase_proj_N(nc, name, w_in[:, :, D + off:2 * D + off], KT, hT, 0, 8, 4, 256,
                             lambda e, gr, t, ps, dst=dst, off=off: e.tensor_tensor(
                                 dst[:, t, bass.ds(gr * 256, 256)], ps, bb[:, bass.ds(gr * 256 + off, 256)], ALU.add), uses_dve=True)
        phase_silu(nc, "gsilu", g[:, :, :].rearrange("p a n -> p (a n)"))
        phase_retention(nc, I, K, R, qk, v, g, hT, spare.rearrange("p (d a) (b n) -> p d (a b) n", d=2, n=RV))


def hyena(nc, I, K, w_in, hT, hyT):
    with Mem(nc, "hy") as m:
        H = m.sb("H", [P, 4, 4, C])
        with Mem(nc, "hyf") as mf:
            he, ho = mf.sb("he", [P, 8, C]), mf.sb("ho", [P, 8, C])
            phase_filters(nc, I, K, he, ho, K.X)
            phase_forward(nc, "fwdfilt", I, he, ho, H)
        xc = m.sb("xc", [P, 12, SEQ])
        prod = K.X[:, :, :].rearrange("p (a b) (c n) -> p a (b c) n", b=2, n=C)
        phase_hyena_in(nc, I, K, w_in[:, :, 3072:4608], hT, xc, PLACES["b_in"][0] + 24)
        zn = xc[:, 8:12, :].rearrange("p a (b c) -> p (a b) c", c=C)
        phase_hyena_turn(nc, K, xc, zn)
        phase_forward(nc, "fwdz", I, zn, zn, H, prod, hyT[:, :, 0:C])
        phase_inverse(nc, I, K, prod, xc, hyT)


def moe(nc, tag, I, K, S, hidden, scale, shift, names, gate):
    rgw, rgb, rew, reb, w1, w3, w2 = names
    with Mem(nc, f"moe{tag}") as m:
        T = Named()
        T.dest = m.sb("dest", [P, 2, 8], U32)
        T.wt = m.sb("wt", [P, 2, 8])
        T.be = m.sb("be", [1, MAXB], I32)
        T.nb = m.sb("nb", [1, 1], I32)
        with Mem(nc, f"u{tag}") as mu:
            uT = mu.sb("uT", [P, KT, SEQ])
            phase_norm(nc, f"moenorm{tag}", None, 8, uT, 0, scale, shift, K, src_sb=K.X, y_dram=S.normed)
            phase_router(nc, f"router{tag}", I, K, uT, I[rgw], I[rgb], I[rew], I[reb], T, S.slot)
        phase_experts(nc, f"experts{tag}", K, hidden, experts_to_tiles(I[w1]), experts_to_tiles(I[w3]), experts_to_tiles(I[w2]),
                      scale, shift, T, S.slot, S.normed, S.rows)
        phase_combine(nc, f"combine{tag}", K.X, T, S.rows, gate)


def first(nc, I, K, S):
    with Mem(nc, "b1") as m:
        K.mod, K.gt, K.X = m.sb("mod", [P, 3, 2, 8]), m.sb("gt", [P, 2, D]), m.sb("X", [P, KT, D])
        w_in = rows_to_tiles(I["w_in"])
        phase_vectors(nc, I, K)
        with Mem(nc, "mix") as mm:
            hyT = mm.sb("hyT", [P, 4, SEQ]); hT = mm.sb("hT", [P, KT, SEQ])
            phase_norm(nc, "norm1", I["x"][0], 8, hT, 0, lambda k: K.mod[:, 0, 0, k:k + 1], lambda k: K.mod[:, 0, 1, k:k + 1], K)
            hyena(nc, I, K, w_in, hT, hyT)
            Mem.retire(nc)
            phase_move(nc, "keep1", [(S.hT, hT[:, :, :]), (S.hyT, hyT[:, :, :])])
            retention_branch(nc, I, K, w_in, hT, hyT[:, :, :])
            retT, h2T, mixedT = hT, mm.sb("h2T", [P, KT, SEQ]), mm.sb("mixedT", [P, KT, SEQ])
            phase_move(nc, "again1", [(h2T[:, :, :], S.hT), (hyT[:, :, :], S.hyT), (K.X[:, :, :], I["x"][0].rearrange("(t p) d -> p t d", p=P))])
            phase_merge(nc, "merge1", ((rows_to_tiles(I["ret_w_o"]), 8, retT), (rows_to_tiles(I["hy_w_o"]), 4, hyT)), K, mixedT,
                        (w_in[:, :, 4608:], h2T), PLACES["b_in"][0] + 36)
            phase_residual(nc, "resid1", rows_to_tiles(I["w_out"]), mixedT, K.X, K.gt[:, 0, :])
        Mem.retire(nc)
        moe(nc, 1, I, K, S, 512, lambda k: K.mod[:, 2, 0, k:k + 1], lambda k: K.mod[:, 2, 1, k:k + 1],
            ("router_group_w", "router_group_b", "router_expert_w", "router_expert_b", "expert_w1", "expert_w3", "expert_w2"), K.gt[:, 1, :])
        phase_rownorm(nc, "between", K, K.X, I["final_norm_g"], S.x)


def rwkv(nc, I, K, S, w_in, Z):
    with Mem(nc, "rwkv") as m:
        W = Named()
        W.tri = m.sb("tri", [P, 2, 2, P])
        W.level = m.sb("level", [P, 2, 6, P])
        W.headones = m.sb("headones", [P, P])
        W.carry = m.sb("carry", [P, SEQ])
        W.eye64 = m.sb("eye64", [P, 64])
        W.wup = m.sb("wup", [P, RC])
        W.aup = m.sb("aup", [P, RC])
        W.gup = m.sb("gup", [P, RC])
        W.mid = m.sb("mid", [P, 15])
        W.ka1 = m.sb("ka1", [P, 4])
        W.lnx_eps = m.sb("lnx_eps", [P, 1])
        W.zero = m.sb("zero", [P, 1])
        W.tot = m.sb("tot", [P, 2, NC])
        W.junk = m.sb("junk", [P, 1])
        phase_rwkv_consts(nc, I, K, W)
        with Mem(nc, "rwkvh") as mh:
            hT = mh.sb("hT", [P, KT, SEQ])
            phase_move(nc, "again2", [(hT[:, :, :], S.hT)])
            col = lambda base: (lambda t: K.cols[:, bass.ds(t + base, 1)])
            taps = (col(PLACES["mu_prev_2"][0]), lambda t: W.mid[:, bass.ds(t, 1)], col(PLACES["mu_next_2"][0]), lambda t: W.zero[:, 0:1])
            phase_taps(nc, "taps", w_in[:, :, 672:2592], hT, Z, 15, 3, lambda j, t: taps[j](t))
        phase_rwkv_gates(nc, Z)
        pr, elc, bv, Y = m.sb("pr", [P, 2, 4, SEQ]), m.sb("elc", [P, 2, NC]), m.sb("bv", [P, SEQ]), m.sb("Y", [P, 2, NC, CH])
        for p in range(NP):
            phase_rwkv_prep(nc, K, W, Z, p, pr, elc, bv)
            phase_rwkv_chunks(nc, K, W, Z, p, pr, elc, Y)
            phase_rwkv_out(nc, K, W, Z, p, Y, bv)


def second(nc, I, K, S, out):
    with Mem(nc, "b2") as m:
        oT, Z = m.sb("oT", [P, 4, SEQ]), m.sb("Z", [P, 15, SEQ])
        w_in = rows_to_tiles(I["w_in_2"])
        with Mem(nc, "b2h") as mh:
            hT = mh.sb("hT", [P, KT, SEQ])
            phase_norm(nc, "norm2", S.x, 8, hT, 0, lambda k: vec(K.cols, "norm_mix_g_2", k), None, K)
            phase_move(nc, "keep2", [(S.hT, hT[:, :, :])])
            mla(nc, I, K, w_in, hT, oT)
        Mem.retire(nc)
        rwkv(nc, I, K, S, w_in, Z)
        Mem.retire(nc)
        mixedT = Z[:, 4:12, :]
        with Mem(nc, "b2m") as mh:
            hT = mh.sb("hT", [P, KT, SEQ])
            phase_move(nc, "again3", [(hT[:, :, :], S.hT)])
            phase_merge(nc, "merge2", ((rows_to_tiles(I["w_br_mla_2"]), 4, oT), (rows_to_tiles(I["w_br_rwkv_2"]), 4, Z)), K, mixedT,
                        (w_in[:, :, 2592:], hT), PLACES["gate_b_2"][0])
        K.X = m.sb("X", [P, KT, D])
        phase_move(nc, "again4", [(K.X[:, :, :], S.x.rearrange("(t p) d -> p t d", p=P))])
        phase_residual(nc, "resid2", rows_to_tiles(I["w_out_2"]), mixedT, K.X)
        moe(nc, 2, I, K, S, 256, lambda k: vec(K.cols, "norm_ffn_g_2", k), None,
            ("router_group_w_2", "router_group_b_2", "router_expert_w_2", "router_expert_b_2", "w1_2", "w3_2", "w2_2"), None)
        phase_rownorm(nc, "last", K, K.X, I["norm_final_g_2"], out)


def two_blocks(nc, I, out):
    Mem.spent = []
    with Mem(nc, "all") as m:
        K = Named()
        K.ident = m.sb("ident", [P, P])
        K.ones = m.sb("ones", [P, P])
        K.eps = m.sb("eps", [P, 1])
        K.cols = m.sb("cols", [P, VGROUPS * P])
        S = Named()
        S.hT = nc.dram_tensor("keep_hT", [P, KT, SEQ], F32, kind="Internal").ap()
        S.hyT = nc.dram_tensor("keep_hyT", [P, 4, SEQ], F32, kind="Internal").ap()
        S.x = nc.dram_tensor("keep_x", [SEQ, D], F32, kind="Internal").ap()
        S.normed = nc.dram_tensor("keep_normed", [SEQ, D], F32, kind="Internal").ap()
        S.slot = nc.dram_tensor("keep_slot", [MAXB * P], I32, kind="Internal").ap()
        S.rows = nc.dram_tensor("keep_rows", [(MAXB + 2) * P, D], F32, kind="Internal").ap()
        first(nc, I, K, S)
        Mem.retire(nc)
        second(nc, I, K, S, out)


def constants():
    f = np.float32
    c = {}
    c["k_eye"] = np.eye(128, dtype=f)
    i = np.arange(128, dtype=np.float64)
    j = i[:, None]
    pos = np.zeros((128, 6, 128))
    pos[:, 0] = i + 1; pos[:, 1] = 128 - i
    pos[:, 2] = np.maximum(i - j, 0); pos[:, 3] = np.maximum(j - i, 0)
    pos[:, 4] = i >= j; pos[:, 5] = j > i
    c["k_pos"] = pos.astype(f)
    p = i
    c["k_cpos"] = np.stack([127 - p, 255 - p, 127 - p, 0 * p + 128, p, p, p + 128, 0 * p + 128], 1).astype(f)
    n = np.arange(1024)
    inv = 10000.0 ** (-np.arange(32) / 32)
    row, col = (n // 64)[None] * inv[:, None], (n % 64)[None] * inv[:, None]
    ang = np.concatenate([row, row, col, col])
    sgn = np.concatenate([-np.ones(32), np.ones(32)] * 2)[:, None]
    c["k_rope1"] = np.stack([np.cos(ang), np.sin(ang)], 1).astype(f)
    rot = np.zeros((128, 128))
    for d in range(128):
        src = d + 32 if d % 64 < 32 else d - 32
        rot[src, d] = sgn[d, 0]
    c["k_rot1"] = rot.astype(f)
    return c


def hyena_constants():
    f = np.float32
    c = {}
    n = np.concatenate([np.arange(0, 1024, 2), np.arange(1, 1024, 2)])
    t = (np.arange(1024, dtype=f) / f(1024))
    bands = np.linspace(1e-4, 15, 16, dtype=f)
    phase = (f(2.0 * np.pi) * t[:, None] * bands[None, :]).astype(f)
    feats = np.concatenate([t[:, None], np.cos(phase), -np.sin(phase)], -1).astype(f)
    c["k_feats"] = np.ascontiguousarray(feats[n].T)
    c["k_negt"] = np.ascontiguousarray(-t[n].reshape(8, 128).T)
    slow, fast = abs(np.log(1e-2)) / 1.5, abs(np.log(1e-2)) / 0.3
    c["k_delta"] = np.tile(np.linspace(slow, fast, 512, dtype=f)[None], (128, 1))
    th = 2 * np.pi * (np.arange(512) + 0.5) / 2048
    m = np.arange(512)
    tab = [fn(th[:, None] * (2 * m + par)[None]) for par in (0, 1) for fn in (np.cos, np.sin)]
    order = [tab[0], tab[2], tab[1], tab[3]]
    fwd = np.zeros((4, 128, 4, 4, 128), f)
    for a, T in enumerate(order):
        for kt in range(4):
            for mt in range(4):
                fwd[kt, :, a, mt, :] = T[kt * 128:(kt + 1) * 128, mt * 128:(mt + 1) * 128].T
    c["k_fwd"] = fwd.reshape(4, 128, 2048)
    inv = np.zeros((2, 128, 2, 4, 512), f)
    for par in (0, 1):
        for a in (0, 1):
            for kt in range(4):
                inv[par, :, a, kt, :] = tab[2 * par + a][kt * 128:(kt + 1) * 128] / 1024
    c["k_inv"] = inv.reshape(2, 128, 4096)
    return c


def router_constants():
    f = np.float32
    c = {}
    r = np.zeros((128, 3, 48), f)
    r[:, 0, :4] = [4, 3, 2, 1]
    r[:, 1, :8] = np.arange(8, 0, -1)
    r[:, 2, :48] = np.arange(48)
    c["k_iotas"] = r
    c["k_upper"] = np.triu(np.ones((128, 128), f), 1)
    return c


def rwkv_constants():
    f = np.float32
    c = {}
    i = np.arange(128)
    r, q = i[:, None], i[None, :]
    same = (r // 64) == (q // 64)
    m2 = np.zeros((128, 2, 2, 128), f)
    m2[:, 0, 0] = same & (r < q); m2[:, 0, 1] = same & (r <= q)
    m2[:, 1, 0] = same & (r > q); m2[:, 1, 1] = same & (r >= q)
    c["k_tri"] = m2
    lv = np.zeros((128, 2, 6, 128), f)
    for l in range(6):
        b = 1 << l
        blk = (r // (2 * b)) == (q // (2 * b))
        lv[:, 0, l] = blk & (r % (2 * b) < b) & (q % (2 * b) >= b)
        lv[:, 1, l] = blk & (r % (2 * b) >= b) & (q % (2 * b) < b)
    c["k_level"] = lv
    c["k_headones"] = same.astype(f)
    ch = np.ones((128, 1024), f); ch[:, ::64] = 0
    c["k_carry"] = ch
    c["k_eye64"] = np.concatenate([np.eye(64, dtype=f)] * 2)
    return c


def mla_constants():
    f = np.float32
    inv = (f(10000.0) ** (-np.arange(0, 32, 2, dtype=f) / f(32))).astype(f)
    ang = (np.arange(1024, dtype=f)[None] * inv[:, None]).astype(f).astype(np.float64)
    cos, sin = np.cos(ang), np.sin(ang)
    tab = np.ones((128, 1024))
    tab[64:] = np.concatenate([cos, cos, -sin, sin])
    fold = np.zeros((128, 64))
    for p in range(64, 128):
        for q in range(64):
            fold[p, q] = p % 32 == q % 32
    return {"k_rope2": tab.astype(f), "k_fold": fold.astype(f)}


_INPUTS = ("x", "c", "ctx", "c_ctx", "ada_w", "ada_b", "norm1_g", "norm2_g", "w_in", "b_in", "ret_decay_logit",
           "ret_w_o", "hy_conv_w", "hy_conv_b", "hy_ffn_w1", "hy_ffn_b1", "hy_ffn_freq", "hy_ffn_w2", "hy_ffn_b2",
           "hy_ffn_w3", "hy_skip", "hy_w_o", "w_out", "router_group_w", "router_group_b", "router_expert_w",
           "router_expert_b", "expert_w1", "expert_w3", "expert_w2", "final_norm_g", "norm_mix_g_2", "w_in_2",
           "q_norm_g_2", "kv_norm_g_2", "w_uq_2", "w_ukv_2", "w_br_mla_2", "mu_prev_2", "mu_next_2", "w0_2",
           "w_up_2", "a0_2", "a_up_2", "g_up_2", "k_k_2", "k_a_2", "r_k_2", "lnx_g_2", "lnx_b_2", "w_br_rwkv_2",
           "gate_b_2", "w_out_2", "norm_ffn_g_2", "router_group_w_2", "router_group_b_2", "router_expert_w_2",
           "router_expert_b_2", "w1_2", "w3_2", "w2_2", "norm_final_g_2")


def kernel(**inputs):
    import concourse.bacc as bacc
    from concourse.bass_utils import run_bass_kernel_spmd

    nc = bacc.Bacc("TRN2", target_bir_lowering=False, num_devices=1)
    tables = {**constants(), **hyena_constants(), **router_constants(), **rwkv_constants(), **mla_constants()}
    arrays, I = {}, {}
    for name in _INPUTS + tuple(tables):
        a = np.ascontiguousarray(tables[name] if name in tables else inputs[name])
        arrays[f"in_{name}"] = a
        I[name] = nc.dram_tensor(f"in_{name}", a.shape, mybir.dt.from_np(a.dtype), kind="ExternalInput").ap()
    out = nc.dram_tensor("out", (SEQ, D), F32, kind="ExternalOutput").ap()
    two_blocks(nc, I, out)
    result = run_bass_kernel_spmd(nc, [arrays], core_ids=[0])
    return result.results[0]["out"].reshape(1, SEQ, D)
```

```python
import concourse.bass as bass
from concourse import mybir
from contextlib import ExitStack
import numpy as np

F32 = mybir.dt.float32
I32 = mybir.dt.int32
U32 = mybir.dt.uint32
ALU = mybir.AluOpType
ACT = mybir.ActivationFunctionType
AXX = mybir.AxisListType.X
P = 128
D = 1024
KT = D // P
SEQ = 1024
CTX = 256
HALF = 512
EPS = 1e-6


class Named:
    pass


class Mem:
    spent = []

    def __init__(self, nc, phase):
        self.nc, self.phase, self.stack, self.own = nc, phase, ExitStack(), []

    def __enter__(self):
        return self

    def __exit__(self, *exc):
        Mem.spent.extend(self.own)
        return self.stack.__exit__(*exc)

    def sb(self, name, shape, dt=F32):
        return self.stack.enter_context(self.nc.sbuf_tensor(f"{self.phase}_{name}", shape, dt))

    def banks(self, count):
        return [self.stack.enter_context(self.nc.psum_tensor(f"{self.phase}_bank{n}", [P, HALF], F32))
                for n in range(count)]

    def sems(self, *names):
        new = [self.nc.alloc_semaphore(name=f"{self.phase}_{n}") for n in names]
        self.own.extend(new)
        return new

    def block(self):
        return self.stack.enter_context(self.nc.Block())

    @staticmethod
    def retire(nc):
        nc.clear_and_free_semaphores(Mem.spent)
        nc.all_engine_barrier()
        Mem.spent = []


def hold(act, sem, value):
    act.wait_ge(sem, value)
    act.nop(nofuse=True)


VECS = [("norm1_g", 8), ("norm2_g", 8), ("b_in", 52), ("hy_conv_w", 36), ("hy_conv_b", 12), ("hy_skip", 4),
        None,
        ("ada_b", 48), ("c", 8), ("c_ctx", 8), ("q_norm_g_2", 3), ("kv_norm_g_2", 2), ("k_k_2", 4), ("k_a_2", 4),
        ("r_k_2", 4), ("lnx_g_2", 4), ("lnx_b_2", 4), ("gate_b_2", 16), ("norm_mix_g_2", 8), ("norm_ffn_g_2", 8),
        None,
        ("mu_prev_2", 15), ("mu_next_2", 15), ("w0_2", 8), ("a0_2", 8)]


def vec_places():
    places, group, row = {}, 0, 0
    for v in VECS:
        if v is None:
            group, row = group + 1, 0
        else:
            places[v[0]] = (group * P + row, v[1])
            row += v[1]
    return places, group + 1


PLACES, VGROUPS = vec_places()


def vec(cols, name, n=0):
    return cols[:, PLACES[name][0] + n:PLACES[name][0] + n + 1]


def flat(ap):
    names = "abcdefg"[:len(ap.shape)]
    return ap.rearrange(f"{' '.join(names)} -> ({' '.join(names)})") if len(ap.shape) > 1 else ap


def tiles_of(dst, src):
    return tuple((dst[:, k:k + 2, :], src[:, k:k + 2, :]) for k in range(0, KT, 2))


def copy_aside(m, b, pairs):
    asided, = m.sems("asided")

    @b.gpsimd
    def _(gp):
        for n, (dst, src) in enumerate(pairs):
            gp.dma_start(dst, src).then_inc(asided, 16)
            gp.wait_ge(asided, 16 * (n + 1))


class Chain:

    def __init__(self, eng, sem, i=None, per=0):
        self.eng, self.sem, self.i, self.per, self.n = eng, sem, i, per, 0

    def __call__(self, ins):
        self.n += 1
        ins.then_inc(self.sem, 1)
        self.eng.wait_ge(self.sem, self.n if self.i is None else self.i * self.per + self.n)

    def end(self):
        assert self.n == self.per, (self.n, self.per)


def one(ap):
    return ap.rearrange("p a n -> p (a n)")


def rows_to_tiles(ap):
    return ap.rearrange("l (k p) n -> p (l k) n", p=P)


def experts_to_tiles(ap):
    return ap.rearrange("l e (k p) n -> p (l e) k n", p=P)


def phase_vectors(nc, I, K):
    W3 = 3
    with Mem(nc, "vec") as m:
        rows = m.sb("rows", [P, VGROUPS, P])
        w = m.sb("w", [P, W3, KT, HALF])
        cc = m.sb("cc", [P, KT, 2])
        brow = m.sb("brow", [2, 6 * D])
        arow = m.sb("arow", [2, 6 * D])
        ada = m.sb("ada", [P, 48, 2])
        sel = m.sb("sel", [2, P])
        bk = m.banks(8)
        wfull = m.sems(*[f"wfull{s}" for s in range(W3)])
        loaded, wfree, zeroed, turned, cols_ok, silu_ok, ada_mm, rowed, ada_turned, spread, chain = m.sems(
            "loaded", "wfree", "zeroed", "turned", "cols_ok", "silu_ok", "ada_mm", "rowed", "ada_turned", "spread", "chain")
        ada_w = rows_to_tiles(I["ada_w"])
        vectors = [v for v in VECS if v]
        STEPS = 12 // W3
        b = m.block()

        @b.sync
        def _(sp):
            sp.dma_start(K.ident[:, :], I["k_eye"]).then_inc(loaded, 16)
            sp.wait_ge(zeroed, 1)
            for name, n in vectors:
                g, r = divmod(PLACES[name][0], P)
                sp.dma_start(rows[r:r + n, g, :], flat(I[name]).rearrange("(n p) -> n p", p=P)).then_inc(loaded, 16)

        @b.scalar
        def _(act):
            act.dma_start(brow[:, :], I["ada_b"].to_broadcast([2, 6 * D])).then_inc(loaded, 16)
            act.wait_ge(cols_ok, 1)
            for j, name in enumerate(("c", "c_ctx")):
                r = PLACES[name][0]
                act.activation(cc[:, :, j], K.cols[:, r:r + 8], ACT.Silu).then_inc(silu_ok, 1)
            for n in range(4):
                act.wait_ge(spread, n + 1)
                act.activation(K.gt[:, n // 2, n % 2 * HALF:(n % 2 + 1) * HALF], bk[4 + n][:, :], ACT.Copy)

        @b.gpsimd
        def _(gp):
            gp.memset(rows[:, :, :], 0.0).then_inc(zeroed, 1)
            gp.memset(K.ones[:, :], 1.0).then_inc(zeroed, 1)
            gp.memset(K.eps[:, :], EPS).then_inc(zeroed, 1)
            gp.memset(sel[:, :], 0.0).then_inc(zeroed, 1)
            gp.wait_ge(zeroed, 4)
            gp.memset(sel[0:1, :], 1.0).then_inc(zeroed, 1)
            with gp.Fori(0, STEPS) as i:
                for s in range(W3):
                    hold(gp, wfree, i * W3 + (s + 1))
                    gp.dma_start(w[:, s, :, :], ada_w[:, :, bass.ds(i * (W3 * HALF) + s * HALF, HALF)]).then_inc(wfull[s], 16)

        @b.tensor
        def _(pe):
            pe.sem_inc(wfree, W3)
            pe.wait_ge(loaded, 16 * (2 + len(vectors)))
            for g in range(VGROUPS):
                pe.transpose(bk[0][:, g * P:(g + 1) * P], rows[:, g, :], K.ident[:, :]).then_inc(turned, 1)
            pe.wait_ge(silu_ok, 2)
            with pe.Fori(0, STEPS) as i:
                for s in range(W3):
                    pe.wait_ge(wfull[s], i * 16 + 16)
                    pe.wait_ge(rowed, i * W3 + (s + 1))
                    for k in range(KT):
                        last = pe.matmul(bk[1 + s][0:2, :], cc[:, k, :], w[:, s, k, :], start=(k == 0), stop=(k == KT - 1))
                    last.then_inc(ada_mm, 1)
                    pe.wait_ge(ada_mm, i * W3 + (s + 1))
                    pe.sem_inc(wfree, 1)
            pe.wait_ge(rowed, W3 + 12)
            pe.wait_ge(cols_ok, 1)
            for n in range(48):
                last = pe.transpose(bk[0][:, 2 * n:2 * n + 2], arow[:, n * P:(n + 1) * P], K.ident[0:2, 0:2])
            last.then_inc(ada_turned, 1)
            pe.wait_ge(zeroed, 5)
            for n in range(4):
                c0 = (2 if n < 2 else 5) * D + n % 2 * HALF
                pe.matmul(bk[4 + n][:, :], sel[:, :], arow[:, c0:c0 + HALF], start=True, stop=True).then_inc(spread, 1)

        @b.vector
        def _(dve):
            dve.sem_inc(rowed, W3)
            dve.wait_ge(turned, VGROUPS)
            dve.tensor_copy(K.cols[:, :], bk[0][:, 0:VGROUPS * P]).then_inc(cols_ok, 1)
            dve.wait_ge(loaded, 16 * (2 + len(vectors)))
            with dve.Fori(0, STEPS) as i:
                for s in range(W3):
                    cols = bass.ds(i * (W3 * HALF) + s * HALF, HALF)
                    dve.wait_ge(ada_mm, i * W3 + (s + 1))
                    dve.tensor_tensor(arow[:, cols], bk[1 + s][0:2, :], brow[:, cols], ALU.add).then_inc(rowed, 1)
            then = Chain(dve, chain)
            dve.wait_ge(ada_turned, 1)
            dve.wait_ge(cols_ok, 1)
            then(dve.tensor_copy(ada[:, :, :].rearrange("p n j -> p (n j)"), bk[0][:, 0:96]))
            for out, vecname, sc, sh, j in ((0, "norm1_g", 1, 0, 0), (1, "norm1_g", 1, 0, 1), (2, "norm2_g", 4, 3, 0)):
                g = PLACES[vecname][0]
                dve.scalar_tensor_tensor(K.mod[:, out, 0, :], ada[:, sc * 8:sc * 8 + 8, j], 1.0,
                                         K.cols[:, g:g + 8], ALU.add, ALU.mult)
                dve.tensor_copy(K.mod[:, out, 1, :], ada[:, sh * 8:sh * 8 + 8, j])


def phase_norm(nc, name, X, ntiles, outT, scale, shift, K, src=None, y_dram=None):
    SLOTS = 4
    with Mem(nc, name) as m:
        sq = m.sb("sq", [P, 2, D])
        ys = m.sb("y", [P, SLOTS, D])
        ss = m.sb("ss", [P, ntiles, 4])
        bk = m.banks(8)
        summed, rooted, inv, yok, turned, evac0, evac1 = m.sems("summed", "rooted", "inv", "yok", "turned", "evac0", "evac1")
        xin = m.sems(*[f"xin{t}" for t in range(ntiles)])
        ysaved = m.sems(*[f"ysaved{s}" for s in range(SLOTS)])
        b = m.block()
        tok = lambda t: slice(t * P, (t + 1) * P)

        @b.sync
        def _(sp):
            if src is not None:
                for t in range(ntiles):
                    sp.dma_start(X[:, t, :], src[tok(t), :]).then_inc(xin[t], 16)
            if y_dram is not None:
                for t in range(ntiles):
                    sp.wait_ge(yok, t + 1)
                    sp.dma_start(y_dram[tok(t), :], ys[:, t % SLOTS, :]).then_inc(ysaved[t % SLOTS], 16)
                for s in range(SLOTS):
                    sp.wait_ge(ysaved[s], 16 * (ntiles // SLOTS))

        @b.scalar
        def _(act):
            for t in range(ntiles + 2):
                if t < ntiles:
                    if src is not None:
                        act.wait_ge(xin[t], 16)
                    if t >= 2:
                        act.wait_ge(summed, t - 1)
                    act.activation(sq[:, t % 2, :], X[:, t, :], ACT.Square, accum_out=ss[:, t, 0:1]).then_inc(summed, 1)
                    act.wait_ge(summed, t + 1)
                    act.activation(ss[:, t, 1:2], ss[:, t, 0:1], ACT.Sqrt, scale=1.0 / D, bias=K.eps[:, 0:1]).then_inc(rooted, 1)
                if t >= 2:
                    u = t - 2
                    act.wait_ge(turned, 2 * u + 1)
                    for k in range(4):
                        last = act.activation(outT[:, k, tok(u)], bk[2 * (u % 4)][:, k * P:(k + 1) * P], ACT.Identity, scale=scale(k),
                                              bias=shift(k) if shift else 0.0)
                    last.then_inc(evac0, 1)

        @b.vector
        def _(dve):
            for t in range(ntiles + 1):
                if t < ntiles:
                    dve.wait_ge(rooted, t + 1)
                    dve.reciprocal(ss[:, t, 2:3], ss[:, t, 1:2]).then_inc(inv, 1)
                    dve.wait_ge(inv, t + 1)
                    if t >= SLOTS:
                        dve.wait_ge(turned, 2 * (t - SLOTS) + 2)
                        if y_dram is not None:
                            dve.wait_ge(ysaved[t % SLOTS], 16 * (t // SLOTS))
                    dve.tensor_scalar(ys[:, t % SLOTS, :], X[:, t, :], ss[:, t, 2:3], None, ALU.mult).then_inc(yok, 1)
                if t >= 1:
                    u = t - 1
                    dve.wait_ge(turned, 2 * u + 2)
                    for k in range(4, 8):
                        last = dve.tensor_scalar(outT[:, k, tok(u)], bk[2 * (u % 4) + 1][:, (k - 4) * P:(k - 3) * P], scale(k),
                                                 shift(k) if shift else None, ALU.mult, *([ALU.add] if shift else []))
                    last.then_inc(evac1, 1)

        @b.tensor
        def _(pe):
            for t in range(ntiles):
                pe.wait_ge(yok, t + 1)
                for h in range(2):
                    if t >= 4:
                        pe.wait_ge((evac0, evac1)[h], t - 3)
                    for q in range(4):
                        last = pe.transpose(bk[2 * (t % 4) + h][:, q * P:(q + 1) * P],
                                            ys[:, t % SLOTS, (4 * h + q) * P:(4 * h + q + 1) * P], K.ident[:, :])
                    last.then_inc(turned, 1)


def phase_proj_T(nc, name, w, kt, xT, ntiles, unroll, evac, uses_dve=False, ntok=SEQ):
    with Mem(nc, name) as m:
        wt = m.sb("w", [P, unroll, kt, P])
        nh = max(1, ntok // HALF)
        width = ntok // nh
        nb = unroll * nh
        bk = m.banks(nb)
        wfull = m.sems(*[f"wfull{s}" for s in range(unroll)])
        wfree, done, free = m.sems("wfree", "done", "free")
        b = m.block()
        steps = ntiles // unroll
        assert steps * unroll == ntiles

        @b.sync
        def _(sp):
            with sp.Fori(0, steps) as i:
                for s in range(unroll):
                    sp.wait_ge(wfree, i * unroll + (s + 1))
                    sp.dma_start(wt[:, s, :, :], w[:, :, bass.ds(i * (unroll * P) + s * P, P)]).then_inc(wfull[s], 16)

        @b.tensor
        def _(pe):
            pe.sem_inc(wfree, unroll)
            with pe.Fori(0, steps) as i:
                for s in range(unroll):
                    pe.wait_ge(wfull[s], i * 16 + 16)
                    for h in range(nh):
                        pe.wait_ge(free, i * nb + (s * nh + h + 1))
                        for k in range(kt):
                            last = pe.matmul(bk[s * nh + h][:, 0:width], wt[:, s, k, :], xT[:, k, h * width:(h + 1) * width],
                                             start=(k == 0), stop=(k == kt - 1))
                        last.then_inc(done, 1)
                    pe.wait_ge(done, i * nb + (s + 1) * nh)
                    pe.sem_inc(wfree, 1)

        wait = (lambda e, sem, n: e.wait_ge(sem, n)) if uses_dve else hold

        def readout(eng):
            eng.sem_inc(free, nb)
            with eng.Fori(0, steps) as i:
                for s in range(unroll):
                    for h in range(nh):
                        wait(eng, done, i * nb + (s * nh + h + 1))
                        evac(eng, i * unroll + s, h, bk[s * nh + h][:, 0:width]).then_inc(free, 1)

        if uses_dve:
            b.vector(readout)
        else:
            b.scalar(readout)


def phase_proj_N(nc, name, w, kt, xT, tok0, ntok_tiles, ngroups, width, evac, uses_dve=False, unroll=2, aside=()):
    with Mem(nc, name) as m:
        wt = m.sb("w", [P, unroll, kt, width])
        T = ntok_tiles
        nb = min(8, T)
        bk = m.banks(nb)
        wfull = m.sems(*[f"wfull{s}" for s in range(unroll)])
        wfree, done, free = m.sems("wfree", "done", "free")
        b = m.block()
        steps = ngroups // unroll
        assert steps * unroll == ngroups and T == nb

        @b.sync
        def _(sp):
            with sp.Fori(0, steps) as i:
                for s in range(unroll):
                    sp.wait_ge(wfree, i * unroll + (s + 1))
                    sp.dma_start(wt[:, s, :, :], w[:, :, bass.ds(i * (unroll * width) + s * width, width)])\
                      .then_inc(wfull[s], 16)

        @b.tensor
        def _(pe):
            pe.sem_inc(wfree, unroll)
            with pe.Fori(0, steps) as i:
                for s in range(unroll):
                    pe.wait_ge(wfull[s], i * 16 + 16)
                    for t in range(T):
                        pe.wait_ge(free, i * (unroll * T) + (s * T + t + 1))
                        for k in range(kt):
                            last = pe.matmul(bk[t][:, 0:width], xT[:, k, tok0 + t * P:tok0 + (t + 1) * P],
                                             wt[:, s, k, :], start=(k == 0), stop=(k == kt - 1))
                        last.then_inc(done, 1)
                    pe.wait_ge(done, i * (unroll * T) + (s + 1) * T)
                    pe.sem_inc(wfree, 1)

        if aside:
            copy_aside(m, b, aside)

        wait = (lambda e, sem, n: e.wait_ge(sem, n)) if uses_dve else hold

        def readout(eng):
            eng.sem_inc(free, T)
            with eng.Fori(0, steps) as i:
                for s in range(unroll):
                    for t in range(T):
                        wait(eng, done, i * (unroll * T) + (s * T + t + 1))
                        evac(eng, i * unroll + s, t, bk[t][:, 0:width]).then_inc(free, 1)

        if uses_dve:
            b.vector(readout)
        else:
            b.scalar(readout)


RH = 4
RV = 256
KSCALE = 128 ** -0.5


def phase_decay(nc, I, K, R):
    with Mem(nc, "dec") as m:
        z = m.sb("z", [P, 8]); a = m.sb("a", [P, 8]); e = m.sb("e", [P, 8]); l1 = m.sb("l1", [P, 8]); mn = m.sb("mn", [P, 8])
        pos = m.sb("pos", [P, 6, P])
        cpos = m.sb("cpos", [P, 8])
        tmp = m.sb("tmp", [P, 2, P])
        come, chain, ex, lg, tt = m.sems("come", "chain", "ex", "lg", "tt")
        b = m.block()

        @b.sync
        def _(sp):
            sp.dma_start(z[:, :], flat(I["ret_decay_logit"]).rearrange("(a n) -> a n", a=1).to_broadcast([P, 8])).then_inc(come, 16)
            sp.dma_start(pos[:, :, :], I["k_pos"]).then_inc(come, 16)
            sp.dma_start(cpos[:, :], I["k_cpos"]).then_inc(come, 16)

        @b.vector
        def _(dve):
            then = Chain(dve, chain)
            dve.wait_ge(come, 48)
            then(dve.tensor_scalar(mn[:, :], z[:, :], 0.0, None, ALU.min))
            then(dve.scalar_tensor_tensor(a[:, :], z[:, :], -1.0, z[:, :], ALU.mult, ALU.min))
            dve.wait_ge(ex, 2)
            dve.tensor_tensor(R.lg[:, :], mn[:, :], l1[:, :], ALU.subtract).then_inc(lg, 1)
            for h in range(RH):
                for d in range(2):
                    dve.wait_ge(tt, 2 * h + d + 1)
                    then(dve.tensor_tensor(tmp[:, d, :], tmp[:, d, :], pos[:, 4 + d, :], ALU.mult))
                then(dve.tensor_tensor(R.DT[:, h, :], tmp[:, 0, :], tmp[:, 1, :], ALU.add))

        @b.scalar
        def _(act):
            act.wait_ge(chain, 2)
            act.activation(e[:, :], a[:, :], ACT.Exp).then_inc(ex, 1)
            act.wait_ge(ex, 1)
            act.activation(l1[:, :], e[:, :], ACT.Ln, bias=1.0).then_inc(ex, 1)
            act.wait_ge(lg, 1)
            for d in range(2):
                for h in range(RH):
                    c = R.lg[:, d * RH + h:d * RH + h + 1]
                    act.activation(R.DQ[:, h, d, :], pos[:, d, :], ACT.Exp, scale=c)
                    act.activation(R.DC[:, d, h, :], cpos[:, d * 4:d * 4 + 4], ACT.Exp, scale=c)
            for h in range(RH):
                for d in range(2):
                    if h:
                        act.wait_ge(chain, 2 + 3 * h)
                    c = R.lg[:, d * RH + h:d * RH + h + 1]
                    act.activation(tmp[:, d, :], pos[:, 2 + d, :], ACT.Exp, scale=c).then_inc(tt, 1)


def phase_ctx(nc, I, K, R, hcT, w_in):
    with Mem(nc, "ctx") as m:
        kv = m.sb("kv", [P, 2, 1536])
        w = m.sb("w", [P, 3, KT, HALF])
        kd = m.sb("kd", [P, 2, 2, HALF])
        bias = m.sb("bias", [P, 1536])
        bk = m.banks(8)
        w0, w1, w2, done, ev, kds, st = m.sems("w0", "w1", "w2", "done", "ev", "kds", "st")
        wf = [w0, w1, w2]
        b = m.block()

        @b.sync
        def _(sp):
            sp.dma_start(w[:, 0, :, :], w_in[:, :, 512:1024]).then_inc(w0, 16)
            sp.dma_start(w[:, 1, :, :], w_in[:, :, 1024:1536]).then_inc(w1, 16)
            sp.dma_start(bias[:, :], I["b_in"][:, 512:2048].to_broadcast([P, 1536])).then_inc(w2, 16)
            sp.dma_start(w[:, 2, :, :], w_in[:, :, 1536:2048]).then_inc(w2, 16)

        @b.tensor
        def _(pe):
            for g in range(3):
                pe.wait_ge(wf[g], 16 if g < 2 else 32)
                for t in range(2):
                    for k in range(KT):
                        last = pe.matmul(bk[g * 2 + t][:, :], hcT[:, k, t * P:(t + 1) * P], w[:, g, k, :],
                                         start=(k == 0), stop=(k == KT - 1))
                    last.then_inc(done, 1)
            pe.wait_ge(ev, 6)
            pe.wait_ge(kds, 16)
            for d in range(2):
                for h in range(RH):
                    o = bk[d * 2 + h // 2][:, h % 2 * RV:(h % 2 + 1) * RV]
                    for t in range(2):
                        last = pe.matmul(o, kd[:, d, t, h * P:(h + 1) * P], kv[:, t, 512 + h * RV:512 + (h + 1) * RV],
                                         start=(t == 0), stop=(t == 1))
                    last.then_inc(done, 1)

        @b.vector
        def _(dve):
            dve.wait_ge(w2, 32)
            for g in range(3):
                for t in range(2):
                    dve.wait_ge(done, g * 2 + t + 1)
                    dve.tensor_tensor(kv[:, t, g * HALF:(g + 1) * HALF], bk[g * 2 + t][:, :], bias[:, g * HALF:(g + 1) * HALF],
                                      ALU.add).then_inc(ev, 1)
            dve.wait_ge(ev, 6)
            for d in range(2):
                for t in range(2):
                    for h in range(RH):
                        dve.tensor_scalar(kd[:, d, t, h * P:(h + 1) * P], kv[:, t, h * P:(h + 1) * P],
                                          R.DC[:, d, h, 1 + t:2 + t], KSCALE, ALU.mult, ALU.mult).then_inc(kds, 1)
            for d in range(2):
                for h in range(RH):
                    dve.wait_ge(done, 6 + d * 4 + h // 2 * 2 + 2)
                    dve.tensor_copy(R.S0[:, d, h, :], bk[d * 2 + h // 2][:, h % 2 * RV:(h % 2 + 1) * RV])


def phase_retention(nc, I, K, R, qk, v, g, retT, st):
    NCH = SEQ // P
    with Mem(nc, "ret") as m:
        cs = m.sb("cs", [P, 2, SEQ])
        rot = m.sb("rot", [P, P])
        qr = m.sb("qr", [P, 2, SEQ])
        qd = m.sb("qd", [P, 2, SEQ])
        kn = m.sb("kn", [P, 2, NCH, P])
        t1, t2 = (kn[:, j, :, :].rearrange("p c n -> p (c n)") for j in range(2))
        on = qr[:, :, :].rearrange("p j (c n) -> p (j c) n", n=RV)
        sc = m.sb("sc", [P, NCH, P])
        sq = m.sb("sq", [P, 2, RV])
        ss = m.sb("ss", [P, 3, NCH])
        bk = m.banks(8)
        (come, swapped, roped, qdone, kturn, kscaled, scored, masked, upd, stated, outd, ssum, rstd, normed, turned,
         stored, chain, inv) = m.sems(
            "come", "swapped", "roped", "qdone", "kturn", "kscaled", "scored", "masked", "upd", "stated", "outd", "ssum",
            "rstd", "normed", "turned", "stored", "chain", "inv")
        b = m.block()

        @b.sync
        def _(sp):
            sp.dma_start(cs[:, :, :], I["k_rope1"]).then_inc(come, 16)
            sp.dma_start(rot[:, :], I["k_rot1"]).then_inc(come, 16)

        def head(ap, h, off=0):
            return ap[:, bass.ds(h + off, 1), :].rearrange("p a n -> p (a n)")

        @b.tensor
        def _(pe):
            pe.wait_ge(come, 32)
            pe.sem_inc(turned, 1)
            with pe.Fori(0, RH) as h:
                pe.wait_ge(normed, h * NCH + 1)
                for j in range(2):
                    for x in range(2):
                        pe.matmul(bk[2 * j + x][:, :], rot[:, :], qk[:, bass.ds(h + 4 * j, 1), x * HALF:(x + 1) * HALF].rearrange("p a n -> p (a n)"),
                                  start=True, stop=True).then_inc(swapped, 1)
                pe.wait_ge(roped, h * 2 + 2)
                pe.wait_ge(stored, h * 8 + 1)
                for c in range(NCH):
                    cc = slice(c * P, (c + 1) * P)
                    pe.transpose(bk[6 + c // 4][:, c % 4 * P:(c % 4 + 1) * P], qr[:, 1, cc], K.ident[:, :]).then_inc(kturn, 1)
                for c in range(NCH):
                    cc = slice(c * P, (c + 1) * P)
                    pe.matmul(bk[4 + c // 4][:, c % 4 * P:(c % 4 + 1) * P], qr[:, 1, cc], qr[:, 0, cc],
                              start=True, stop=True).then_inc(scored, 1)
                vch = lambda c: v[:, c, bass.ds(h * RV, RV)]
                pe.wait_ge(kscaled, h * 16 + 16)
                pe.wait_ge(masked, h * 2 + 2)
                for d in range(2):
                    for n in range(NCH - 1):
                        c = n if d == 0 else NCH - 1 - n
                        pe.matmul(bk[4 * d + n // 2][:, n % 2 * RV:(n % 2 + 1) * RV], kn[:, d, c, :], vch(c),
                                  start=True, stop=True).then_inc(upd, 1)
                pe.wait_ge(qdone, h * 2 + 2)
                pe.wait_ge(stated, h * 16 + 16)
                for c in range(NCH):
                    cc = slice(c * P, (c + 1) * P)
                    o = bk[c // 2][:, c % 2 * RV:(c % 2 + 1) * RV]
                    pe.matmul(o, sc[:, c, :], vch(c), start=True, stop=False)
                    pe.matmul(o, qd[:, 0, cc], st[:, 0, c, :], start=False, stop=False)
                    pe.matmul(o, qd[:, 1, cc], st[:, 1, c, :], start=False, stop=True).then_inc(outd, 1)
                for c in range(NCH):
                    pe.wait_ge(normed, h * NCH + (c + 2))
                    for x in range(2):
                        pe.transpose(bk[4 + c // 4 + 2 * x][:, c % 4 * P:(c % 4 + 1) * P], on[:, c, x * P:(x + 1) * P],
                                     K.ident[:, :]).then_inc(turned, 1)

        @b.vector
        def _(dve):
            dve.wait_ge(come, 32)
            dve.sem_inc(normed, 1)
            with dve.Fori(0, RH) as h:
                then = Chain(dve, chain, h, 4)
                dve.wait_ge(turned, h * 16 + 1)
                for j in range(2):
                    then(dve.scalar_tensor_tensor(t1, head(qk, h, 4 * j), KSCALE if j else 1.0, cs[:, 0, :],
                                             ALU.mult, ALU.mult))
                    dve.wait_ge(swapped, h * 4 + 2 * j + 2)
                    for x in range(2):
                        xx = slice(x * HALF, (x + 1) * HALF)
                        last = dve.scalar_tensor_tensor(t2[:, xx], bk[2 * j + x][:, :], KSCALE if j else 1.0, cs[:, 1, xx],
                                                        ALU.mult, ALU.mult)
                    then(last)
                    dve.tensor_tensor(qr[:, j, :], t1, t2, ALU.add).then_inc(roped, 1)
                    dve.wait_ge(roped, h * 2 + j + 1)
                then.end()
                for d in range(2):
                    dq = R.DQ[:, bass.ds(h, 1), d, :].to_broadcast([P, NCH, P])
                    dve.tensor_tensor(qd[:, d, :].rearrange("p (c n) -> p c n", n=P),
                                      qr[:, 0, :].rearrange("p (c n) -> p c n", n=P), dq, ALU.mult).then_inc(qdone, 1)
                for x in range(2):
                    dve.wait_ge(scored, h * 8 + 4 * x + 4)
                    dve.tensor_tensor(sc[:, 4 * x:4 * x + 4, :], bk[4 + x][:, :].rearrange("p (c n) -> p c n", n=P),
                                      R.DT[:, bass.ds(h, 1), :].to_broadcast([P, 4, P]), ALU.mult).then_inc(masked, 1)
                for d in range(2):
                    first = 0 if d == 0 else NCH - 1
                    dve.tensor_copy(st[:, d, first, :], head(R.S0[:, d, :, :], h)).then_inc(stated, 1)
                    for n in range(NCH - 1):
                        c, nx = (n, n + 1) if d == 0 else (NCH - 1 - n, NCH - 2 - n)
                        dve.wait_ge(stated, h * 16 + d * 8 + n + 1)
                        dve.wait_ge(upd, h * 14 + (d * 7 + min(n // 2 * 2 + 2, NCH - 1)))
                        dve.scalar_tensor_tensor(st[:, d, nx, :], st[:, d, c, :], R.DC[:, d, bass.ds(h, 1), 3:4].rearrange("p a b -> p (a b)"),
                                                 bk[4 * d + n // 2][:, n % 2 * RV:(n % 2 + 1) * RV], ALU.mult, ALU.add).then_inc(stated, 1)
                dve.wait_ge(rstd, h + 1)
                dve.reciprocal(ss[:, 2, :], ss[:, 1, :]).then_inc(inv, 1)
                dve.wait_ge(inv, h + 1)
                dve.wait_ge(turned, h * 16 + 1)
                for c in range(NCH):
                    dve.scalar_tensor_tensor(on[:, c, :], bk[c // 2][:, c % 2 * RV:(c % 2 + 1) * RV], ss[:, 2, c:c + 1],
                                             g[:, c, bass.ds(h * RV, RV)], ALU.mult, ALU.mult).then_inc(normed, 1)

        @b.scalar
        def _(act):
            act.sem_inc(stored, 1)
            with act.Fori(0, RH) as h:
                for c in range(NCH):
                    hold(act, kturn, h * 8 + (c // 4 * 4 + 4))
                    for d in range(2):
                        act.activation(kn[:, d, c, :], bk[6 + c // 4][:, c % 4 * P:(c % 4 + 1) * P], ACT.Copy,
                                       scale=R.DC[:, d, bass.ds(h, 1), 0:1].rearrange("p a b -> p (a b)")).then_inc(kscaled, 1)
                for c in range(NCH):
                    act.wait_ge(outd, h * 8 + (c // 2 * 2 + 2))
                    if c >= 2:
                        act.wait_ge(ssum, h * 8 + (c - 1))
                    act.activation(sq[:, c % 2, :], bk[c // 2][:, c % 2 * RV:(c % 2 + 1) * RV], ACT.Square,
                                   accum_out=ss[:, 0, c:c + 1]).then_inc(ssum, 1)
                act.wait_ge(ssum, h * 8 + 8)
                act.activation(ss[:, 1, :], ss[:, 0, :], ACT.Sqrt, scale=1.0 / RV, bias=K.eps[:, 0:1]).then_inc(rstd, 1)
                for x in range(2):
                    for y in range(2):
                        hold(act, turned, h * 16 + (8 * y + 9))
                        act.activation(retT[:, bass.ds(h * 2 + x, 1), y * HALF:(y + 1) * HALF].rearrange("p a n -> p (a n)"),
                                       bk[4 + y + 2 * x][:, :], ACT.Copy).then_inc(stored, 2)


C = 512
MAGIC = 12582912.0
TWO_PI_HI, TWO_PI_LO = 6.28125, 0.0019353071795864769
PI_BELOW = 3.1415925


def phase_filters(nc, I, K, he, ho, fl):
    NT = SEQ // P
    with Mem(nc, "filt") as m:
        feats = m.sb("feats", [33, SEQ])
        w1 = m.sb("w1", [33, 64])
        w2 = m.sb("w2", [64, 64])
        w3 = m.sb("w3", [64, 2 * C])
        vecs = m.sb("vecs", [64, 3])
        negt = m.sb("negt", [P, NT])
        delta = m.sb("delta", [P, C])
        arg = m.sb("arg", [64, SEQ])
        turns = m.sb("turns", [64, SEQ])
        hid = m.sb("hid", [64, SEQ])
        dec = m.sb("dec", [P, 2, C])

        ab = m.sb("ab", [P, 2, 2 * C])
        rn = m.sb("rn", [P, 2 * C])
        bk = m.banks(8)
        (come, lin, chain, sine, mm, decs, fls, abss, sums) = m.sems(
            "come", "lin", "chain", "sine", "mm", "decs", "fls", "abss", "sums")
        b = m.block()

        @b.sync
        def _(sp):
            loads = [(feats[:, :], I["k_feats"]), (w1[:, :], I["hy_ffn_w1"][0]), (w2[:, :], I["hy_ffn_w2"][0]),
                     (w3[:, :], I["hy_ffn_w3"][0]), (negt[:, :], I["k_negt"]), (delta[:, :], I["k_delta"])]
            loads += [(vecs[:, j:j + 1], I[n].rearrange("a p -> p a")) for j, n in
                      enumerate(("hy_ffn_b1", "hy_ffn_freq", "hy_ffn_b2"))]
            for dst, src in loads:
                sp.dma_start(dst, src).then_inc(come, 16)

        def norm_sum(pe, t):
            pe.wait_ge(abss, t + 1)
            for x in range(2):
                last = pe.matmul(bk[6 + x][:, :], K.ones[:, :], ab[:, t % 2, x * C:(x + 1) * C], start=(t == 0), stop=(t == NT - 1))
            last.then_inc(sums, 1)

        @b.tensor
        def _(pe):
            pe.wait_ge(come, 16 * 9)
            for x in range(2):
                pe.matmul(bk[x][0:64, :], w1[:, :], feats[:, x * HALF:(x + 1) * HALF], start=True, stop=True).then_inc(lin, 1)
            pe.wait_ge(sine, 1)
            for x in range(2):
                pe.matmul(bk[x][0:64, :], w2[:, :], hid[:, x * HALF:(x + 1) * HALF], start=True, stop=True).then_inc(lin, 1)
            pe.wait_ge(sine, 2)
            for t in range(NT):
                if t >= 2:
                    pe.wait_ge(fls, t - 1)
                for x in range(2):
                    last = pe.matmul(bk[2 + t % 2 * 2 + x][:, :], hid[:, t * P:(t + 1) * P], w3[:, x * C:(x + 1) * C],
                                     start=True, stop=True)
                last.then_inc(mm, 1)
                if t >= 1:
                    norm_sum(pe, t - 1)
            norm_sum(pe, NT - 1)

        @b.scalar
        def _(act):
            for n in range(2):
                act.wait_ge(chain, 6 * (n + 1))
                act.activation(hid[:, :], arg[:, :], ACT.Sin).then_inc(sine, 1)
            for t in range(NT):
                if t >= 2:
                    act.wait_ge(fls, t - 1)
                act.activation(dec[:, t % 2, :], delta[:, :], ACT.Exp, scale=negt[:, t:t + 1]).then_inc(decs, 1)
                act.wait_ge(fls, t + 1)
                if t >= 2:
                    act.wait_ge(sums, t - 1)
                act.activation(ab[:, t % 2, :], fl[:, t, :], ACT.Abs).then_inc(abss, 1)

        @b.vector
        def _(dve):
            then = Chain(dve, chain)
            dve.wait_ge(come, 16 * 9)
            for n in range(2):
                dve.wait_ge(lin, 2 * n + 2)
                if n:
                    dve.wait_ge(sine, 1)
                for x in range(2):
                    last = dve.tensor_scalar(arg[:, x * HALF:(x + 1) * HALF], bk[x][0:64, :], vecs[:, 2 * n:2 * n + 1],
                                             vecs[:, 1:2], ALU.add, ALU.mult)
                then(last)
                then(dve.tensor_scalar(turns[:, :], arg[:, :], float(1 / (2 * np.pi)), MAGIC, ALU.mult, ALU.add))
                then(dve.tensor_scalar(turns[:, :], turns[:, :], MAGIC, None, ALU.subtract))
                then(dve.scalar_tensor_tensor(arg[:, :], turns[:, :], -TWO_PI_HI, arg[:, :], ALU.mult, ALU.add))
                then(dve.scalar_tensor_tensor(arg[:, :], turns[:, :], -TWO_PI_LO, arg[:, :], ALU.mult, ALU.add))
                then(dve.tensor_scalar(arg[:, :], arg[:, :], PI_BELOW, -PI_BELOW, ALU.min, ALU.max))
            for t in range(NT):
                dve.wait_ge(mm, t + 1)
                dve.wait_ge(decs, t + 1)
                for x in range(2):
                    last = dve.tensor_tensor(fl[:, t, x * C:(x + 1) * C], bk[2 + t % 2 * 2 + x][:, :], dec[:, t % 2, :], ALU.mult)
                last.then_inc(fls, 1)
            dve.wait_ge(sums, NT)
            for x in range(2):
                last = dve.reciprocal(rn[:, x * C:(x + 1) * C], bk[6 + x][:, :])
            then(last)
            for t in range(NT):
                last = dve.tensor_tensor(fl[:, t, :], fl[:, t, :], rn[:, :], ALU.mult)
            then(last)
            for t in range(NT):
                dve.tensor_tensor(he[:, t, :], fl[:, t, 0:C], fl[:, t, C:2 * C], ALU.add)
                dve.tensor_tensor(ho[:, t, :], fl[:, t, 0:C], fl[:, t, C:2 * C], ALU.subtract)


def phase_forward(nc, name, I, cos_in, sin_in, H, prod=None, y=None):
    with Mem(nc, name) as m:
        tab = m.sb("tab", [P, 2, 16, P])
        odd = m.sb("odd", [P, 2, C])
        z = m.sb("z", [P, 4, C]) if prod is not None else None
        t = m.sb("t", [P, 4, C]) if prod is not None else None
        bk = m.banks(8)
        full = m.sems("full0", "full1")
        mm, free, copied, outs, chain = m.sems("mm", "free", "copied", "outs", "chain")
        b = m.block()

        @b.sync
        def _(sp):
            for kt in range(4):
                if kt >= 2:
                    sp.wait_ge(mm, 4 * (kt - 1))
                sp.dma_start(tab[:, kt % 2, :, :], I["k_fwd"][kt].rearrange("p (a n) -> p a n", n=P)).then_inc(full[kt % 2], 16)

        @b.tensor
        def _(pe):
            for kt in range(4):
                pe.wait_ge(full[kt % 2], 16 * (kt // 2 + 1))
                if kt >= 2:
                    pe.wait_ge(outs, kt - 1)
                for a in range(4):
                    src = cos_in if a < 2 else sin_in
                    for mt in range(4):
                        last = pe.matmul(bk[kt % 2 * 4 + a][:, :], tab[:, kt % 2, a * 4 + mt, :], src[:, (a % 2) * 4 + mt, :],
                                         start=(mt == 0), stop=(mt == 3))
                    last.then_inc(mm, 1)

        @b.scalar
        def _(act):
            for kt in range(4):
                for j in range(2):
                    act.wait_ge(mm, 4 * kt + (2 if j == 0 else 4))
                    if kt:
                        act.wait_ge(outs, kt)
                    act.activation(odd[:, j, :], bk[kt % 2 * 4 + 1 + 2 * j][:, :], ACT.Copy).then_inc(copied, 1)

        @b.vector
        def _(dve):
            then = Chain(dve, chain)
            for kt in range(4):
                dst = [H[:, kt, n, :] for n in range(4)] if prod is None else [z[:, n, :] for n in range(4)]
                dve.wait_ge(copied, 2 * kt + 2)
                e = [bk[kt % 2 * 4], bk[kt % 2 * 4 + 2]]
                dve.tensor_tensor(dst[0], e[0][:, :], odd[:, 0, :], ALU.add)
                dve.tensor_tensor(dst[1], e[0][:, :], odd[:, 0, :], ALU.subtract)
                dve.tensor_tensor(dst[2], odd[:, 1, :], e[1][:, :], ALU.add)
                dve.tensor_tensor(dst[3], odd[:, 1, :], e[1][:, :], ALU.subtract).then_inc(outs, 1)
                if prod is None:
                    continue
                dve.wait_ge(outs, kt + 1)
                h = [H[:, kt, n, :] for n in range(4)]
                for j in range(2):
                    dve.tensor_tensor(t[:, 0, :], z[:, j, :], h[j], ALU.mult)
                    dve.tensor_tensor(t[:, 1, :], z[:, 2 + j, :], h[2 + j], ALU.mult)
                    dve.tensor_tensor(t[:, 2, :], z[:, j, :], h[2 + j], ALU.mult)
                    then(dve.tensor_tensor(t[:, 3, :], z[:, 2 + j, :], h[j], ALU.mult))
                    dve.tensor_tensor(y[:, j, :], t[:, 0, :], t[:, 1, :], ALU.subtract)
                    then(dve.tensor_tensor(y[:, 2 + j, :], t[:, 2, :], t[:, 3, :], ALU.add))
                dve.tensor_tensor(prod[:, kt, 0, :], y[:, 0, :], y[:, 1, :], ALU.add)
                dve.tensor_tensor(prod[:, kt, 1, :], y[:, 2, :], y[:, 3, :], ALU.subtract)
                dve.tensor_tensor(prod[:, kt, 2, :], y[:, 0, :], y[:, 1, :], ALU.subtract)
                then(dve.tensor_tensor(prod[:, kt, 3, :], y[:, 2, :], y[:, 3, :], ALU.add))


def phase_hyena_turn(nc, K, xc, zn):
    with Mem(nc, "hturn") as m:
        bk = m.banks(8)
        z, tr, = m.sems("z", "tr")
        b = m.block()

        @b.vector
        def _(dve):
            for c in range(4):
                dve.tensor_tensor(xc[:, 4 + c, :], xc[:, 4 + c, :], xc[:, 8 + c, :], ALU.mult).then_inc(z, 1)
            for n in range(8):
                dve.wait_ge(tr, 4 * n + 4)
                dve.tensor_copy(zn[:, n, :], bk[n][:, :])

        @b.tensor
        def _(pe):
            pe.wait_ge(z, 4)
            for par in range(2):
                for mt in range(4):
                    for c in range(4):
                        src = xc[:, 4 + c, :].rearrange("p (n two) -> p two n", two=2)[:, par, mt * P:(mt + 1) * P]
                        pe.transpose(bk[par * 4 + mt][:, c * P:(c + 1) * P], src, K.ident[:, :]).then_inc(tr, 1)


def phase_inverse(nc, I, K, prod, xc, hyT):
    with Mem(nc, "inv") as m:
        tab = m.sb("tab", [P, 2, 8, C])
        t = m.sb("t", [P, 2, C])
        bk = m.banks(8)
        full = m.sems("full0", "full1")
        mm, tdone = m.sems("mm", "tdone")
        b = m.block()

        @b.sync
        def _(sp):
            for par in range(2):
                sp.dma_start(tab[:, par, :, :], I["k_inv"][par].rearrange("p (a n) -> p a n", n=C)).then_inc(full[par], 16)

        @b.tensor
        def _(pe):
            for par in range(2):
                pe.wait_ge(full[par], 16)
                for c in range(4):
                    for n in range(8):
                        a, kt = divmod(n, 4)
                        last = pe.matmul(bk[par * 4 + c][:, :], prod[:, kt, 2 * par + a, c * P:(c + 1) * P],
                                         tab[:, par, n, :], start=(n == 0), stop=(n == 7))
                    last.then_inc(mm, 1)

        @b.vector
        def _(dve):
            split = lambda ap, par: ap.rearrange("p (n two) -> p two n", two=2)[:, par, :]
            for par in range(2):
                for c in range(4):
                    n = par * 4 + c
                    dve.wait_ge(mm, n + 1)
                    dve.scalar_tensor_tensor(t[:, n % 2, :], split(xc[:, 4 + c, :], par), vec(K.cols, "hy_skip", c),
                                             bk[n][:, :], ALU.mult, ALU.add).then_inc(tdone, 1)
                    dve.wait_ge(tdone, n + 1)
                    dve.tensor_tensor(split(hyT[:, c, :], par), t[:, n % 2, :], split(xc[:, c, :], par), ALU.mult)


BIG = 1e30
NG, EG, NE = 4, 8, 32
MAXB = 48


def phase_merge(nc, name, parts, K, mixedT, gate_w, gate_col, aside=()):
    (wa, ka, aT), (wb, kb, bT) = parts
    wg, hT = gate_w
    nk = 2 * KT + ka + kb
    with Mem(nc, name) as m:
        w = m.sb("w", [P, 2, nk, P])
        sg = m.sb("sg", [P, 2, 2, HALF])
        pr = m.sb("pr", [P, 2, 2, HALF])
        bk = m.banks(8)
        full = m.sems("full0", "full1")
        wfree, mm, sig, prod, summed = m.sems("wfree", "mm", "sig", "prod", "summed")
        b = m.block()
        if aside:
            copy_aside(m, b, aside)
        srcs = [(0, KT, wg, 0), (KT, KT, wg, D), (2 * KT, ka, wa, 0), (2 * KT + ka, kb, wb, 0)]

        @b.sync
        def _(sp):
            with sp.Fori(0, 4) as i:
                for s in range(2):
                    sp.wait_ge(wfree, i * 2 + (s + 1))
                    for k0, n, src, off in srcs:
                        sp.dma_start(w[:, s, k0:k0 + n, :], src[:, :, bass.ds(i * 256 + (s * P + off), P)]).then_inc(full[s], 16)

        @b.tensor
        def _(pe):
            pe.sem_inc(wfree, 2)
            with pe.Fori(0, 4) as i:
                for s in range(2):
                    pe.wait_ge(full[s], i * 64 + 64)
                    for h in range(2):
                        hh = slice(h * HALF, (h + 1) * HALF)
                        pe.wait_ge(sig, i * 8 + (4 * s + 2 * h + 2))
                        pe.wait_ge(prod, i * 8 + (4 * s + 2 * h + 2))
                        for j, (k0, n, x) in enumerate(((0, KT, hT), (KT, KT, hT), (2 * KT, ka, aT), (2 * KT + ka, kb, bT))):
                            for k in range(n):
                                last = pe.matmul(bk[4 * h + j][:, :], w[:, s, k0 + k, :], x[:, k, hh], start=(k == 0), stop=(k == n - 1))
                            last.then_inc(mm, 1)
                    pe.wait_ge(mm, i * 16 + (8 * s + 8))
                    pe.sem_inc(wfree, 1)

        @b.scalar
        def _(act):
            act.sem_inc(sig, 4)
            with act.Fori(0, 4) as i:
                for s in range(2):
                    for h in range(2):
                        act.wait_ge(summed, i * 4 + (2 * s + h + 1))
                        for j in range(2):
                            hold(act, mm, i * 16 + (8 * s + 4 * h + j + 1))
                            act.activation(sg[:, h, j, :], bk[4 * h + j][:, :], ACT.Sigmoid,
                                           bias=K.cols[:, bass.ds(i * 2 + (s + gate_col + 8 * j), 1)]).then_inc(sig, 1)

        @b.vector
        def _(dve):
            dve.sem_inc(prod, 4)
            dve.sem_inc(summed, 2)
            with dve.Fori(0, 4) as i:
                for s in range(2):
                    for h in range(2):
                        for j in range(2):
                            dve.wait_ge(mm, i * 16 + (8 * s + 4 * h + 2 + j + 1))
                            dve.wait_ge(sig, i * 8 + (4 * s + 2 * h + j + 5))
                            dve.tensor_tensor(pr[:, h, j, :], bk[4 * h + 2 + j][:, :], sg[:, h, j, :], ALU.mult).then_inc(prod, 1)
                        dve.wait_ge(prod, i * 8 + (4 * s + 2 * h + 6))
                        dve.tensor_tensor(mixedT[:, bass.ds(i * 2 + s, 1), h * HALF:(h + 1) * HALF].rearrange("p a n -> p (a n)"),
                                          pr[:, h, 0, :], pr[:, h, 1, :], ALU.add).then_inc(summed, 1)


def phase_residual(nc, name, w, xT, X, gate=None):
    with Mem(nc, name) as m:
        wt = m.sb("w", [P, 2, KT, HALF])
        t = m.sb("t", [P, 2, HALF])
        bk = m.banks(8)
        full = m.sems("full0", "full1")
        mm, gated, added = m.sems("mm", "gated", "added")
        b = m.block()

        @b.sync
        def _(sp):
            for g in range(2):
                sp.dma_start(wt[:, g, :, :], w[:, :, g * HALF:(g + 1) * HALF]).then_inc(full[g], 16)

        @b.tensor
        def _(pe):
            for g in range(2):
                pe.wait_ge(full[g], 16)
                for n in range(8):
                    if g:
                        pe.wait_ge(added, n + 1)
                    for k in range(KT):
                        last = pe.matmul(bk[n][:, :], xT[:, k, n * P:(n + 1) * P], wt[:, g, k, :], start=(k == 0), stop=(k == KT - 1))
                    last.then_inc(mm, 1)

        @b.vector
        def _(dve):
            for g in range(2):
                gg = slice(g * HALF, (g + 1) * HALF)
                for n in range(8):
                    dve.wait_ge(mm, 8 * g + n + 1)
                    if gate is None:
                        dve.tensor_tensor(X[:, n, gg], X[:, n, gg], bk[n][:, :], ALU.add).then_inc(added, 1)
                        continue
                    c = 8 * g + n
                    if c >= 2:
                        dve.wait_ge(added, c - 1)
                    dve.tensor_tensor(t[:, c % 2, :], bk[n][:, :], gate[:, gg], ALU.mult).then_inc(gated, 1)
                    dve.wait_ge(gated, c + 1)
                    dve.tensor_tensor(X[:, n, gg], X[:, n, gg], t[:, c % 2, :], ALU.add).then_inc(added, 1)


def phase_rownorm(nc, name, K, X, gain, out=None):
    NT = SEQ // P
    with Mem(nc, name) as m:
        sq = m.sb("sq", [P, 2, D])
        ss = m.sb("ss", [P, 3, NT])
        gr = m.sb("gr", [P, D])
        come, summed, rooted, inv, normed, saved = m.sems("come", "summed", "rooted", "inv", "normed", "saved")
        b = m.block()

        @b.sync
        def _(sp):
            sp.dma_start(gr[:, :], gain.rearrange("(a n) -> a n", a=1).to_broadcast([P, D])).then_inc(come, 16)
            if out is not None:
                for t in range(NT):
                    sp.wait_ge(normed, t + 1)
                    sp.dma_start(out[t * P:(t + 1) * P, :], X[:, t, :]).then_inc(saved, 16)
                sp.wait_ge(saved, 16 * NT)

        @b.scalar
        def _(act):
            for t in range(NT):
                if t >= 2:
                    act.wait_ge(summed, t - 1)
                act.activation(sq[:, t % 2, :], X[:, t, :], ACT.Square, accum_out=ss[:, 0, t:t + 1]).then_inc(summed, 1)
            act.wait_ge(summed, NT)
            act.activation(ss[:, 1, :], ss[:, 0, :], ACT.Sqrt, scale=1.0 / D, bias=K.eps[:, 0:1]).then_inc(rooted, 1)

        @b.vector
        def _(dve):
            dve.wait_ge(rooted, 1)
            dve.reciprocal(ss[:, 2, :], ss[:, 1, :]).then_inc(inv, 1)
            dve.wait_ge(inv, 1)
            dve.wait_ge(come, 16)
            for t in range(NT):
                dve.scalar_tensor_tensor(X[:, t, :], X[:, t, :], ss[:, 2, t:t + 1], gr[:, :], ALU.mult, ALU.mult).then_inc(normed, 1)


def phase_router(nc, name, I, K, uT, rgw, rgb, rew, reb, T, slot_dram):
    NT = SEQ // P
    with Mem(nc, name) as m:
        rw = m.sb("rw", [P, KT, NG + NE])
        rb = m.sb("rb", [P, NG + NE])
        L = m.sb("L", [P, NT, NG + NE])
        rc = m.sb("rc", [P, 3, NE + 16])
        upper = m.sb("upper", [P, P])
        a4 = m.sb("a4", [P, NT, NG]); b4 = m.sb("b4", [P, NT, NG]); g1 = m.sb("g1", [P, NT, 1])
        oh = m.sb("oh", [P, NT, NG]); ps = m.sb("ps", [P, NT, 1])
        big = m.sb("big", [P, NT, NG, EG]); sel = m.sb("sel", [P, NT, EG])
        m12 = m.sb("m12", [P, 2, NT, 1]); o12 = m.sb("o12", [P, 2, NT, EG]); c8 = m.sb("c8", [P, NT, EG]); s2 = m.sb("s2", [P, NT, EG])
        e2 = m.sb("e2", [P, NT, 1]); d2 = m.sb("d2", [P, NT, 1])
        A12 = m.sb("A12", [P, 2, NT, NE]); A = m.sb("A", [P, NT, NE])
        pre = m.sb("pre", [P, NT + 1, NE]); rank = m.sb("rank", [P, NT, NE])
        nbf = m.sb("nbf", [P, NE]); nbi = m.sb("nbi", [P, NE], I32); inc = m.sb("inc", [P, NE]); one = m.sb("one", [P, NE])
        start = m.sb("start", [P, NE])
        df = m.sb("df", [P, 2, NT, 1])
        cmp_ = m.sb("cmp", [1, MAXB, NE]); bef = m.sb("bef", [1, MAXB])
        tok = m.sb("tok", [P, NT], I32); zero = m.sb("zero", [MAXB + 1, P], I32)
        bk = m.banks(3)
        come, mm, ev, chain, ex, az, cnt, pool, zeroed, scat = m.sems("come", "mm", "ev", "chain", "ex", "az", "cnt", "pool", "zeroed", "scat")
        b = m.block()
        slots = slot_dram.rearrange("(b p) -> b p", p=P)

        @b.sync
        def _(sp):
            rk = lambda ap: ap.rearrange("l (k p) n -> p (l k) n", p=P)
            sp.dma_start(rw[:, :, 0:NG], rk(rgw)).then_inc(come, 16)
            sp.dma_start(rw[:, :, NG:], rk(rew)).then_inc(come, 16)
            sp.dma_start(rb[:, 0:NG], rgb.to_broadcast([P, NG])).then_inc(come, 16)
            sp.dma_start(rb[:, NG:], reb.to_broadcast([P, NE])).then_inc(come, 16)
            sp.dma_start(rc[:, :, :], I["k_iotas"]).then_inc(come, 16)
            sp.dma_start(upper[:, :], I["k_upper"]).then_inc(come, 16)
            sp.wait_ge(pool, 2)
            sp.dma_start(slots, zero[:, :]).then_inc(zeroed, 16)

        @b.gpsimd
        def _(gp):
            gp.iota(tok[:, :], pattern=[[P, NT]], base=0, channel_multiplier=1).then_inc(pool, 1)
            gp.memset(zero[:, :], 0).then_inc(pool, 1)
            gp.wait_ge(az, 1)
            gp.wait_ge(pool, 2)
            gp.wait_ge(zeroed, 16)
            for j in range(2):
                for t in range(NT):
                    gp.indirect_dma_start(slot_dram.rearrange("(n a) -> n a", a=1),
                                          bass.IndirectOffsetOnAxis(T.dest[:, j, t:t + 1], 0),
                                          tok[:, t:t + 1], None).then_inc(scat, 16)
            gp.wait_ge(scat, 16 * 2 * NT)

        @b.tensor
        def _(pe):
            pe.wait_ge(come, 16 * 6)
            for t in range(NT):
                for k in range(KT):
                    last = pe.matmul(bk[0][:, t * (NG + NE):(t + 1) * (NG + NE)], uT[:, k, t * P:(t + 1) * P], rw[:, k, :],
                                     start=(k == 0), stop=(k == KT - 1))
            last.then_inc(mm, 1)
            pe.wait_ge(cnt, 1)
            flatA = A[:, :, :].rearrange("p t e -> p (t e)")
            pe.matmul(bk[1][:, 0:NT * NE], upper[:, :], flatA, start=True, stop=True)
            pe.matmul(bk[2][:, 0:NT * NE], K.ones[:, :], flatA, start=True, stop=True).then_inc(mm, 1)

        @b.scalar
        def _(act):
            act.wait_ge(chain, 3)
            act.activation(b4[:, :, :], a4[:, :, :], ACT.Exp).then_inc(ex, 1)
            act.wait_ge(cnt, 1)
            act.activation(e2[:, :, :], d2[:, :, :], ACT.Exp).then_inc(ex, 1)

        @b.vector
        def _(dve):
            then = Chain(dve, chain)
            dve.wait_ge(mm, 1)
            dve.wait_ge(come, 16 * 6)
            bc = lambda ap, n: ap.to_broadcast([P, NT, n])
            row = lambda ap, n: ap.rearrange("p (a n) -> p a n", a=1).to_broadcast([P, NT, n])
            then(dve.tensor_tensor(L[:, :, :], bk[0][:, 0:NT * (NG + NE)].rearrange("p (t n) -> p t n", t=NT), row(rb[:, :], NG + NE), ALU.add))
            LG = L[:, :, 0:NG]
            then(dve.tensor_reduce(g1[:, :, :], LG, AXX, ALU.max))
            then(dve.tensor_tensor(a4[:, :, :], LG, bc(g1[:, :, :], NG), ALU.subtract))
            dve.wait_ge(ex, 1)
            then(dve.tensor_reduce(ps[:, :, :], b4[:, :, :], AXX, ALU.add))
            then(dve.reciprocal(ps[:, :, :], ps[:, :, :]))

            def first(out, scratch, x, best, iota, n):
                then(dve.tensor_tensor(scratch, x, bc(best, n), ALU.is_equal))
                then(dve.tensor_tensor(scratch, scratch, iota, ALU.mult))
                then(dve.tensor_reduce(g1[:, :, :], scratch, AXX, ALU.max))
                then(dve.tensor_tensor(out, scratch, bc(g1[:, :, :], n), ALU.is_equal))

            then(dve.tensor_reduce(g1[:, :, :], LG, AXX, ALU.max))
            then(dve.tensor_tensor(b4[:, :, :], LG, bc(g1[:, :, :], NG), ALU.is_equal))
            then(dve.tensor_tensor(b4[:, :, :], b4[:, :, :], row(rc[:, 0, 0:NG], NG), ALU.mult))
            then(dve.tensor_reduce(g1[:, :, :], b4[:, :, :], AXX, ALU.max))
            then(dve.tensor_tensor(oh[:, :, :], b4[:, :, :], bc(g1[:, :, :], NG), ALU.is_equal))
            for t in range(NT):
                last = dve.tensor_tensor(big[:, t, :, :], L[:, t, NG:].rearrange("p (g e) -> p g e", g=NG),
                                         oh[:, t, :].rearrange("p (g a) -> p g a", a=1).to_broadcast([P, NG, EG]), ALU.mult)
            then(last)
            then(dve.tensor_tensor(sel[:, :, :], big[:, :, 0, :], big[:, :, 1, :], ALU.add))
            then(dve.tensor_tensor(sel[:, :, :], sel[:, :, :], big[:, :, 2, :], ALU.add))
            then(dve.tensor_tensor(sel[:, :, :], sel[:, :, :], big[:, :, 3, :], ALU.add))
            then(dve.tensor_reduce(m12[:, 0, :, :], sel[:, :, :], AXX, ALU.max))
            first(o12[:, 0, :, :], c8[:, :, :], sel[:, :, :], m12[:, 0, :, :], row(rc[:, 1, 0:EG], EG), EG)
            then(dve.scalar_tensor_tensor(s2[:, :, :], o12[:, 0, :, :], -BIG, sel[:, :, :], ALU.mult, ALU.add))
            then(dve.tensor_reduce(m12[:, 1, :, :], s2[:, :, :], AXX, ALU.max))
            first(o12[:, 1, :, :], c8[:, :, :], s2[:, :, :], m12[:, 1, :, :], row(rc[:, 1, 0:EG], EG), EG)
            then(dve.tensor_tensor(d2[:, :, :], m12[:, 1, :, :], m12[:, 0, :, :], ALU.subtract))
            for j in range(2):
                for t in range(NT):
                    last = dve.tensor_tensor(A12[:, j, t, :].rearrange("p (g e) -> p g e", g=NG),
                                             oh[:, t, :].rearrange("p (g a) -> p g a", a=1).to_broadcast([P, NG, EG]),
                                             o12[:, j, t, :].rearrange("p (a e) -> p a e", a=1).to_broadcast([P, NG, EG]), ALU.mult)
            then(last)
            dve.tensor_tensor(A[:, :, :], A12[:, 0, :, :], A12[:, 1, :, :], ALU.add).then_inc(cnt, 1)
            dve.wait_ge(ex, 2)
            then(dve.tensor_scalar(d2[:, :, :], e2[:, :, :], 1.0, None, ALU.add))
            then(dve.reciprocal(d2[:, :, :], d2[:, :, :]))
            w = lambda j: T.wt[:, j, :].rearrange("p (t a) -> p t a", a=1)
            then(dve.tensor_tensor(w(0), ps[:, :, :], d2[:, :, :], ALU.mult))
            then(dve.tensor_tensor(w(1), w(0), e2[:, :, :], ALU.mult))
            dve.wait_ge(mm, 2)
            then(dve.memset(pre[:, 0, :], 0.0))
            for t in range(NT):
                then(dve.tensor_tensor(pre[:, t + 1, :], pre[:, t, :], bk[2][:, t * NE:(t + 1) * NE], ALU.add))
            then(dve.tensor_scalar(nbf[:, :], pre[:, NT, :], float(P - 1), None, ALU.add))
            then(dve.tensor_copy(nbi[:, :], nbf[:, :]))
            then(dve.tensor_scalar(nbi[:, :], nbi[:, :], 7, None, ALU.arith_shift_right))
            then(dve.tensor_copy(nbf[:, :], nbi[:, :]))
            then(dve.memset(one[:, :], 1.0))
            then(dve.tensor_tensor_scan(inc[:, :], one[:, :], nbf[:, :], 0.0, ALU.mult, ALU.add))
            then(dve.tensor_tensor(start[:, :], inc[:, :], nbf[:, :], ALU.subtract))
            then(dve.tensor_tensor(rank[:, :, :], bk[1][:, 0:NT * NE].rearrange("p (t e) -> p t e", t=NT), pre[:, 0:NT, :], ALU.add))
            then(dve.scalar_tensor_tensor(rank[:, :, :], row(start[:, :], NE), float(P), rank[:, :, :], ALU.mult, ALU.add))
            for j in range(2):
                then(dve.tensor_tensor(A12[:, j, :, :], A12[:, j, :, :], rank[:, :, :], ALU.mult))
                then(dve.tensor_reduce(df[:, j, :, :], A12[:, j, :, :], AXX, ALU.add))
            dve.tensor_copy(T.dest[:, :, :], df[:, :, :, :].rearrange("p j t a -> p j (t a)")).then_inc(az, 1)
            then(dve.tensor_tensor(cmp_[:, :, :], inc[0:1, :].rearrange("p (a e) -> p a e", a=1).to_broadcast([1, MAXB, NE]),
                                   rc[0:1, 2, 0:MAXB].rearrange("p (b a) -> p b a", a=1).to_broadcast([1, MAXB, NE]), ALU.is_le))
            then(dve.tensor_reduce(bef[:, :].rearrange("p (b a) -> p b a", a=1), cmp_[:, :, :], AXX, ALU.add))
            then(dve.tensor_scalar(bef[:, :], bef[:, :], float(NE - 1), None, ALU.min))
            dve.tensor_copy(T.be[:, :], bef[:, :])
            then(dve.tensor_scalar(nbf[0:1, 0:1], inc[0:1, NE - 1:NE], 1.0, None, ALU.add))
            then(dve.tensor_copy(nbi[0:1, 0:1], nbf[0:1, 0:1]))
            dve.tensor_scalar(T.nb[:, :], nbi[0:1, 0:1], 1, None, ALU.arith_shift_right)


def phase_experts(nc, name, K, hidden, w1, w3, w2, scale, shift, T, slot_dram, y_dram, out_dram):
    HT = hidden // P
    NB = MAXB + 1
    with Mem(nc, name) as m:
        wu = m.sb("wu", [P, 2, 2, KT, hidden])
        wd = m.sb("wd", [P, 2, HT, D])
        rows = m.sb("rows", [NB, P], I32); rowsf = m.sb("rowsf", [NB, P])
        idx = m.sb("idx", [P, NB], I32); now = m.sb("now", [P, 2], I32)
        xg = m.sb("xg", [P, 2, D])
        uT = m.sb("uT", [P, 2, KT, P])
        si = m.sb("si", [P, hidden])
        hT = m.sb("hT", [P, hidden])
        yo = m.sb("yo", [P, 2, D])
        bk = m.banks(8)
        wufull = m.sems("wufull0", "wufull1"); wdfull = m.sems("wdfull0", "wdfull1")
        xfull = m.sems("xfull0", "xfull1"); saved = m.sems("saved0", "saved1")
        rcome, rfloat, rturn, rint, picked = m.sems("rcome", "rfloat", "rturn", "rint", "picked")
        wufree, wdfree, xt, ux, up, sil, gated, ymm, yout = m.sems(
            "wufree", "wdfree", "xt", "ux", "up", "sil", "gated", "ymm", "yout")
        b = m.block()
        pairs = dict(min_val=1, max_val=MAXB // 2)

        @b.sync
        def _(sp):
            sp.dma_start(rows[:, :], slot_dram.rearrange("(b p) -> b p", p=P)).then_inc(rcome, 16)
            n = sp.value_load(T.nb[0:1, 0:1], **pairs)
            with sp.Fori(0, n) as i:
                for s in range(2):
                    e = sp.value_load(T.be[0:1, bass.ds(i * 2 + s, 1)], min_val=0, max_val=NE - 1)
                    sp.wait_ge(wufree, i * 2 + (s + 1))
                    for j, wj in enumerate((w1, w3)):
                        sp.dma_start(wu[:, s, j, :, :], wj[:, bass.ds(e, 1), :, :].rearrange("p a k n -> p (a k) n")).then_inc(wufull[s], 16)
                    sp.wait_ge(wdfree, i * 2 + (s + 1))
                    sp.dma_start(wd[:, s, :, :], w2[:, bass.ds(e, 1), :, :].rearrange("p a k n -> p (a k) n")).then_inc(wdfull[s], 16)

        @b.gpsimd
        def _(gp):
            n = gp.value_load(T.nb[0:1, 0:1], **pairs)
            gp.wait_ge(rint, 1)
            gp.indirect_dma_start(xg[:, 0, :], None, y_dram, bass.IndirectOffsetOnAxis(idx[:, 0:1], 0)).then_inc(xfull[0], 16)
            with gp.Fori(0, n) as i:
                for s in range(2):
                    hold(gp, xt, i * 2 + (s + 2))
                    gp.tensor_copy(now[:, 1 - s:2 - s], idx[:, bass.ds(i * 2 + (s + 1), 1)]).then_inc(picked, 1)
                    hold(gp, picked, i * 2 + (s + 1))
                    gp.indirect_dma_start(xg[:, 1 - s, :], None, y_dram, bass.IndirectOffsetOnAxis(now[:, 1 - s:2 - s], 0)).then_inc(xfull[1 - s], 16)

        @b.tensor
        def _(pe):
            pe.wait_ge(rfloat, 1)
            pe.transpose(bk[4][:, 0:NB], rowsf[:, :], K.ident[0:NB, 0:NB]).then_inc(rturn, 1)
            n = pe.value_load(T.nb[0:1, 0:1], **pairs)
            pe.sem_inc(wufree, 2)
            pe.sem_inc(wdfree, 2)
            pe.sem_inc(xt, 2)
            pe.sem_inc(ymm, 1)

            def turn(slot):
                for k in range(KT):
                    last = pe.transpose(bk[k // 4][:, k % 4 * P:(k % 4 + 1) * P], xg[:, slot, k * P:(k + 1) * P], K.ident[:, :])
                last.then_inc(xt, 1)

            pe.wait_ge(xfull[0], 16)
            turn(0)
            with pe.Fori(0, n) as i:
                for s in range(2):
                    pe.wait_ge(ux, i * 4 + (2 * s + 2))
                    pe.wait_ge(wufull[s], i * 32 + 32)
                    pe.wait_ge(gated, i * 2 + (s + 1))
                    for j in range(2):
                        for h in range(HT):
                            for k in range(KT):
                                last = pe.matmul(bk[2 + j][:, h * P:(h + 1) * P], wu[:, s, j, k, h * P:(h + 1) * P], uT[:, s, k, :],
                                                 start=(k == 0), stop=(k == KT - 1))
                        last.then_inc(up, 1)
                    pe.wait_ge(xfull[1 - s], i * 16 + (16 + 16 * s))
                    turn(1 - s)
                    pe.wait_ge(up, i * 4 + (2 * s + 2))
                    pe.sem_inc(wufree, 1)
                    pe.wait_ge(gated, i * 2 + (s + 2))
                    pe.wait_ge(wdfull[s], i * 16 + 16)
                    pe.wait_ge(yout, i * 4 + (2 * s + 2))
                    for j in range(2):
                        for k in range(HT):
                            last = pe.matmul(bk[5 + j][:, :], hT[:, k * P:(k + 1) * P], wd[:, s, k, j * HALF:(j + 1) * HALF], start=(k == 0), stop=(k == HT - 1))
                        last.then_inc(ymm, 1)
                    pe.wait_ge(ymm, i * 4 + (2 * s + 3))
                    pe.sem_inc(wdfree, 1)

        @b.scalar
        def _(act):
            n = act.value_load(T.nb[0:1, 0:1], **pairs)

            def scaled(slot):
                for k in range(KT):
                    last = act.activation(uT[:, slot, k, :], bk[k // 4][:, k % 4 * P:(k % 4 + 1) * P], ACT.Identity, scale=scale(k),
                                          bias=shift(k) if shift else 0.0)
                    if k % 4 == 3:
                        last.then_inc(ux, 1)

            act.wait_ge(xt, 3)
            scaled(0)
            with act.Fori(0, n) as i:
                for s in range(2):
                    hold(act, up, i * 4 + (2 * s + 1))
                    hold(act, gated, i * 2 + (s + 1))
                    act.activation(si[:, :], bk[2][:, 0:hidden], ACT.Silu).then_inc(sil, 1)
                    hold(act, xt, i * 2 + (s + 4))
                    scaled(1 - s)
                    for j in range(2):
                        hold(act, ymm, i * 4 + (2 * s + j + 2))
                        if j == 0:
                            hold(act, saved[s], i * 16 + 16)
                        act.activation(yo[:, s, j * HALF:(j + 1) * HALF], bk[5 + j][:, :], ACT.Copy).then_inc(yout, 1)
                    act.wait_ge(yout, i * 4 + (2 * s + 4))
                    act.dma_start(out_dram[bass.ds(i * 256 + s * P, P), :], yo[:, s, :]).then_inc(saved[s], 16)
            for s in range(2):
                hold(act, saved[s], n * 16 + 16)

        @b.vector
        def _(dve):
            dve.wait_ge(rcome, 16)
            dve.tensor_copy(rowsf[:, :], rows[:, :]).then_inc(rfloat, 1)
            dve.wait_ge(rturn, 1)
            dve.tensor_copy(idx[:, :], bk[4][:, 0:NB]).then_inc(rint, 1)
            n = dve.value_load(T.nb[0:1, 0:1], **pairs)
            dve.sem_inc(gated, 1)
            dve.sem_inc(yout, 2)
            for s in range(2):
                dve.sem_inc(saved[s], 16)
            with dve.Fori(0, n) as i:
                for s in range(2):
                    dve.wait_ge(sil, i * 2 + (s + 1))
                    dve.wait_ge(up, i * 4 + (2 * s + 2))
                    dve.wait_ge(ymm, i * 4 + (2 * s + 1))
                    dve.tensor_tensor(hT[:, :], si[:, :], bk[3][:, 0:hidden], ALU.mult).then_inc(gated, 1)


def phase_combine(nc, name, X, T, out_dram, gate=None):
    NT = SEQ // P
    with Mem(nc, name) as m:
        g = m.sb("g", [P, 2, 2, D])
        a = m.sb("a", [P, 2, D])
        full = m.sems("full0", "full1")
        free, chain = m.sems("free", "chain")
        b = m.block()

        @b.gpsimd
        def _(gp):
            for t in range(NT):
                if t >= 2:
                    gp.wait_ge(free, t - 1)
                for j in range(2):
                    gp.indirect_dma_start(g[:, t % 2, j, :], None, out_dram[0:MAXB * P, :], bass.IndirectOffsetOnAxis(T.dest[:, j, t:t + 1], 0)).then_inc(full[t % 2], 16)

        @b.vector
        def _(dve):
            then = Chain(dve, chain)
            for t in range(NT):
                s = t % 2
                dve.wait_ge(full[s], 32 * (t // 2 + 1))
                then(dve.tensor_scalar(a[:, s, :], g[:, s, 0, :], T.wt[:, 0, t:t + 1], None, ALU.mult))
                dve.scalar_tensor_tensor(a[:, s, :], g[:, s, 1, :], T.wt[:, 1, t:t + 1], a[:, s, :], ALU.mult, ALU.add).then_inc(free, 1)
                dve.wait_ge(free, t + 1)
                if gate is not None:
                    then(dve.tensor_tensor(a[:, s, :], a[:, s, :], gate, ALU.mult))
                then(dve.tensor_tensor(X[:, t, :], X[:, t, :], a[:, s, :], ALU.add))


RC = 512
NP = 4
CH = 64
NC = SEQ // CH
DECAY = float(np.exp(-0.5))
LNX_EPS = 64e-5
LEVELS = 5


def phase_taps(nc, name, w, xT, zc, ntiles, unroll, tap, bias=None, aside=()):
    with Mem(nc, name) as m:
        wt = m.sb("w", [P, unroll, KT, P])
        up = m.sb("up", [P, unroll, SEQ + 2])
        nb = 2 * unroll
        bk = m.banks(nb)
        wfull = m.sems(*[f"wfull{s}" for s in range(unroll)])
        wfree, done, free, evac, conv, chain, zero, asided = m.sems("wfree", "done", "free", "evac", "conv", "chain", "zero", "asided")
        b = m.block()
        steps = ntiles // unroll
        assert steps * unroll == ntiles

        @b.sync
        def _(sp):
            with sp.Fori(0, steps) as i:
                for s in range(unroll):
                    sp.wait_ge(wfree, i * unroll + (s + 1))
                    sp.dma_start(wt[:, s, :, :], w[:, :, bass.ds(i * (unroll * P) + s * P, P)]).then_inc(wfull[s], 16)

        @b.gpsimd
        def _(gp):
            for s in range(unroll):
                for n in (0, SEQ + 1):
                    gp.memset(up[:, s, n:n + 1], 0.0).then_inc(zero, 1)
            for n, (dst, src) in enumerate(aside):
                gp.dma_start(dst, src).then_inc(asided, 16)
                gp.wait_ge(asided, 16 * (n + 1))

        @b.tensor
        def _(pe):
            pe.sem_inc(wfree, unroll)
            with pe.Fori(0, steps) as i:
                for s in range(unroll):
                    pe.wait_ge(wfull[s], i * 16 + 16)
                    for h in range(2):
                        pe.wait_ge(free, i * nb + (s * 2 + h + 1))
                        for k in range(KT):
                            last = pe.matmul(bk[s * 2 + h][:, :], wt[:, s, k, :], xT[:, k, h * HALF:(h + 1) * HALF],
                                             start=(k == 0), stop=(k == KT - 1))
                        last.then_inc(done, 1)
                    pe.wait_ge(done, i * nb + (s + 1) * 2)
                    pe.sem_inc(wfree, 1)

        @b.scalar
        def _(act):
            act.sem_inc(free, nb)
            with act.Fori(0, steps) as i:
                for s in range(unroll):
                    act.wait_ge(conv, i * unroll + (s + 1))
                    for h in range(2):
                        hold(act, done, i * nb + (s * 2 + h + 1))
                        act.activation(up[:, s, 1 + h * HALF:1 + (h + 1) * HALF], bk[s * 2 + h][:, :], ACT.Identity,
                                       bias=bias(i * unroll + s) if bias else 0.0).then_inc(evac, 1)
                    act.wait_ge(evac, i * nb + (s * 2 + 2))
                    act.sem_inc(free, 2)

        @b.vector
        def _(dve):
            dve.sem_inc(conv, unroll)
            dve.wait_ge(zero, 2 * unroll)
            with dve.Fori(0, steps) as i:
                then = Chain(dve, chain, i, 2 * unroll)
                for s in range(unroll):
                    t = i * unroll + s
                    dve.wait_ge(evac, i * nb + (s * 2 + 2))
                    o = zc[:, bass.ds(t, 1), :].rearrange("p a n -> p (a n)")
                    then(dve.tensor_scalar(o, up[:, s, 0:SEQ], tap(0, t), tap(3, t), ALU.mult, ALU.add))
                    then(dve.scalar_tensor_tensor(o, up[:, s, 1:SEQ + 1], tap(1, t), o, ALU.mult, ALU.add))
                    dve.scalar_tensor_tensor(o, up[:, s, 2:SEQ + 2], tap(2, t), o, ALU.mult, ALU.add).then_inc(conv, 1)
                then.end()


def phase_rwkv_consts(nc, I, K, W, aside):
    with Mem(nc, "rwc") as m:
        come, s = m.sems("come", "s")
        b = m.block()

        @b.sync
        def _(sp):
            for dst, src in ((W.tri[:, :, :, :], I["k_tri"]), (W.level[:, :, :, :], I["k_level"]),
                             (W.headones[:, :], I["k_headones"]), (W.carry[:, :], I["k_carry"]), (W.eye64[:, :], I["k_eye64"]),
                             (W.wup[:, :], I["w_up_2"].rearrange("l d r c -> (l d r) c")),
                             (W.aup[:, :], I["a_up_2"].rearrange("l d r c -> (l d r) c")), (W.gup[:, :], I["g_up_2"][0])) + aside:
                sp.dma_start(dst, src).then_inc(come, 16)
            sp.wait_ge(come, 16 * (8 + len(aside)))

        @b.vector
        def _(dve):
            p, n = PLACES["mu_prev_2"][0], PLACES["mu_next_2"][0]
            k = PLACES["k_a_2"][0]
            dve.tensor_tensor(W.mid[:, :], K.cols[:, p:p + 15], K.cols[:, n:n + 15], ALU.add).then_inc(s, 1)
            dve.wait_ge(s, 1)
            dve.tensor_scalar(W.mid[:, :], W.mid[:, :], -1.0, 1.0, ALU.mult, ALU.add)
            dve.tensor_scalar(W.ka1[:, :], K.cols[:, k:k + 4], -1.0, 1.0, ALU.mult, ALU.add)
            dve.memset(W.lnx_eps[:, :], LNX_EPS)
            dve.memset(W.zero[:, :], 0.0)


def phase_rwkv_gates(nc, Z):
    with Mem(nc, "rwg") as m:
        b = m.block()

        @b.scalar
        def _(act):
            act.activation(Z[:, 12, :], Z[:, 12, :], ACT.Tanh)
            act.activation(Z[:, 14, :], Z[:, 14, :], ACT.Sigmoid)


def phase_rwkv_prep(nc, K, W, Z, p, pr, elc, bv):
    with Mem(nc, f"rp{p}") as m:
        sw = m.sb("sw", [P, 2, SEQ]); ag = m.sb("ag", [P, 2, SEQ]); kk = m.sb("kk", [P, SEQ]); sq = m.sb("sq", [P, SEQ])
        cs = m.sb("cs", [P, 2, SEQ]); ex = m.sb("ex", [P, 2, SEQ]); E = m.sb("E", [P, 3, SEQ]); kd = m.sb("kd", [P, 2, SEQ])
        bk = m.banks(8)
        (mm, scaled, squared, sg, root, inv, floored, normed, summed, shifted, kmade, bmade, ksum, decay, scaled_up, bonus) = m.sems(
            "mm", "scaled", "squared", "sg", "root", "inv", "floored", "normed", "summed", "shifted", "kmade", "bmade", "ksum",
            "decay", "scaled_up", "bonus")
        r, k, v = Z[:, p, :], Z[:, 4 + p, :], Z[:, 8 + p, :]
        hs = [slice(0, HALF), slice(HALF, SEQ)]
        b = m.block()

        @b.tensor
        def _(pe):
            for j, (up, src) in enumerate(((W.wup, 12), (W.aup, 13))):
                for d in range(2):
                    dd = slice(64 * d, 64 * d + 64)
                    for x in range(2):
                        pe.matmul(bk[4 * j + 2 * d + x][:, :], up[dd, p * P:(p + 1) * P], Z[dd, src, hs[x]], start=True, stop=True).then_inc(mm, 1)
            pe.wait_ge(sg, 2)
            pe.wait_ge(squared, 1)
            for x in range(2):
                pe.matmul(bk[x][:, :], W.headones[:, :], sq[:, hs[x]], start=True, stop=True).then_inc(mm, 1)
            pe.wait_ge(sg, 4)
            pe.wait_ge(bonus, 1)
            for x in range(2):
                pe.matmul(bk[2 + x][:, :], W.headones[:, :], sq[:, hs[x]], start=True, stop=True).then_inc(mm, 1)

        @b.scalar
        def _(act):
            act.wait_ge(scaled, 1)
            act.activation(sq[:, :], kk[:, :], ACT.Square).then_inc(squared, 1)
            for j, (dst, name) in enumerate(((sw, "w0_2"), (ag, "a0_2"))):
                for d in range(2):
                    for x in range(2):
                        act.wait_ge(mm, 4 * j + 2 * d + x + 1)
                        act.activation(dst[:, d, hs[x]], bk[4 * j + 2 * d + x][:, :], ACT.Sigmoid, bias=vec(K.cols, name, 4 * d + p)).then_inc(sg, 1)
            for x in range(2):
                act.wait_ge(mm, 9 + x)
                act.activation(E[:, 0, hs[x]], bk[x][:, :], ACT.Sqrt).then_inc(root, 1)
            act.wait_ge(inv, 1)
            for d in range(2):
                act.wait_ge(shifted, d + 1)
                if d:
                    act.wait_ge(scaled_up, 4)
                act.activation(E[:, 0, :], cs[:, d, :], ACT.Exp, scale=-DECAY).then_inc(decay, 1)
                act.activation(E[:, 1, :], cs[:, d, :], ACT.Exp, scale=DECAY).then_inc(decay, 1)
                act.activation(E[:, 2, :], ex[:, d, :], ACT.Exp, scale=-DECAY).then_inc(decay, 1)
                act.activation(elc[:, d, :], W.tot[:, d, :], ACT.Exp, scale=-DECAY)

        @b.gpsimd
        def _(gp):
            gp.wait_ge(sg, 8)
            for d in range(2):
                gp.tensor_scalar(kd[:, d, :], ag[:, d, :], vec(K.cols, "k_a_2", p), W.ka1[:, p:p + 1], ALU.mult, ALU.add).then_inc(kmade, 1)
            for d in range(2):
                gp.wait_ge(kmade, 1 + d)
                gp.tensor_tensor(kd[:, d, :], kd[:, d, :], k, ALU.mult).then_inc(kmade, 1)
            gp.wait_ge(inv, 1)
            gp.tensor_tensor(ag[:, 0, :], ag[:, 0, :], kk[:, :], ALU.mult).then_inc(bmade, 1)
            gp.tensor_tensor(ag[:, 1, :], ag[:, 1, :], kk[:, :], ALU.mult).then_inc(bmade, 1)
            gp.wait_ge(mm, 10)
            gp.wait_ge(kmade, 4)
            gp.tensor_tensor(sq[:, :], kd[:, 0, :], kd[:, 1, :], ALU.add).then_inc(ksum, 1)

        @b.vector
        def _(dve):
            dve.tensor_scalar(kk[:, :], k, vec(K.cols, "k_k_2", p), None, ALU.mult).then_inc(scaled, 1)
            t3 = lambda ap: ap.rearrange("p (c n) -> p c n", n=CH)
            for d in range(2):
                dve.wait_ge(sg, 2 * d + 2)
                dve.tensor_tensor_scan(cs[:, d, :], W.carry[:, :], sw[:, d, :], 0.0, ALU.mult, ALU.add).then_inc(summed, 1)
            dve.wait_ge(summed, 1)
            dve.tensor_copy(W.tot[:, 0, :], t3(cs[:, 0, :])[:, :, CH - 1])
            dve.tensor_tensor(ex[:, 0, :], cs[:, 0, :], sw[:, 0, :], ALU.subtract).then_inc(shifted, 1)
            dve.wait_ge(summed, 2)
            dve.tensor_copy(W.tot[:, 1, :], t3(cs[:, 1, :])[:, :, CH - 1]).then_inc(summed, 1)
            dve.tensor_tensor(t3(ex[:, 1, :]), t3(cs[:, 1, :])[:, :, CH - 1:CH].to_broadcast([P, NC, CH]), t3(cs[:, 1, :]), ALU.subtract).then_inc(summed, 1)
            dve.wait_ge(summed, 4)
            dve.tensor_tensor(cs[:, 1, :], ex[:, 1, :], sw[:, 1, :], ALU.add).then_inc(shifted, 1)
            dve.wait_ge(scaled, 1)
            dve.wait_ge(root, 2)
            dve.tensor_scalar(E[:, 0, :], E[:, 0, :], 1e-12, None, ALU.max).then_inc(floored, 1)
            dve.wait_ge(floored, 1)
            dve.reciprocal(E[:, 0, :], E[:, 0, :]).then_inc(normed, 1)
            dve.wait_ge(normed, 1)
            dve.wait_ge(squared, 1)
            dve.tensor_tensor(kk[:, :], kk[:, :], E[:, 0, :], ALU.mult).then_inc(inv, 1)
            dve.wait_ge(inv, 1)
            for d in range(2):
                dve.wait_ge(decay, 3 * d + 1)
                dve.tensor_tensor(pr[:, d, 3, :], r, E[:, 0, :], ALU.mult).then_inc(scaled_up, 1)
                dve.wait_ge(decay, 3 * d + 3)
                dve.scalar_tensor_tensor(pr[:, d, 0, :], kk[:, :], -1.0, E[:, 2, :], ALU.mult, ALU.mult).then_inc(scaled_up, 1)
                dve.wait_ge(kmade, 4)
                dve.tensor_tensor(pr[:, d, 2, :], kd[:, d, :], E[:, 1, :], ALU.mult).then_inc(scaled_up, 1)
                dve.wait_ge(bmade, d + 1)
                dve.tensor_tensor(pr[:, d, 1, :], ag[:, d, :], E[:, 1, :], ALU.mult).then_inc(scaled_up, 1)
                if d == 0:
                    dve.wait_ge(ksum, 1)
                    dve.scalar_tensor_tensor(sq[:, :], sq[:, :], vec(K.cols, "r_k_2", p), r, ALU.mult, ALU.mult).then_inc(bonus, 1)
            for x in range(2):
                dve.wait_ge(mm, 11 + x)
                dve.tensor_tensor(bv[:, hs[x]], bk[2 + x][:, :], v[:, hs[x]], ALU.mult)


PE_O = ["b1", "b2", "b0", "b3", "x1", "akv"] + [f"{s}_{l}" for l in range(1, 6) for s in ("p1", "p2", "p3") if (s, l) != ("p2", 5)] + ["w", "qg", "h0", "s1", "y", "s2"]
ACT_O = ["aN", "bN", "kvN", "x1", "akv"] + [f"p1_{l}" for l in range(1, 6)] + ["w", "h"]
DVE_O = ["ATk", "ATb"] + [f"{s}{l}" for l in range(1, 6) for s in ("x", "xt") if (s, l) != ("x", 5)] + ["qg", "s1", "s2", "y"]
POOL_O = ["fillA", "fillR", "y1"] + [f"m{l}" for l in range(1, 6)]


def count(order, i, name):
    return i * len(order) + (len(order) + order.index(name) + 1)


def before(order, i, name):
    return i * len(order) + (order.index(name) + 1)


def phase_rwkv_chunks(nc, K, W, Z, p, pr, elc, Y):
    with Mem(nc, f"rc{p}") as m:
        sb2 = lambda name, shape: [m.sb(f"{name}{d}", [P] + shape) for d in range(2)]
        ar = sb2("ar", [2, 2, P])
        bT, kT, vT = sb2("bT", [2, P]), sb2("kT", [2, P]), sb2("vT", [2, P])
        ri = sb2("ri", [2, 2, P])
        lev = sb2("lev", [6, 2, P])
        arb = sb2("arb", [2, 3, P])
        ark = sb2("ark", [2, 2, P])
        rw = sb2("rw", [2, 2, P])
        kv = sb2("kv", [2, 2, P])
        xy = sb2("xy", [2, 2, P])
        p1 = sb2("p1", [2, P])
        w = sb2("w", [2, 2, P])
        qg = sb2("qg", [2, 2, P])
        hh = sb2("hh", [2, P])
        S = sb2("S", [P])
        bk8 = m.banks(8)
        bk = [bk8[0:4], bk8[4:8]]
        pes, acs, dvs, pos = m.sems("pe0", "pe1"), m.sems("act0", "act1"), m.sems("dve0", "dve1"), m.sems("pool0", "pool1")
        zeroed, = m.sems("zeroed")
        xyinit = m.sems("xyinit0", "xyinit1")
        b = m.block()
        STEPS = NC // 2
        b4 = lambda bank: bank[:, :].rearrange("p (j x n) -> p j x n", j=2, x=2)
        bj = lambda bank, j: bank[:, j * P:(j + 1) * P]
        b2 = lambda bank, half=0: bank[:, half * 256:half * 256 + 256].rearrange("p (j n) -> p j n", j=2)
        tok0 = lambda it, d: it * 128 if d == 0 else it * -128 + 14 * CH
        order = lambda d: (0, 1) if d == 0 else (1, 0)

        @b.gpsimd
        def _(gp):
            for d in range(2):
                gp.memset(S[d][:, :], 0.0).then_inc(zeroed, 1)
            gp.wait_ge(zeroed, 2)
            for d in range(2):
                for j in range(2):
                    gp.tensor_copy(ri[d][:, j, 1, :], K.ident[:, :])
            for d in range(2):
                gp.sem_inc(pos[d], len(POOL_O))
            with gp.Fori(0, STEPS) as it:
                for d in range(2):
                    def spread(dst, src):
                        for j in range(2):
                            last = gp.tensor_tensor(dst[:, j, :].rearrange("p (h n) -> p h n", h=2),
                                                    src[:, bass.ds(tok0(it, d) + j * CH, CH)].rearrange("p (a n) -> p a n", a=1).to_broadcast([P, 2, CH]),
                                                    W.headones[:, :].rearrange("p (h n) -> p h n", h=2), ALU.mult)
                        return last
                    hold(gp, pes[d], before(PE_O, it, "b3"))
                    spread(ar[d][:, :, 0, :], pr[:, d, 0, :])
                    spread(ar[d][:, :, 1, :], pr[:, d, 3, :])
                    spread(bT[d], pr[:, d, 1, :])
                    spread(kT[d], pr[:, d, 2, :])
                    spread(vT[d], Z[:, 8 + p, :]).then_inc(pos[d], 1)
                    hold(gp, dvs[d], before(DVE_O, it, "qg"))
                    spread(ri[d][:, :, 0, :], pr[:, d, 3, :]).then_inc(pos[d], 1)
                for l in range(6):
                    for d in range(2):
                        if l == 0:
                            hold(gp, dvs[d], count(DVE_O, it, "ATb"))
                        gp.tensor_tensor(lev[d][:, l, :, :], arb[d][:, :, 0, :], W.level[:, d, l:l + 1, :].to_broadcast([P, 2, P]),
                                         ALU.mult).then_inc(pos[d], 1)

        @b.tensor
        def _(pe):
            pe.wait_ge(zeroed, 2)
            for d in range(2):
                pe.sem_inc(pes[d], len(PE_O))
            with pe.Fori(0, STEPS) as it:
                at = lambda sems, o, d, name: pe.wait_ge(sems[d], count(o, it, name))
                for d in range(2):
                    B = bk[d]
                    at(pos, POOL_O, d, "fillA")
                    pe.wait_ge(dvs[d], before(DVE_O, it, "qg"))
                    for j in range(2):
                        last = pe.matmul(B[1][:, j * 256:(j + 1) * 256], kT[d][:, j, :], ar[d][:, j, :, :].rearrange("p x n -> p (x n)"), start=True, stop=True)
                    last.then_inc(pes[d], 1)
                    pe.wait_ge(acs[d], before(ACT_O, it, "h"))
                    for j in range(2):
                        pe.transpose(bj(B[2], j), ar[d][:, j, 0, :], K.ident[:, :])
                    for j in range(2):
                        last = pe.transpose(bj(B[2], 2 + j), bT[d][:, j, :], K.ident[:, :])
                    last.then_inc(pes[d], 1)
                    pe.wait_ge(dvs[d], before(DVE_O, it, "s2"))
                    for j in range(2):
                        last = pe.matmul(B[0][:, j * 256:(j + 1) * 256], bT[d][:, j, :], ar[d][:, j, :, :].rearrange("p x n -> p (x n)"), start=True, stop=True)
                    last.then_inc(pes[d], 1)
                    pe.wait_ge(dvs[d], before(DVE_O, it, "y"))
                    for j in range(2):
                        pe.transpose(bj(B[3], j), kT[d][:, j, :], K.ident[:, :])
                    for j in range(2):
                        last = pe.transpose(bj(B[3], 2 + j), vT[d][:, j, :], K.ident[:, :])
                    last.then_inc(pes[d], 1)
                for d in range(2):
                    at(dvs, DVE_O, d, "ATb")
                    at(acs, ACT_O, d, "kvN")
                    for j in range(2):
                        last = pe.matmul(bj(bk[d][1], j), ark[d][:, j, 0, :], kv[d][:, 1, j, :], start=True, stop=True)
                    at(pos, POOL_O, d, "y1")
                    pe.wait_ge(xyinit[d], it + 1)
                    for j in range(2):
                        last2 = pe.transpose(bj(bk[d][0], j), xy[d][:, 1, j, :], K.ident[:, :])
                    last2.then_inc(pes[d], 2)
                def level(d, l, part):
                    if part == 1:
                        at(pos, POOL_O, d, f"m{l}")
                        at(*((acs, ACT_O, d, "akv") if l == 1 else (dvs, DVE_O, d, f"x{l - 1}")))
                    elif part == 2 or l == 5:
                        at(acs, ACT_O, d, f"p1_{l}")
                        if l > 1:
                            at(dvs, DVE_O, d, f"xt{l - 1}")
                    for j in range(2):
                        if part == 1:
                            last = pe.matmul(bj(bk[d][2], j), lev[d][:, l, j, :], xy[d][:, 0, j, :], start=True, stop=True)
                        elif part == 2:
                            last = pe.matmul(bj(bk[d][0], j), xy[d][:, 1, j, :], p1[d][:, j, :], start=True, stop=True)
                        else:
                            last = pe.matmul(bj(bk[d][3], j), p1[d][:, j, :], xy[d][:, 1, j, :], start=True, stop=True)
                    last.then_inc(pes[d], 1)

                level(0, 1, 1)
                level(1, 1, 1)
                for l in range(1, 5):
                    level(0, l, 2)
                    level(0, l, 3)
                    level(1, l, 2)
                    level(0, l + 1, 1)
                    level(1, l, 3)
                    level(1, l + 1, 1)
                level(0, 5, 3)
                level(1, 5, 3)
                for d in range(2):
                    at(dvs, DVE_O, d, "xt5")
                    for j in range(2):
                        last = pe.matmul(bk[d][0][:, j * 256:(j + 1) * 256], xy[d][:, 1, j, :], rw[d][:, j, :, :].rearrange("p x n -> p (x n)"), start=True, stop=True)
                    last.then_inc(pes[d], 1)
                for d in range(2):
                    at(acs, ACT_O, d, "w")
                    for j in range(2):
                        last = pe.matmul(bk[d][1][:, j * 256:(j + 1) * 256], w[d][:, j, 0, :], arb[d][:, j, 1:3, :].rearrange("p x n -> p (x n)"), start=True, stop=True)
                    last.then_inc(pes[d], 1)
                    for j in range(2):
                        pe.matmul(bj(bk[d][2], j), arb[d][:, j, 2, :], w[d][:, j, 1, :], start=True, stop=False)
                        last = pe.matmul(bj(bk[d][2], j), kv[d][:, 0, j, :], kv[d][:, 1, j, :], start=False, stop=True)
                    last.then_inc(pes[d], 1)
                for n in range(2):
                    for d in range(2):
                        j = order(d)[n]
                        at(dvs, DVE_O, d, "qg" if n == 0 else "s1")
                        y = lambda: (pe.matmul(bj(bk[d][3], j), qg[d][:, j, 0, :], S[d][:, :], start=True, stop=False),
                                     pe.matmul(bj(bk[d][3], j), arb[d][:, j, 1, :], w[d][:, j, 1, :], start=False, stop=False),
                                     pe.matmul(bj(bk[d][3], j), ark[d][:, j, 1, :], kv[d][:, 1, j, :], start=False, stop=True))[-1]
                        if n == 0:
                            y()
                        else:
                            y().then_inc(pes[d], 1)
                        pe.matmul(bj(bk[d][0], j), qg[d][:, j, 1, :], S[d][:, :], start=True, stop=True).then_inc(pes[d], 1)

        @b.scalar
        def _(act):
            for d in range(2):
                act.sem_inc(acs[d], len(ACT_O))
            with act.Fori(0, STEPS) as it:
                at = lambda sems, o, d, name: hold(act, sems[d], count(o, it, name))
                for d in range(2):
                    at(pes, PE_O, d, "b2")
                    act.activation(rw[d][:, :, 0, :], b2(bk[d][2]), ACT.Copy).then_inc(acs[d], 1)
                    act.activation(arb[d][:, :, 2, :], b2(bk[d][2], 1), ACT.Copy).then_inc(acs[d], 1)
                    at(pes, PE_O, d, "b3")
                    act.activation(kv[d][:, :, :, :].rearrange("p x j n -> p (x j n)"), bk[d][3][:, :], ACT.Copy).then_inc(acs[d], 1)
                for d in range(2):
                    at(pes, PE_O, d, "akv")
                    act.activation(xy[d][:, 0, :, :], b2(bk[d][0]), ACT.Copy).then_inc(acs[d], 1)
                    act.activation(rw[d][:, :, 1, :], b2(bk[d][1]), ACT.Copy).then_inc(acs[d], 1)
                for l in range(1, 6):
                    for d in range(2):
                        at(pes, PE_O, d, f"p1_{l}")
                        act.activation(p1[d][:, :, :], b2(bk[d][2]), ACT.Copy).then_inc(acs[d], 1)
                for d in range(2):
                    at(pes, PE_O, d, "w")
                    act.activation(w[d][:, :, :, :].rearrange("p j x n -> p (j x n)"), bk[d][0][:, :], ACT.Copy).then_inc(acs[d], 1)
                for d in range(2):
                    at(pes, PE_O, d, "h0")
                    for j in range(2):
                        c = it * 2 + j if d == 0 else it * -2 + (14 + j)
                        last = act.activation(hh[d][:, j, :], bj(bk[d][2], j), ACT.Copy, scale=elc[:, d, bass.ds(c, 1)])
                    last.then_inc(acs[d], 1)

        @b.vector
        def _(dve):
            for d in range(2):
                dve.sem_inc(dvs[d], len(DVE_O))
            with dve.Fori(0, STEPS) as it:
                at = lambda sems, o, d, name: dve.wait_ge(sems[d], count(o, it, name))
                for d in range(2):
                    mask = W.tri[:, d:d + 1, :, :].rearrange("p a x n -> p a (x n)").to_broadcast([P, 2, 256])
                    halves = lambda bank: bank[:, :].rearrange("p (j n) -> p j n", j=2)
                    at(pes, PE_O, d, "b1")
                    dve.tensor_tensor(ark[d][:, :, :, :].rearrange("p j x n -> p j (x n)"), halves(bk[d][1]), mask, ALU.mult).then_inc(dvs[d], 1)
                    at(pes, PE_O, d, "b0")
                    dve.tensor_tensor(arb[d][:, :, 0:2, :].rearrange("p j x n -> p j (x n)"), halves(bk[d][0]), mask, ALU.mult).then_inc(dvs[d], 1)
                for d in range(2):
                    at(pos, POOL_O, d, "y1")
                    dve.tensor_tensor(xy[d][:, 1, :, :], lev[d][:, 0, :, :], ri[d][:, :, 1, :], ALU.add).then_inc(xyinit[d], 1)
                for l in range(1, 6):
                    for d in range(2):
                        for x, bank, p23 in ((0, 0, "p2"), (1, 3, "p3")):
                            if x == 0 and l == 5:
                                continue
                            at(pes, PE_O, d, f"{p23}_{l}")
                            dve.tensor_tensor(xy[d][:, x, :, :], xy[d][:, x, :, :], b2(bk[d][bank]), ALU.add).then_inc(dvs[d], 1)
                for d in range(2):
                    at(pes, PE_O, d, "qg")
                    at(pos, POOL_O, d, "fillR")
                    dve.tensor_tensor(qg[d][:, :, :, :].rearrange("p j x n -> p (j x n)"), bk[d][1][:, :],
                                      ri[d][:, :, :, :].rearrange("p j x n -> p (j x n)"), ALU.add).then_inc(dvs[d], 1)
                for n in range(2):
                    for d in range(2):
                        j = order(d)[n]
                        c = it * 2 + j if d == 0 else it * -2 + (14 + j)
                        at(acs, ACT_O, d, "h")
                        at(pes, PE_O, d, f"s{n + 1}")
                        dve.scalar_tensor_tensor(S[d][:, :], bj(bk[d][0], j), elc[:, d, bass.ds(c, 1)], hh[d][:, j, :], ALU.mult, ALU.add).then_inc(dvs[d], 1)
                for d in range(2):
                    at(pes, PE_O, d, "y")
                    c = it * 2 if d == 0 else it * -2 + 14
                    dve.tensor_reduce(Y[:, d, bass.ds(c, 2), :].rearrange("p c v -> p (c v)").rearrange("p (c v a) -> p c v a", c=2, a=1),
                                      bk[d][3][:, 0:256].rearrange("p (j h v) -> p j v h", j=2, h=2), AXX, ALU.add).then_inc(dvs[d], 1)


def phase_rwkv_out(nc, K, W, Z, p, Y, bv):
    with Mem(nc, f"ro{p}") as m:
        y2 = m.sb("y2", [P, NC, CH]); st = m.sb("st", [P, 4, NC, 1]); t = m.sb("t", [P, SEQ])
        bk = m.banks(4)
        chain, rooted, mm = m.sems("chain", "rooted", "mm")
        b = m.block()
        hs = [slice(0, HALF), slice(HALF, SEQ)]

        @b.vector
        def _(dve):
            then = Chain(dve, chain)
            bc = lambda n: st[:, n, :, :].to_broadcast([P, NC, CH])
            then(dve.tensor_tensor(Y[:, 0, :, :], Y[:, 0, :, :], Y[:, 1, :, :], ALU.add))
            then(dve.tensor_reduce(st[:, 0, :, :], Y[:, 0, :, :], AXX, ALU.add))
            then(dve.tensor_scalar(st[:, 1, :, :], st[:, 0, :, :], 1.0 / CH, None, ALU.mult))
            then(dve.tensor_tensor(Y[:, 0, :, :], Y[:, 0, :, :], bc(1), ALU.subtract))
            then(dve.tensor_tensor(y2[:, :, :], Y[:, 0, :, :], Y[:, 0, :, :], ALU.mult))
            then(dve.tensor_reduce(st[:, 2, :, :], y2[:, :, :], AXX, ALU.add))
            dve.wait_ge(rooted, 1)
            then(dve.reciprocal(st[:, 3, :, :], st[:, 3, :, :]))
            then(dve.tensor_tensor(Y[:, 0, :, :], Y[:, 0, :, :], bc(3), ALU.mult))
            dve.wait_ge(mm, 4)
            for x in range(2):
                last = dve.tensor_scalar(t[:, hs[x]], bk[x][:, :], vec(K.cols, "lnx_g_2", p), vec(K.cols, "lnx_b_2", p), ALU.mult, ALU.add)
            then(last)
            then(dve.tensor_tensor(t[:, :], t[:, :], bv[:, :], ALU.add))
            for x in range(2):
                dve.tensor_tensor(Z[:, p, hs[x]], t[:, hs[x]], bk[2 + x][:, :], ALU.mult)

        @b.scalar
        def _(act):
            act.wait_ge(chain, 6)
            act.activation(st[:, 3, :, :], st[:, 2, :, :], ACT.Sqrt, scale=1.0 / CH, bias=W.lnx_eps[:, 0:1]).then_inc(rooted, 1)

        @b.tensor
        def _(pe):
            for x in range(2):
                pe.matmul(bk[2 + x][:, :], W.gup[:, p * P:(p + 1) * P], Z[:, 14, hs[x]], start=True, stop=True).then_inc(mm, 1)
            pe.wait_ge(chain, 8)
            for x in range(2):
                for c in range(8):
                    for h in range(2):
                        hp = slice(64 * h, 64 * h + 64)
                        last = pe.matmul(bk[x][hp, c * CH:(c + 1) * CH], Y[hp, 0, x * 8 + c, :], W.eye64[hp, :], start=True, stop=True)
                last.then_inc(mm, 1)


QL, KVL, ROPE, NOPE = 384, 256, 32, 64
MH = 8
LQ = KVL + QL
MSCALE = float((NOPE + ROPE) ** -0.5)


def phase_mla_norm(nc, name, K, zm, cT):
    NT = SEQ // P
    parts = ((0, QL, 0, 3, "q_norm_g_2"), (QL, KVL, 3, 2, "kv_norm_g_2"))
    with Mem(nc, name) as m:
        sq = m.sb("sq", [P, 2, LQ])
        ss = m.sb("ss", [P, 3, 2, NT])
        bk = m.banks(4)
        squared, rooted, inv, normed, turned, evac = m.sems("squared", "rooted", "inv", "normed", "turned", "evac")
        b = m.block()

        @b.scalar
        def _(act):
            for t in range(NT):
                if t >= 2:
                    act.wait_ge(squared, 2 * (t - 1))
                for j, (c0, n, _, _, _) in enumerate(parts):
                    act.activation(sq[:, t % 2, c0:c0 + n], zm[:, t, c0:c0 + n], ACT.Square, accum_out=ss[:, 0, j, t:t + 1]).then_inc(squared, 1)
            act.wait_ge(squared, 2 * NT)
            for j, (_, n, _, _, _) in enumerate(parts):
                act.activation(ss[:, 1, j, :], ss[:, 0, j, :], ACT.Sqrt, scale=1.0 / n, bias=K.eps[:, 0:1]).then_inc(rooted, 1)
            act.sem_inc(evac, 4)
            with act.Fori(0, NT // 2) as i:
                for s in range(2):
                    for j, (_, _, k0, kn, gain) in enumerate(parts):
                        hold(act, turned, i * 4 + (2 * s + j + 1))
                        for k in range(kn):
                            last = act.activation(cT[:, k0 + k, bass.ds(i * 256 + s * P, P)], bk[2 * s + j][:, k * P:(k + 1) * P],
                                                  ACT.Copy, scale=vec(K.cols, gain, k))
                        last.then_inc(evac, 1)

        @b.vector
        def _(dve):
            dve.wait_ge(rooted, 2)
            dve.reciprocal(ss[:, 2, :, :], ss[:, 1, :, :]).then_inc(inv, 1)
            dve.wait_ge(inv, 1)
            for t in range(NT):
                for j, (c0, n, _, _, _) in enumerate(parts):
                    last = dve.tensor_scalar(zm[:, t, c0:c0 + n], zm[:, t, c0:c0 + n], ss[:, 2, j, t:t + 1], None, ALU.mult)
                last.then_inc(normed, 1)

        @b.tensor
        def _(pe):
            for t in range(NT):
                pe.wait_ge(normed, t + 1)
                for j, (c0, _, _, kn, _) in enumerate(parts):
                    pe.wait_ge(evac, 2 * t + j + 1)
                    for k in range(kn):
                        last = pe.transpose(bk[2 * (t % 2) + j][:, k * P:(k + 1) * P], zm[:, t, c0 + k * P:c0 + (k + 1) * P], K.ident[:, :])
                    last.then_inc(turned, 1)


def phase_mla_values(nc, name, I, w_in, w_ukv, hT, cT, rope, KTs, V):
    with Mem(nc, name) as m:
        wr = m.sb("wr", [P, KT, 64]); wv = m.sb("wv", [P, 2, MH, NOPE])
        fold = m.sb("fold", [P, 64]); t = m.sb("t", [P, SEQ])
        bk = m.banks(8)
        wcome, vcome, mm, turned, folded, vmm, ev = m.sems("wcome", "vcome", "mm", "turned", "folded", "vmm", "ev")
        b = m.block()

        @b.sync
        def _(sp):
            r0, half = LQ, ROPE // 2
            sp.dma_start(wr[:, :, 0:32], w_in[:, :, r0:r0 + 32]).then_inc(wcome, 16)
            sp.dma_start(wr[:, :, 32:48], w_in[:, :, r0 + half:r0 + 32]).then_inc(wcome, 16)
            sp.dma_start(wr[:, :, 48:64], w_in[:, :, r0:r0 + half]).then_inc(wcome, 16)
            sp.dma_start(fold[:, :], I["k_fold"]).then_inc(wcome, 16)
            sp.dma_start(rope[:, :], I["k_rope2"]).then_inc(wcome, 16)
            for k in range(2):
                sp.dma_start(wv[:, k, :, :], w_ukv[:, k, :].rearrange("p (h n) -> p h n", n=128)[:, :, 64:128]).then_inc(vcome, 16)

        @b.tensor
        def _(pe):
            pe.wait_ge(wcome, 80)
            for h in range(2):
                for k in range(KT):
                    last = pe.matmul(bk[h][64:128, :], wr[:, k, :], hT[:, k, h * HALF:(h + 1) * HALF], start=(k == 0), stop=(k == KT - 1))
                last.then_inc(mm, 1)
            for h in range(2):
                pe.wait_ge(turned, h + 1)
                pe.matmul(bk[2 + h][64:128, :], fold[64:128, :], t[64:128, h * HALF:(h + 1) * HALF], start=True, stop=True).then_inc(folded, 1)
            pe.wait_ge(vcome, 32)
            for n in range(8):
                if n >= 4:
                    pe.wait_ge(ev, n - 3)
                for k in range(2):
                    last = pe.matmul(bk[4 + n % 4][:, :], cT[:, 3 + k, n * P:(n + 1) * P], wv[:, k, :, :].rearrange("p h n -> p (h n)"),
                                     start=(k == 0), stop=(k == 1))
                last.then_inc(vmm, 1)

        @b.vector
        def _(dve):
            for h in range(2):
                hh = slice(h * HALF, (h + 1) * HALF)
                dve.wait_ge(mm, h + 1)
                dve.tensor_tensor(t[64:128, hh], bk[h][64:128, :], rope[64:128, hh], ALU.mult).then_inc(turned, 1)
            for n in range(8):
                dve.wait_ge(vmm, n + 1)
                dve.tensor_copy(V[:, n, :], bk[4 + n % 4][:, :]).then_inc(ev, 1)

        @b.scalar
        def _(act):
            for h in range(2):
                act.wait_ge(folded, h + 1)
                for s in range(2):
                    act.activation(KTs[64:128, s, h * HALF:(h + 1) * HALF], bk[2 + h][64:128, :], ACT.Copy, scale=MSCALE)


def phase_mla_heads(nc, name, K, w_uq, w_ukv, cT, rope, KTs, V, oN):
    NQ = SEQ // P
    with Mem(nc, name) as m:
        wq = m.sb("wq", [P, 2, 3, P]); wk = m.sb("wk", [P, 2, 2, NOPE])
        QT = m.sb("QT", [P, 2, SEQ])
        pb = m.sb("pb", [P, 2, SEQ]); pt = m.sb("pt", [P, 2, NQ, P])
        mx = m.sb("mx", [P, 2]); sm = m.sb("sm", [P, 2]); rs = m.sb("rs", [P, 2])
        sc = [m.stack.enter_context(nc.psum_tensor(f"{name}_sc{n}", [P, SEQ], F32)) for n in range(2)]
        bk = m.banks(4)
        tb, ob = bk[0:2], bk[2:4]
        full = m.sems("full0", "full1")
        wfree, proj, qe, ke, sdone, mxed, exped, tdone, pt0, pt1, odone, inv, oout = m.sems(
            "wfree", "proj", "qe", "ke", "sdone", "mxed", "exped", "tdone", "pt0", "pt1", "odone", "inv", "oout")
        b = m.block()
        NP2 = MH // 2

        @b.sync
        def _(sp):
            with sp.Fori(0, NP2) as i:
                for s in range(2):
                    q0 = i * 192 + s * 96
                    sp.wait_ge(wfree, i * 2 + (s + 1))
                    sp.dma_start(wq[:, s, :, 0:96], w_uq[:, :, bass.ds(q0, 96)]).then_inc(full[s], 16)
                    sp.dma_start(wq[:, s, :, 96:112], w_uq[:, :, bass.ds(q0 + 80, 16)]).then_inc(full[s], 16)
                    sp.dma_start(wq[:, s, :, 112:128], w_uq[:, :, bass.ds(q0 + 64, 16)]).then_inc(full[s], 16)
                    sp.dma_start(wk[:, s, :, :], w_ukv[:, :, bass.ds(i * 256 + s * P, NOPE)]).then_inc(full[s], 16)

        @b.tensor
        def _(pe):
            pe.sem_inc(wfree, 2)
            pe.sem_inc(tdone, 1)
            with pe.Fori(0, NP2) as i:
                for s in range(2):
                    c = lambda u, o=1: i * (2 * NQ) + (s * NQ + u + o)

                    def scores(u):
                        if u >= 2:
                            pe.wait_ge(exped, c(u, 0))
                        for h in range(2):
                            last = pe.matmul(sc[u % 2][:, h * HALF:(h + 1) * HALF], QT[:, s, u * P:(u + 1) * P],
                                             KTs[:, s, h * HALF:(h + 1) * HALF], start=True, stop=True)
                        last.then_inc(sdone, 1)

                    def turn(u):
                        pe.wait_ge(exped, c(u, 2))
                        for x in range(2):
                            pe.wait_ge((pt0, pt1)[x], c(u))
                            for k in range(4):
                                last = pe.transpose(tb[x][:, k * P:(k + 1) * P], pb[:, u % 2, (4 * x + k) * P:(4 * x + k + 1) * P], K.ident[:, :])
                            last.then_inc(tdone, 1)

                    def values(u):
                        pe.wait_ge(oout, c(u))
                        for k in range(NQ):
                            if k == 0:
                                pe.wait_ge(pt0, c(u, 2))
                            if k == 4:
                                pe.wait_ge(pt1, c(u, 2))
                            last = pe.matmul(ob[u % 2][:, 0:P], pt[:, u % 2, k, :], V[:, k, bass.ds(i * P, P)], start=(k == 0), stop=(k == NQ - 1))
                        last.then_inc(odone, 1)

                    pe.wait_ge(full[s], i * 64 + 64)
                    pe.wait_ge(exped, c(0))
                    for h in range(2):
                        for k in range(3):
                            last = pe.matmul(sc[0][:, h * HALF:(h + 1) * HALF], wq[:, s, k, :], cT[:, k, h * HALF:(h + 1) * HALF], start=(k == 0), stop=(k == 2))
                    last.then_inc(proj, 1)
                    for h in range(2):
                        for k in range(2):
                            last = pe.matmul(sc[1][0:64, h * HALF:(h + 1) * HALF], wk[:, s, k, :], cT[:, 3 + k, h * HALF:(h + 1) * HALF], start=(k == 0), stop=(k == 1))
                    last.then_inc(proj, 1)
                    pe.wait_ge(proj, i * 4 + (2 * s + 2))
                    pe.sem_inc(wfree, 1)
                    pe.wait_ge(qe, i * 2 + (s + 1))
                    pe.wait_ge(ke, i * 2 + (s + 1))
                    scores(0)
                    for u in range(NQ):
                        if u + 1 < NQ:
                            scores(u + 1)
                        if u:
                            values(u - 1)
                        turn(u)
                    values(NQ - 1)

        @b.scalar
        def _(act):
            act.sem_inc(exped, 1)
            with act.Fori(0, NP2) as i:
                for s in range(2):
                    c = lambda u, o=1: i * (2 * NQ) + (s * NQ + u + o)

                    def exps(u):
                        hold(act, mxed, c(u))
                        hold(act, tdone, i * (4 * NQ) + (2 * (s * NQ + u) + 1))
                        hold(act, oout, c(u))
                        act.activation(pb[:, u % 2, :], sc[u % 2][:, :], ACT.Exp, bias=mx[:, u % 2:u % 2 + 1], accum_out=sm[:, u % 2:u % 2 + 1]).then_inc(exped, 1)

                    hold(act, proj, i * 4 + (2 * s + 2))
                    act.activation(KTs[0:64, s, :], sc[1][0:64, :], ACT.Copy, scale=MSCALE).then_inc(ke, 1)
                    exps(0)
                    for u in range(NQ):
                        if u + 1 < NQ:
                            exps(u + 1)
                        hold(act, tdone, i * (4 * NQ) + (2 * (s * NQ + u) + 3))
                        hold(act, odone, c(u))
                        act.activation(pt[:, u % 2, 4:8, :].rearrange("p k n -> p (k n)"), tb[1][:, :], ACT.Copy).then_inc(pt1, 1)

        @b.vector
        def _(dve):
            dve.sem_inc(pt0, 1)
            dve.sem_inc(pt1, 1)
            dve.sem_inc(oout, 2)
            dve.sem_inc(odone, 2)
            with dve.Fori(0, NP2) as i:
                for s in range(2):
                    c = lambda u, o=1: i * (2 * NQ) + (s * NQ + u + o)

                    def maxima(u):
                        dve.wait_ge(sdone, c(u))
                        dve.wait_ge(exped, c(u, 0)) if s * NQ + u >= 1 else None
                        dve.tensor_reduce(mx[:, u % 2:u % 2 + 1], sc[u % 2][:, :], AXX, ALU.max, negate=True).then_inc(mxed, 1)

                    def out(u):
                        dve.reciprocal(rs[:, u % 2:u % 2 + 1], sm[:, u % 2:u % 2 + 1]).then_inc(inv, 1)
                        dve.wait_ge(inv, c(u))
                        dve.wait_ge(odone, c(u, 3))
                        o = oN[:, u, bass.ds(i * P + s * NOPE, NOPE)]
                        dve.tensor_scalar(o, ob[u % 2][:, s * NOPE:(s + 1) * NOPE], rs[:, u % 2:u % 2 + 1], None, ALU.mult).then_inc(oout, 1)

                    dve.wait_ge(proj, i * 4 + (2 * s + 1))
                    dve.tensor_tensor(QT[:, s, :], sc[0][:, :], rope[:, :], ALU.mult).then_inc(qe, 1)
                    maxima(0)
                    for u in range(NQ):
                        if u + 1 < NQ:
                            maxima(u + 1)
                        if u:
                            out(u - 1)
                        dve.wait_ge(tdone, i * (4 * NQ) + (2 * (s * NQ + u) + 2))
                        dve.wait_ge(odone, c(u))
                        dve.tensor_copy(pt[:, u % 2, 0:4, :].rearrange("p k n -> p (k n)"), tb[0][:, :]).then_inc(pt0, 1)
                    out(NQ - 1)


def phase_turn_out(nc, name, K, oN, oT):
    with Mem(nc, name) as m:
        bk = m.banks(8)
        mm, = m.sems("mm")
        b = m.block()

        @b.tensor
        def _(pe):
            for n in range(8):
                f, h = divmod(n, 2)
                for q in range(4):
                    last = pe.transpose(bk[n][:, q * P:(q + 1) * P], oN[:, 4 * h + q, f * P:(f + 1) * P], K.ident[:, :])
                last.then_inc(mm, 1)

        @b.vector
        def _(dve):
            for n in range(0, 8, 2):
                dve.wait_ge(mm, n + 1)
                dve.tensor_copy(oT[:, n // 2, 0:HALF], bk[n][:, :])

        @b.scalar
        def _(act):
            for n in range(1, 8, 2):
                act.wait_ge(mm, n + 1)
                act.activation(oT[:, n // 2, HALF:SEQ], bk[n][:, :], ACT.Copy)


def mla(nc, I, K, S, w_in, hT, oT):
    rr = lambda n: I[n].rearrange("l (k p) n -> p (l k) n", p=P)
    with Mem(nc, "mla") as m:
        cT = m.sb("cT", [P, 5, SEQ])
        rope = m.sb("rope", [P, SEQ]); KTs = m.sb("KTs", [P, 2, SEQ]); V = m.sb("V", [P, 8, MH * NOPE])
        with Mem(nc, "mlz") as mz:
            zm = mz.sb("zm", [P, 8, LQ])
            phase_proj_N(nc, "mp", w_in[:, :, 0:LQ], KT, hT, 0, 8, 2, LQ // 2,
                         lambda e, g, t, ps: e.tensor_copy(zm[:, t, bass.ds(g * (LQ // 2), LQ // 2)], ps), uses_dve=True,
                         aside=tiles_of(S.hT, hT))
            phase_mla_norm(nc, "mn", K, zm, cT)
        phase_mla_values(nc, "mv", I, w_in, rr("w_ukv_2"), hT, cT, rope, KTs, V)
        with Mem(nc, "mlo") as mo:
            oN = mo.sb("oN", [P, 8, MH * NOPE])
            phase_mla_heads(nc, "mh", K, rr("w_uq_2"), rr("w_ukv_2"), cT, rope, KTs, V, oN)
            phase_turn_out(nc, "mt", K, oN, oT)


def phase_move(nc, name, pairs):
    with Mem(nc, name) as m:
        moved, = m.sems("moved")
        b = m.block()

        @b.sync
        def _(sp):
            for dst, src in pairs:
                sp.dma_start(dst, src).then_inc(moved, 16)
            sp.wait_ge(moved, 16 * len(pairs))


def phase_clear(nc, t):
    with Mem(nc, "clear") as m:
        b = m.block()

        @b.gpsimd
        def _(gp):
            gp.memset(t, 0.0)


def phase_silu(nc, name, t):
    with Mem(nc, name) as m:
        b = m.block()

        @b.scalar
        def _(act):
            act.activation(t, t, ACT.Silu)


def retention_branch(nc, I, K, w_in, hT, spare):
    with Mem(nc, "ret") as m:
        R = Named()
        R.lg = m.sb("lg", [P, 8])
        R.DQ = m.sb("DQ", [P, RH, 2, P])
        R.DC = m.sb("DC", [P, 2, RH, 4])
        R.DT = m.sb("DT", [P, RH, P])
        R.S0 = m.sb("S0", [P, 2, RH, RV])
        phase_decay(nc, I, K, R)
        with Mem(nc, "ctx") as mc:
            hcT = mc.sb("hcT", [P, KT, CTX])
            phase_norm(nc, "ctxnorm", K.X, 2, hcT, lambda k: K.mod[:, 1, 0, k:k + 1], lambda k: K.mod[:, 1, 1, k:k + 1], K, src=I["ctx"][0])
            phase_ctx(nc, I, K, R, hcT, w_in)
        qk = m.sb("qk", [P, 8, SEQ]); v = m.sb("v", [P, 8, D]); g = K.X
        b0 = PLACES["b_in"][0]
        phase_proj_T(nc, "qkproj", w_in[:, :, 0:D], KT, hT, 8, 2,
                     lambda e, t, h, ps: e.activation(one(qk[:, bass.ds(t, 1), h * HALF:(h + 1) * HALF]), ps, ACT.Identity,
                                                      bias=K.cols[:, bass.ds(t + b0, 1)]))
        with Mem(nc, "vg") as mb:
            bb = mb.sb("bb", [P, 2 * D])
            phase_move(nc, "vgbias", [(bb[:, :], I["b_in"][:, D:3 * D].to_broadcast([P, 2 * D]))])
            for name, dst, off in (("vproj", v, 0), ("gproj", g, D)):
                phase_proj_N(nc, name, w_in[:, :, D + off:2 * D + off], KT, hT, 0, 8, 4, 256,
                             lambda e, gr, t, ps, dst=dst, off=off: e.tensor_tensor(
                                 dst[:, t, bass.ds(gr * 256, 256)], ps, bb[:, bass.ds(gr * 256 + off, 256)], ALU.add), uses_dve=True)
        phase_silu(nc, "gsilu", g[:, :, :].rearrange("p a n -> p (a n)"))
        phase_retention(nc, I, K, R, qk, v, g, hT, spare.rearrange("p (d a) (b n) -> p d (a b) n", d=2, n=RV))


def hyena(nc, I, K, S, w_in, hT, hyT):
    with Mem(nc, "hy") as m:
        H = m.sb("H", [P, 4, 4, C])
        with Mem(nc, "hyf") as mf:
            he, ho = mf.sb("he", [P, 8, C]), mf.sb("ho", [P, 8, C])
            phase_filters(nc, I, K, he, ho, K.X)
            phase_forward(nc, "fwdfilt", I, he, ho, H)
        xc = m.sb("xc", [P, 12, SEQ])
        nil = hyT[:, 0, :]
        phase_clear(nc, nil)
        prod = K.X[:, :, :].rearrange("p (a b) (c n) -> p a (b c) n", b=2, n=C)
        col = lambda base: (lambda t: K.cols[:, bass.ds(t + base, 1)])
        cw, cb, b0 = PLACES["hy_conv_w"][0], PLACES["hy_conv_b"][0], PLACES["b_in"][0] + 24
        taps = [col(cw), col(cw + 12), col(cw + 24), col(cb)]
        rows = S.rows.rearrange("(b p) d -> p b d", p=P)
        clear = tuple((rows[:, n:n + 2, :], nil.rearrange("p (a d) -> p a d", a=1).to_broadcast([P, 2, D])) for n in range(0, MAXB, 2))
        phase_taps(nc, "hin", w_in[:, :, 3072:4608], hT, xc, 12, 2, lambda j, t: taps[j](t), bias=col(b0),
                   aside=tiles_of(S.hT, hT) + clear)
        zn = xc[:, 8:12, :].rearrange("p a (b c) -> p (a b) c", c=C)
        phase_hyena_turn(nc, K, xc, zn)
        phase_forward(nc, "fwdz", I, zn, zn, H, prod, hyT[:, :, 0:C])
        phase_inverse(nc, I, K, prod, xc, hyT)


def moe(nc, tag, I, K, S, hidden, scale, shift, names, gate):
    rgw, rgb, rew, reb, w1, w3, w2 = names
    with Mem(nc, f"moe{tag}") as m:
        T = Named()
        T.dest = m.sb("dest", [P, 2, 8], U32)
        T.wt = m.sb("wt", [P, 2, 8])
        T.be = m.sb("be", [1, MAXB], I32)
        T.nb = m.sb("nb", [1, 1], I32)
        with Mem(nc, f"u{tag}") as mu:
            uT = mu.sb("uT", [P, KT, SEQ])
            phase_norm(nc, f"moenorm{tag}", K.X, 8, uT, scale, shift, K, y_dram=S.normed)
            phase_router(nc, f"router{tag}", I, K, uT, I[rgw], I[rgb], I[rew], I[reb], T, S.slot)
        phase_experts(nc, f"experts{tag}", K, hidden, experts_to_tiles(I[w1]), experts_to_tiles(I[w3]), experts_to_tiles(I[w2]),
                      scale, shift, T, S.slot, S.normed, S.rows)
        phase_combine(nc, f"combine{tag}", K.X, T, S.rows, gate)


def first(nc, I, K, S):
    with Mem(nc, "b1") as m:
        K.mod, K.gt, K.X = m.sb("mod", [P, 3, 2, 8]), m.sb("gt", [P, 2, D]), m.sb("X", [P, KT, D])
        w_in = rows_to_tiles(I["w_in"])
        phase_vectors(nc, I, K)
        with Mem(nc, "mix") as mm:
            hyT = mm.sb("hyT", [P, 4, SEQ]); hT = mm.sb("hT", [P, KT, SEQ])
            phase_norm(nc, "norm1", K.X, 8, hT, lambda k: K.mod[:, 0, 0, k:k + 1], lambda k: K.mod[:, 0, 1, k:k + 1], K, src=I["x"][0])
            hyena(nc, I, K, S, w_in, hT, hyT)
            Mem.retire(nc)
            phase_move(nc, "keep1", [(S.hyT, hyT[:, :, :])])
            retention_branch(nc, I, K, w_in, hT, hyT[:, :, :])
            retT, h2T, mixedT = hT, mm.sb("h2T", [P, KT, SEQ]), mm.sb("mixedT", [P, KT, SEQ])
            phase_move(nc, "again1", [(h2T[:, :, :], S.hT), (hyT[:, :, :], S.hyT)])
            phase_merge(nc, "merge1", ((rows_to_tiles(I["ret_w_o"]), 8, retT), (rows_to_tiles(I["hy_w_o"]), 4, hyT)), K, mixedT,
                        (w_in[:, :, 4608:], h2T), PLACES["b_in"][0] + 36,
                        aside=tiles_of(K.X, I["x"][0].rearrange("(t p) d -> p t d", p=P)))
            phase_residual(nc, "resid1", rows_to_tiles(I["w_out"]), mixedT, K.X, K.gt[:, 0, :])
        Mem.retire(nc)
        moe(nc, 1, I, K, S, 512, lambda k: K.mod[:, 2, 0, k:k + 1], lambda k: K.mod[:, 2, 1, k:k + 1],
            ("router_group_w", "router_group_b", "router_expert_w", "router_expert_b", "expert_w1", "expert_w3", "expert_w2"), K.gt[:, 1, :])
        phase_rownorm(nc, "between", K, K.X, I["final_norm_g"], S.x)


def rwkv(nc, I, K, S, w_in, Z):
    with Mem(nc, "rwkv") as m:
        W = Named()
        W.tri = m.sb("tri", [P, 2, 2, P])
        W.level = m.sb("level", [P, 2, 6, P])
        W.headones = m.sb("headones", [P, P])
        W.carry = m.sb("carry", [P, SEQ])
        W.eye64 = m.sb("eye64", [P, 64])
        W.wup = m.sb("wup", [P, RC])
        W.aup = m.sb("aup", [P, RC])
        W.gup = m.sb("gup", [P, RC])
        W.mid = m.sb("mid", [P, 15])
        W.ka1 = m.sb("ka1", [P, 4])
        W.lnx_eps = m.sb("lnx_eps", [P, 1])
        W.zero = m.sb("zero", [P, 1])
        W.tot = m.sb("tot", [P, 2, NC])
        W.junk = m.sb("junk", [P, 1])
        with Mem(nc, "rwkvh") as mh:
            hT = mh.sb("hT", [P, KT, SEQ])
            phase_rwkv_consts(nc, I, K, W, aside=((hT[:, :, :], S.hT),))
            col = lambda base: (lambda t: K.cols[:, bass.ds(t + base, 1)])
            taps = (col(PLACES["mu_prev_2"][0]), lambda t: W.mid[:, bass.ds(t, 1)], col(PLACES["mu_next_2"][0]), lambda t: W.zero[:, 0:1])
            phase_taps(nc, "taps", w_in[:, :, 672:2592], hT, Z, 15, 3, lambda j, t: taps[j](t))
        phase_rwkv_gates(nc, Z)
        pr, elc, bv, Y = m.sb("pr", [P, 2, 4, SEQ]), m.sb("elc", [P, 2, NC]), m.sb("bv", [P, SEQ]), m.sb("Y", [P, 2, NC, CH])
        for p in range(NP):
            phase_rwkv_prep(nc, K, W, Z, p, pr, elc, bv)
            phase_rwkv_chunks(nc, K, W, Z, p, pr, elc, Y)
            phase_rwkv_out(nc, K, W, Z, p, Y, bv)


def second(nc, I, K, S, out):
    with Mem(nc, "b2") as m:
        oT, Z = m.sb("oT", [P, 4, SEQ]), m.sb("Z", [P, 15, SEQ])
        w_in = rows_to_tiles(I["w_in_2"])
        with Mem(nc, "b2h") as mh:
            hT = mh.sb("hT", [P, KT, SEQ])
            with Mem(nc, "b2x") as mx:
                phase_norm(nc, "norm2", mx.sb("x", [P, KT, D]), 8, hT, lambda k: vec(K.cols, "norm_mix_g_2", k), None, K, src=S.x)
            mla(nc, I, K, S, w_in, hT, oT)
        Mem.retire(nc)
        rwkv(nc, I, K, S, w_in, Z)
        Mem.retire(nc)
        mixedT = Z[:, 4:12, :]
        with Mem(nc, "b2m") as mh:
            hT = mh.sb("hT", [P, KT, SEQ])
            phase_move(nc, "again3", [(hT[:, :, :], S.hT)])
            phase_merge(nc, "merge2", ((rows_to_tiles(I["w_br_mla_2"]), 4, oT), (rows_to_tiles(I["w_br_rwkv_2"]), 4, Z)), K, mixedT,
                        (w_in[:, :, 2592:], hT), PLACES["gate_b_2"][0])
        K.X = m.sb("X", [P, KT, D])
        phase_move(nc, "again4", [(K.X[:, :, :], S.x.rearrange("(t p) d -> p t d", p=P))])
        phase_residual(nc, "resid2", rows_to_tiles(I["w_out_2"]), mixedT, K.X)
        moe(nc, 2, I, K, S, 256, lambda k: vec(K.cols, "norm_ffn_g_2", k), None,
            ("router_group_w_2", "router_group_b_2", "router_expert_w_2", "router_expert_b_2", "w1_2", "w3_2", "w2_2"), None)
        phase_rownorm(nc, "last", K, K.X, I["norm_final_g_2"], out)


def two_blocks(nc, I, out):
    Mem.spent = []
    with Mem(nc, "all") as m:
        K = Named()
        K.ident = m.sb("ident", [P, P])
        K.ones = m.sb("ones", [P, P])
        K.eps = m.sb("eps", [P, 1])
        K.cols = m.sb("cols", [P, VGROUPS * P])
        S = Named()
        S.hT = nc.dram_tensor("keep_hT", [P, KT, SEQ], F32, kind="Internal").ap()
        S.hyT = nc.dram_tensor("keep_hyT", [P, 4, SEQ], F32, kind="Internal").ap()
        S.x = nc.dram_tensor("keep_x", [SEQ, D], F32, kind="Internal").ap()
        S.normed = nc.dram_tensor("keep_normed", [SEQ, D], F32, kind="Internal").ap()
        S.slot = nc.dram_tensor("keep_slot", [(MAXB + 1) * P], I32, kind="Internal").ap()
        S.rows = nc.dram_tensor("keep_rows", [MAXB * P, D], F32, kind="Internal").ap()
        first(nc, I, K, S)
        Mem.retire(nc)
        second(nc, I, K, S, out)


def constants():
    f = np.float32
    c = {}
    c["k_eye"] = np.eye(128, dtype=f)
    i = np.arange(128, dtype=np.float64)
    j = i[:, None]
    pos = np.zeros((128, 6, 128))
    pos[:, 0] = i + 1; pos[:, 1] = 128 - i
    pos[:, 2] = np.maximum(i - j, 0); pos[:, 3] = np.maximum(j - i, 0)
    pos[:, 4] = i >= j; pos[:, 5] = j > i
    c["k_pos"] = pos.astype(f)
    p = i
    c["k_cpos"] = np.stack([127 - p, 255 - p, 127 - p, 0 * p + 128, p, p, p + 128, 0 * p + 128], 1).astype(f)
    n = np.arange(1024)
    inv = 10000.0 ** (-np.arange(32) / 32)
    row, col = (n // 64)[None] * inv[:, None], (n % 64)[None] * inv[:, None]
    ang = np.concatenate([row, row, col, col])
    sgn = np.concatenate([-np.ones(32), np.ones(32)] * 2)[:, None]
    c["k_rope1"] = np.stack([np.cos(ang), np.sin(ang)], 1).astype(f)
    rot = np.zeros((128, 128))
    for d in range(128):
        src = d + 32 if d % 64 < 32 else d - 32
        rot[src, d] = sgn[d, 0]
    c["k_rot1"] = rot.astype(f)
    return c


def hyena_constants():
    f = np.float32
    c = {}
    n = np.concatenate([np.arange(0, 1024, 2), np.arange(1, 1024, 2)])
    t = (np.arange(1024, dtype=f) / f(1024))
    bands = np.linspace(1e-4, 15, 16, dtype=f)
    phase = (f(2.0 * np.pi) * t[:, None] * bands[None, :]).astype(f)
    feats = np.concatenate([t[:, None], np.cos(phase), -np.sin(phase)], -1).astype(f)
    c["k_feats"] = np.ascontiguousarray(feats[n].T)
    c["k_negt"] = np.ascontiguousarray(-t[n].reshape(8, 128).T)
    slow, fast = abs(np.log(1e-2)) / 1.5, abs(np.log(1e-2)) / 0.3
    c["k_delta"] = np.tile(np.linspace(slow, fast, 512, dtype=f)[None], (128, 1))
    th = 2 * np.pi * (np.arange(512) + 0.5) / 2048
    m = np.arange(512)
    tab = [fn(th[:, None] * (2 * m + par)[None]) for par in (0, 1) for fn in (np.cos, np.sin)]
    order = [tab[0], tab[2], tab[1], tab[3]]
    fwd = np.zeros((4, 128, 4, 4, 128), f)
    for a, T in enumerate(order):
        for kt in range(4):
            for mt in range(4):
                fwd[kt, :, a, mt, :] = T[kt * 128:(kt + 1) * 128, mt * 128:(mt + 1) * 128].T
    c["k_fwd"] = fwd.reshape(4, 128, 2048)
    inv = np.zeros((2, 128, 2, 4, 512), f)
    for par in (0, 1):
        for a in (0, 1):
            for kt in range(4):
                inv[par, :, a, kt, :] = tab[2 * par + a][kt * 128:(kt + 1) * 128] / 1024
    c["k_inv"] = inv.reshape(2, 128, 4096)
    return c


def router_constants():
    f = np.float32
    c = {}
    r = np.zeros((128, 3, 48), f)
    r[:, 0, :4] = [4, 3, 2, 1]
    r[:, 1, :8] = np.arange(8, 0, -1)
    r[:, 2, :48] = np.arange(48)
    c["k_iotas"] = r
    c["k_upper"] = np.triu(np.ones((128, 128), f), 1)
    return c


def rwkv_constants():
    f = np.float32
    c = {}
    i = np.arange(128)
    r, q = i[:, None], i[None, :]
    same = (r // 64) == (q // 64)
    m2 = np.zeros((128, 2, 2, 128), f)
    m2[:, 0, 0] = same & (r < q); m2[:, 0, 1] = same & (r <= q)
    m2[:, 1, 0] = same & (r > q); m2[:, 1, 1] = same & (r >= q)
    c["k_tri"] = m2
    lv = np.zeros((128, 2, 6, 128), f)
    for l in range(6):
        b = 1 << l
        blk = (r // (2 * b)) == (q // (2 * b))
        lv[:, 0, l] = blk & (r % (2 * b) < b) & (q % (2 * b) >= b)
        lv[:, 1, l] = blk & (r % (2 * b) >= b) & (q % (2 * b) < b)
    c["k_level"] = lv
    c["k_headones"] = same.astype(f)
    ch = np.ones((128, 1024), f); ch[:, ::64] = 0
    c["k_carry"] = ch
    c["k_eye64"] = np.concatenate([np.eye(64, dtype=f)] * 2)
    return c


def mla_constants():
    f = np.float32
    inv = (f(10000.0) ** (-np.arange(0, 32, 2, dtype=f) / f(32))).astype(f)
    ang = (np.arange(1024, dtype=f)[None] * inv[:, None]).astype(f).astype(np.float64)
    cos, sin = np.cos(ang), np.sin(ang)
    tab = np.ones((128, 1024))
    tab[64:] = np.concatenate([cos, cos, -sin, sin])
    fold = np.zeros((128, 64))
    for p in range(64, 128):
        for q in range(64):
            fold[p, q] = p % 32 == q % 32
    return {"k_rope2": tab.astype(f), "k_fold": fold.astype(f)}


_INPUTS = ("x", "c", "ctx", "c_ctx", "ada_w", "ada_b", "norm1_g", "norm2_g", "w_in", "b_in", "ret_decay_logit",
           "ret_w_o", "hy_conv_w", "hy_conv_b", "hy_ffn_w1", "hy_ffn_b1", "hy_ffn_freq", "hy_ffn_w2", "hy_ffn_b2",
           "hy_ffn_w3", "hy_skip", "hy_w_o", "w_out", "router_group_w", "router_group_b", "router_expert_w",
           "router_expert_b", "expert_w1", "expert_w3", "expert_w2", "final_norm_g", "norm_mix_g_2", "w_in_2",
           "q_norm_g_2", "kv_norm_g_2", "w_uq_2", "w_ukv_2", "w_br_mla_2", "mu_prev_2", "mu_next_2", "w0_2",
           "w_up_2", "a0_2", "a_up_2", "g_up_2", "k_k_2", "k_a_2", "r_k_2", "lnx_g_2", "lnx_b_2", "w_br_rwkv_2",
           "gate_b_2", "w_out_2", "norm_ffn_g_2", "router_group_w_2", "router_group_b_2", "router_expert_w_2",
           "router_expert_b_2", "w1_2", "w3_2", "w2_2", "norm_final_g_2")


def kernel(**inputs):
    import concourse.bacc as bacc
    from concourse.bass_utils import run_bass_kernel_spmd

    nc = bacc.Bacc("TRN2", target_bir_lowering=False, num_devices=1)
    tables = {**constants(), **hyena_constants(), **router_constants(), **rwkv_constants(), **mla_constants()}
    arrays, I = {}, {}
    for name in _INPUTS + tuple(tables):
        a = np.ascontiguousarray(tables[name] if name in tables else inputs[name])
        arrays[f"in_{name}"] = a
        I[name] = nc.dram_tensor(f"in_{name}", a.shape, mybir.dt.from_np(a.dtype), kind="ExternalInput").ap()
    out = nc.dram_tensor("out", (SEQ, D), F32, kind="ExternalOutput").ap()
    two_blocks(nc, I, out)
    result = run_bass_kernel_spmd(nc, [arrays], core_ids=[0])
    return result.results[0]["out"].reshape(1, SEQ, D)
```
